# Optimizing a Trainium2 kernel written in Bass

```python
import jax, jax.numpy as jnp
from jax import lax
import numpy as np
import math

D_MODEL = 1024
BATCH = 1
SEQ = 256
DEPTH = 2

HEAD_DIM = 64
H_GDN = (3 * D_MODEL) // (8 * HEAD_DIM)
H_MOBA = D_MODEL // (4 * HEAD_DIM)
H_MLSTM = D_MODEL // HEAD_DIM - H_GDN - H_MOBA
W_GDN = H_GDN * HEAD_DIM
W_MOBA = H_MOBA * HEAD_DIM
W_MLSTM = H_MLSTM * HEAD_DIM
MIX_WIDTH = W_GDN + W_MOBA + W_MLSTM
CONV_WIDTH = 4
GDN_CHUNK = 64
MLSTM_CHUNK = 64
MOBA_BLOCK = 256
MOBA_TOPK = 3
MOBA_Q_BLOCK = 128
D_FF = 2816
N_SUB = 3
ALPHA = (2 * DEPTH) ** 0.25
BETA_INIT = (8 * DEPTH) ** -0.25
ADA_INIT = 0.1
LN_EPS = 1e-5
NORM_EPS = 1e-6

IN_SIZES = [3 * W_GDN, H_GDN, H_GDN, W_GDN,
            3 * W_MOBA,
            2 * W_MLSTM, W_MLSTM, H_MLSTM, H_MLSTM, W_MLSTM]
IN_SPLITS = [int(s) for s in np.cumsum(IN_SIZES)[:-1]]
D_IN = int(sum(IN_SIZES))


def layer_norm(x, g, b):
    xf = x.astype(jnp.float32)
    mu = jnp.mean(xf, -1, keepdims=True)
    var = jnp.mean(jnp.square(xf - mu), -1, keepdims=True)
    return ((xf - mu) * lax.rsqrt(var + LN_EPS) * g + b).astype(x.dtype)

def modulate(x, shift, scale):
    return x * (1 + scale[:, None, :]) + shift[:, None, :]

def swiglu(h, w13, w2):
    a, b = jnp.split(h @ w13, 2, axis=-1)
    return (jax.nn.silu(a) * b) @ w2

def causal_conv_silu(x, w):
    y = lax.conv_general_dilated(x, w[:, None, :], window_strides=(1,), padding=[(CONV_WIDTH - 1, 0)],
                                 dimension_numbers=('NWC', 'WIO', 'NWC'), feature_group_count=x.shape[-1])
    return jax.nn.silu(y)

def split_heads(t):
    b_, t_, w = t.shape
    return t.reshape(b_, t_, w // HEAD_DIM, HEAD_DIM).transpose(0, 2, 1, 3)

def l2norm(x):
    return x * lax.rsqrt(jnp.sum(x * x, -1, keepdims=True) + NORM_EPS)

def to_chunks(a, size):
    b_, h_, t_ = a.shape[:3]
    return jnp.moveaxis(a.reshape(b_, h_, t_ // size, size, *a.shape[3:]), 2, 0)

def from_chunks(a):
    n, b_, h_, l, d = a.shape
    return jnp.moveaxis(a, 0, 2).reshape(b_, h_, n * l, d)

def gated_delta_rule(q, k, v, g, beta):
    b_, h_, t_, dk = q.shape
    dv = v.shape[-1]
    L = GDN_CHUNK
    q = to_chunks(q * dk ** -0.5, L); k = to_chunks(k, L); v = to_chunks(v, L)
    g = to_chunks(g, L); beta = to_chunks(beta, L)
    G = jnp.cumsum(g, axis=-1)
    incl = jnp.tril(jnp.ones((L, L), dtype=bool))
    strict = jnp.tril(jnp.ones((L, L), dtype=bool), -1)
    decay = jnp.exp(jnp.where(incl, G[..., :, None] - G[..., None, :], -jnp.inf))
    kb = k * beta[..., None]
    A = jnp.where(strict, jnp.einsum('nbhid,nbhjd->nbhij', kb, k) * decay, 0.0)
    M = A + jnp.eye(L, dtype=A.dtype)
    u = lax.linalg.triangular_solve(M, v * beta[..., None], left_side=True, lower=True, unit_diagonal=True)
    w = lax.linalg.triangular_solve(M, kb * jnp.exp(G)[..., None], left_side=True, lower=True, unit_diagonal=True)
    attn = jnp.einsum('nbhid,nbhjd->nbhij', q, k) * decay
    q_dec = q * jnp.exp(G)[..., None]
    k_dec = k * jnp.exp(G[..., -1:] - G)[..., None]
    g_last = jnp.exp(G[..., -1])

    def step(S, inp):
        q_i, w_i, u_i, k_i, a_i, gl_i = inp
        v_new = u_i - jnp.einsum('bhld,bhde->bhle', w_i, S)
        o = jnp.einsum('bhld,bhde->bhle', q_i, S) + jnp.einsum('bhls,bhse->bhle', a_i, v_new)
        S = S * gl_i[..., None, None] + jnp.einsum('bhld,bhle->bhde', k_i, v_new)
        return S, o

    S0 = jnp.zeros((b_, h_, dk, dv), q.dtype)
    _, o = lax.scan(step, S0, (q_dec, w, u, k_dec, attn, g_last))
    return from_chunks(o)

def moba_attention(q, k, v):
    b_, h_, t_, d = q.shape
    n_blk = -(-t_ // MOBA_BLOCK)
    top_k = min(MOBA_TOPK, n_blk)
    pad = n_blk * MOBA_BLOCK - t_
    kp = jnp.pad(k, ((0, 0), (0, 0), (0, pad), (0, 0)))
    vp = jnp.pad(v, ((0, 0), (0, 0), (0, pad), (0, 0)))
    k_blk = kp.reshape(b_, h_, n_blk, MOBA_BLOCK, d)
    v_blk = vp.reshape(b_, h_, n_blk, MOBA_BLOCK, d)
    k_mean = jnp.mean(k_blk, axis=3)
    scale = d ** -0.5
    bi = jnp.arange(b_)[:, None, None, None]
    hi = jnp.arange(h_)[None, :, None, None]
    blk_ids = jnp.arange(n_blk)
    n_sel = top_k * MOBA_BLOCK

    def one_block(qb):
        q0 = qb * MOBA_Q_BLOCK
        own = q0 // MOBA_BLOCK
        qc = lax.dynamic_slice_in_dim(q, q0, MOBA_Q_BLOCK, axis=2)
        gate = jnp.einsum('bhqd,bhnd->bhqn', qc, k_mean)
        gate = jnp.where(blk_ids < own, gate, -jnp.inf)
        _, sel = lax.top_k(gate, top_k)
        sel_ok = jnp.repeat(jnp.arange(top_k) < own, MOBA_BLOCK)
        k_sel = k_blk[bi, hi, sel].reshape(b_, h_, MOBA_Q_BLOCK, n_sel, d)
        v_sel = v_blk[bi, hi, sel].reshape(b_, h_, MOBA_Q_BLOCK, n_sel, d)
        s_sel = jnp.where(sel_ok, jnp.einsum('bhqd,bhqkd->bhqk', qc, k_sel) * scale, -jnp.inf)
        k_own = lax.dynamic_slice_in_dim(kp, own * MOBA_BLOCK, MOBA_BLOCK, axis=2)
        v_own = lax.dynamic_slice_in_dim(vp, own * MOBA_BLOCK, MOBA_BLOCK, axis=2)
        q_pos = q0 + jnp.arange(MOBA_Q_BLOCK)
        k_pos = own * MOBA_BLOCK + jnp.arange(MOBA_BLOCK)
        s_own = jnp.where(k_pos[None, :] <= q_pos[:, None],
                          jnp.einsum('bhqd,bhkd->bhqk', qc, k_own) * scale, -jnp.inf)
        p = jax.nn.softmax(jnp.concatenate([s_sel, s_own], -1).astype(jnp.float32), axis=-1).astype(q.dtype)
        return (jnp.einsum('bhqk,bhqkd->bhqd', p[..., :n_sel], v_sel)
                + jnp.einsum('bhqk,bhkd->bhqd', p[..., n_sel:], v_own))

    out = lax.map(one_block, jnp.arange(t_ // MOBA_Q_BLOCK))
    return from_chunks(out)

def mlstm_chunkwise(q, k, v, i_pre, logf):
    b_, h_, t_, d = q.shape
    L = MLSTM_CHUNK
    q = to_chunks(q, L); k = to_chunks(k * d ** -0.5, L); v = to_chunks(v, L)
    i_pre = to_chunks(i_pre, L); logf = to_chunks(logf, L)
    bcum = jnp.cumsum(logf, axis=-1)
    incl = jnp.tril(jnp.ones((L, L), dtype=bool))
    D = jnp.where(incl, bcum[..., :, None] - bcum[..., None, :] + i_pre[..., None, :], -jnp.inf)
    D_max = jnp.max(D, axis=-1)
    w_end = bcum[..., -1:] - bcum + i_pre
    qk = jnp.einsum('nbhtd,nbhsd->nbhts', q, k)

    def step(carry, inp):
        C, n, m = carry
        q_i, k_i, v_i, b_i, D_i, Dm_i, qk_i, we_i = inp
        inter = b_i + m[..., None]
        m_t = jnp.maximum(inter, Dm_i)
        a_inter = jnp.exp(inter - m_t)
        P = qk_i * jnp.exp(D_i - m_t[..., None])
        num = a_inter[..., None] * jnp.einsum('bhld,bhde->bhle', q_i, C) + jnp.einsum('bhls,bhse->bhle', P, v_i)
        den = a_inter * jnp.einsum('bhld,bhd->bhl', q_i, n) + jnp.sum(P, -1)
        h = num / jnp.maximum(jnp.abs(den), jnp.exp(-m_t))[..., None]
        inter_end = b_i[..., -1] + m
        m_new = jnp.maximum(inter_end, jnp.max(we_i, -1))
        s = jnp.exp(we_i - m_new[..., None])
        decay = jnp.exp(inter_end - m_new)
        C = decay[..., None, None] * C + jnp.einsum('bhl,bhld,bhle->bhde', s, k_i, v_i)
        n = decay[..., None] * n + jnp.einsum('bhl,bhld->bhd', s, k_i)
        return (C, n, m_new), h

    init = (jnp.zeros((b_, h_, d, d), q.dtype), jnp.zeros((b_, h_, d), q.dtype), jnp.zeros((b_, h_), q.dtype))
    _, h = lax.scan(step, init, (q, k, v, bcum, D, D_max, qk, w_end))
    return from_chunks(h)

def token_mixer(h, w_in, w_out, gdn_conv, gdn_a_log, gdn_dt_bias, gdn_norm,
                mlstm_conv, mlstm_i_bias, mlstm_f_bias, mlstm_norm):
    b_, t_, _ = h.shape
    dt = h.dtype
    f32 = jnp.float32
    qkv_a, a_a, b_a, z_a, qkv_b, qk_c, v_c, i_c, f_c, o_c = jnp.split(h @ w_in, IN_SPLITS, axis=-1)
    qa, ka, va = jnp.split(causal_conv_silu(qkv_a, gdn_conv), 3, axis=-1)
    qa = l2norm(split_heads(qa).astype(f32))
    ka = l2norm(split_heads(ka).astype(f32))
    va = split_heads(va).astype(f32)
    g = -jnp.exp(gdn_a_log.astype(f32)) * jax.nn.softplus((a_a + gdn_dt_bias).astype(f32))
    beta = jax.nn.sigmoid(b_a.astype(f32))
    oa = gated_delta_rule(qa, ka, va, g.transpose(0, 2, 1), beta.transpose(0, 2, 1)).transpose(0, 2, 1, 3)
    oa = oa * lax.rsqrt(jnp.mean(oa * oa, -1, keepdims=True) + NORM_EPS) * gdn_norm
    oa = (oa.reshape(b_, t_, W_GDN) * jax.nn.silu(z_a.astype(f32))).astype(dt)
    qb, kb, vb = jnp.split(qkv_b, 3, axis=-1)
    ob = moba_attention(split_heads(qb), split_heads(kb), split_heads(vb))
    ob = ob.transpose(0, 2, 1, 3).reshape(b_, t_, W_MOBA).astype(dt)
    qc, kc = jnp.split(causal_conv_silu(qk_c, mlstm_conv), 2, axis=-1)
    i_pre = (i_c + mlstm_i_bias).astype(f32).transpose(0, 2, 1)
    logf = jax.nn.log_sigmoid((f_c + mlstm_f_bias).astype(f32)).transpose(0, 2, 1)
    hc = mlstm_chunkwise(split_heads(qc).astype(f32), split_heads(kc).astype(f32),
                         split_heads(v_c).astype(f32), i_pre, logf).transpose(0, 2, 1, 3)
    hc = hc * jax.nn.sigmoid(o_c.astype(f32)).reshape(b_, t_, H_MLSTM, HEAD_DIM)
    mu = jnp.mean(hc, -1, keepdims=True)
    var = jnp.mean(jnp.square(hc - mu), -1, keepdims=True)
    hc = (hc - mu) * lax.rsqrt(var + NORM_EPS) * mlstm_norm.reshape(H_MLSTM, HEAD_DIM)
    hc = hc.reshape(b_, t_, W_MLSTM).astype(dt)
    return jnp.concatenate([oa, ob, hc], axis=-1) @ w_out

def first_inputs(seed: int = 0) -> dict:
    key = jax.random.key(seed)
    ks = jax.random.split(key, 18)
    nrm = lambda k, shape, s: jax.random.normal(k, shape, jnp.float32) * s
    dt_init = jnp.exp(jax.random.uniform(ks[10], (DEPTH, H_GDN), jnp.float32,
                                         float(np.log(1e-3)), float(np.log(1e-1))))
    return {
        "x": nrm(ks[0], (BATCH, SEQ, D_MODEL), 1.0),
        "c": nrm(ks[1], (BATCH, D_MODEL), 1.0),
        "ada_w": nrm(ks[2], (DEPTH, D_MODEL, N_SUB * 3 * D_MODEL), ADA_INIT * D_MODEL ** -0.5),
        "ada_b": nrm(ks[3], (DEPTH, N_SUB * 3 * D_MODEL), 0.01),
        "ffn_w13": nrm(ks[4], (DEPTH, 2, D_MODEL, 2 * D_FF), D_MODEL ** -0.5),
        "ffn_w2": nrm(ks[5], (DEPTH, 2, D_FF, D_MODEL), BETA_INIT * D_FF ** -0.5),
        "w_in": nrm(ks[6], (DEPTH, D_MODEL, D_IN), D_MODEL ** -0.5),
        "w_out": nrm(ks[7], (DEPTH, MIX_WIDTH, D_MODEL), BETA_INIT * MIX_WIDTH ** -0.5),
        "gdn_conv": nrm(ks[8], (DEPTH, CONV_WIDTH, 3 * W_GDN), CONV_WIDTH ** -0.5),
        "gdn_a_log": jnp.log(jax.random.uniform(ks[9], (DEPTH, H_GDN), jnp.float32, 1.0, 16.0)),
        "gdn_dt_bias": dt_init + jnp.log(-jnp.expm1(-dt_init)),
        "gdn_norm": 1.0 + nrm(ks[11], (DEPTH, HEAD_DIM), 0.02),
        "mlstm_conv": nrm(ks[12], (DEPTH, CONV_WIDTH, 2 * W_MLSTM), CONV_WIDTH ** -0.5),
        "mlstm_i_bias": nrm(ks[13], (DEPTH, H_MLSTM), 0.1),
        "mlstm_f_bias": jnp.linspace(3.0, 6.0, H_MLSTM, dtype=jnp.float32)[None, :] + nrm(ks[14], (DEPTH, H_MLSTM), 0.1),
        "mlstm_norm": 1.0 + nrm(ks[15], (DEPTH, W_MLSTM), 0.02),
        "ln_g": 1.0 + nrm(ks[16], (DEPTH, N_SUB, D_MODEL), 0.02),
        "ln_b": nrm(ks[17], (DEPTH, N_SUB, D_MODEL), 0.02),
    }

def first_block(x, c, ada_w, ada_b, ffn_w13, ffn_w2, w_in, w_out, gdn_conv, gdn_a_log, gdn_dt_bias,
              gdn_norm, mlstm_conv, mlstm_i_bias, mlstm_f_bias, mlstm_norm, ln_g, ln_b):
    b_ = x.shape[0]
    for l in range(DEPTH):
        mod = (jax.nn.silu(c) @ ada_w[l] + ada_b[l]).reshape(b_, N_SUB, 3, D_MODEL)
        y = swiglu(modulate(x, mod[:, 0, 0], mod[:, 0, 1]), ffn_w13[l, 0], ffn_w2[l, 0])
        x = layer_norm(ALPHA * x + 0.5 * (1 + mod[:, 0, 2])[:, None, :] * y, ln_g[l, 0], ln_b[l, 0])
        y = token_mixer(modulate(x, mod[:, 1, 0], mod[:, 1, 1]), w_in[l], w_out[l], gdn_conv[l], gdn_a_log[l],
                        gdn_dt_bias[l], gdn_norm[l], mlstm_conv[l], mlstm_i_bias[l], mlstm_f_bias[l], mlstm_norm[l])
        x = layer_norm(ALPHA * x + (1 + mod[:, 1, 2])[:, None, :] * y, ln_g[l, 1], ln_b[l, 1])
        y = swiglu(modulate(x, mod[:, 2, 0], mod[:, 2, 1]), ffn_w13[l, 1], ffn_w2[l, 1])
        x = layer_norm(ALPHA * x + 0.5 * (1 + mod[:, 2, 2])[:, None, :] * y, ln_g[l, 2], ln_b[l, 2])
    return x


N_MEM = 256
DA_HEADS = 4
DA_HEAD_DIM = 64
DA_V_DIM = 2 * DA_HEAD_DIM
DA_WIDTH = DA_HEADS * DA_V_DIM
HG_HEADS = 4
HG_DK = 128
HG_DV = 128
HG_WIDTH = HG_HEADS * HG_DV
HG_CHUNK = 64
HG_MIN_FORGET = 1e-20
MX_HEADS = 4
MX_HEAD_DIM = 128
MX_WIDTH = MX_HEADS * MX_HEAD_DIM
MIX_WIDTH_2 = DA_WIDTH + HG_WIDTH + MX_WIDTH
IN_WIDTHS = (
    DA_HEADS * 2 * DA_HEAD_DIM,
    DA_HEADS * 2 * DA_HEAD_DIM,
    DA_WIDTH,
    HG_HEADS * HG_DK,
    HG_HEADS * HG_DK,
    HG_HEADS * HG_DK,
    HG_WIDTH,
    HG_WIDTH,
    MX_WIDTH,
)
IN_WIDTH = 4608
ROPE_THETA = 500000.0
ROPE_DIM = DA_HEAD_DIM // 4
Q_BLOCK = 128
CONV_W = 3
RMS_EPS = 1e-6
DEEPNORM_ALPHA = (2 * DEPTH) ** 0.25
DEEPNORM_BETA = (8 * DEPTH) ** -0.25


def layer_norm_2(x, g, b):
    xf = x.astype(jnp.float32)
    mu = jnp.mean(xf, axis=-1, keepdims=True)
    var = jnp.mean(jnp.square(xf - mu), axis=-1, keepdims=True)
    y = (xf - mu) * lax.rsqrt(var + LN_EPS)
    return (y * g.astype(jnp.float32) + b.astype(jnp.float32)).astype(x.dtype)

def rms_norm(x, g):
    xf = x.astype(jnp.float32)
    y = xf * lax.rsqrt(jnp.mean(jnp.square(xf), axis=-1, keepdims=True) + RMS_EPS)
    return (y * g.astype(jnp.float32)).astype(x.dtype)

def rope_partial(t, cos, sin):
    half = ROPE_DIM // 2
    t1 = t[..., :half]
    t2 = t[..., half:ROPE_DIM]
    return jnp.concatenate([t1 * cos - t2 * sin, t2 * cos + t1 * sin, t[..., ROPE_DIM:]], axis=-1)

def diff_attention(q, k, v, lam):
    B, S, H = q.shape[:3]
    nblk = S // Q_BLOCK
    qb = q.reshape(B, nblk, Q_BLOCK, H, 2, DA_HEAD_DIM).transpose(1, 0, 2, 3, 4, 5)

    def one_block(qi):
        s = jnp.einsum('bqhcd,bkhcd->bhcqk', qi, k).astype(jnp.float32)
        p = jax.nn.softmax(s, axis=-1)
        a = p[:, :, 0] - lam * p[:, :, 1]
        return jnp.einsum('bhqk,bkhv->bqhv', a.astype(v.dtype), v)

    o = lax.map(one_block, qb)
    return o.transpose(1, 0, 2, 3, 4).reshape(B, S, H, DA_V_DIM)

def hgrn2_chunk_scan(q, k, v, g):
    B, S, H, dk = q.shape
    dv = v.shape[-1]
    n = S // HG_CHUNK

    def to_chunks(t):
        return t.reshape(B, n, HG_CHUNK, H, t.shape[-1]).transpose(1, 0, 3, 2, 4)

    qc, kc, vc, gc = to_chunks(q), to_chunks(k), to_chunks(v), to_chunks(g)
    bc = jnp.cumsum(gc, axis=3)
    mask = jnp.tril(jnp.ones((HG_CHUNK, HG_CHUNK), dtype=bool))[:, :, None]

    def step(state, inp):
        qt, kt, vt, bt = inp
        o_inter = jnp.einsum('bhtk,bhkv->bhtv', qt * jnp.exp(bt), state)
        diff = bt[:, :, :, None, :] - bt[:, :, None, :, :]
        dec = jnp.where(mask, jnp.exp(jnp.where(mask, diff, 0.0)), 0.0)
        attn = jnp.einsum('bhtk,bhtsk->bhts', qt, dec * kt[:, :, None, :, :])
        o_intra = jnp.einsum('bhts,bhsv->bhtv', attn, vt)
        b_last = bt[:, :, -1:, :]
        state = jnp.exp(b_last[:, :, 0, :])[..., None] * state + jnp.einsum(
            'bhsk,bhsv->bhkv', kt * jnp.exp(b_last - bt), vt)
        return state, o_inter + o_intra

    s0 = jnp.zeros((B, H, dk, dv), jnp.float32)
    _, o = lax.scan(step, s0, (qc, kc, vc, bc))
    return o.transpose(1, 0, 3, 2, 4).reshape(B, S, H, dv)

def hgrn_lower_bound(lb_logits, layer):
    p = jax.nn.softmax(lb_logits.astype(jnp.float32), axis=0)
    return (jnp.cumsum(p, axis=0) - p[0])[layer]

def hgrn_log_forget(z, lb):
    f = lb + (1.0 - lb) * jax.nn.sigmoid(z)
    return jnp.log(jnp.maximum(f, HG_MIN_FORGET))

def memory_attention(q, mk, mv):
    s = jnp.einsum('bqhd,bmhd->bhqm', q * (MX_HEAD_DIM ** -0.5), mk).astype(jnp.float32)
    p = jax.nn.softmax(s, axis=-1)
    return jnp.einsum('bhqm,bmhd->bqhd', p.astype(mv.dtype), mv)

def depthwise_conv_centred(u, w, b):
    y = lax.conv_general_dilated(
        u, w[:, None, :].astype(u.dtype), window_strides=(1,),
        padding=((CONV_W // 2, CONV_W // 2),),
        dimension_numbers=('NWC', 'WIO', 'NWC'),
        feature_group_count=u.shape[-1])
    return y + b.astype(u.dtype)

def hybrid_layer(x, mem, cos, sin, layer, w_in, da_lambda, da_norm_g, hg_lb_fwd, hg_lb_bwd,
                 hg_norm_g, w_mem_kv, w_out, ln1_g, ln1_b, w_up, conv_w, conv_b, w_down,
                 ln2_g, ln2_b):
    B, S, _ = x.shape
    M = mem.shape[1]
    proj = x @ w_in
    split_idx = [int(i) for i in np.cumsum(IN_WIDTHS)[:-1]]
    da_q, da_k, da_v, hg_q, hg_ff, hg_fb, hg_i, hg_g, mx_q = jnp.split(proj, split_idx, axis=-1)

    dq = rope_partial(da_q.reshape(B, S, DA_HEADS, 2, DA_HEAD_DIM), cos, sin) * (DA_HEAD_DIM ** -0.5)
    dk = rope_partial(da_k.reshape(B, S, DA_HEADS, 2, DA_HEAD_DIM), cos, sin)
    dv = da_v.reshape(B, S, DA_HEADS, DA_V_DIM)
    lam_init = 0.8 - 0.6 * math.exp(-0.3 * layer)
    lf = da_lambda.astype(jnp.float32)
    lam = jnp.exp(jnp.sum(lf[0] * lf[1])) - jnp.exp(jnp.sum(lf[2] * lf[3])) + lam_init
    da_o = diff_attention(dq, dk, dv, lam)
    da_o = (rms_norm(da_o, da_norm_g) * (1.0 - lam_init)).reshape(B, S, DA_WIDTH)

    f32 = jnp.float32
    hq = jax.nn.silu(hg_q.reshape(B, S, HG_HEADS, HG_DK).astype(f32))
    hv = hg_i.reshape(B, S, HG_HEADS, HG_DV).astype(f32)
    lb_f = hgrn_lower_bound(hg_lb_fwd, layer).reshape(HG_HEADS, HG_DK)
    lb_b = hgrn_lower_bound(hg_lb_bwd, layer).reshape(HG_HEADS, HG_DK)
    g_f = hgrn_log_forget(hg_ff.reshape(B, S, HG_HEADS, HG_DK).astype(f32), lb_f)
    g_b = hgrn_log_forget(hg_fb.reshape(B, S, HG_HEADS, HG_DK).astype(f32), lb_b)
    o_fwd = hgrn2_chunk_scan(hq, -jnp.expm1(g_f), hv, g_f)
    o_bwd = jnp.flip(hgrn2_chunk_scan(jnp.flip(hq, 1), jnp.flip(-jnp.expm1(g_b), 1),
                                      jnp.flip(hv, 1), jnp.flip(g_b, 1)), 1)
    hg_o = (o_fwd + o_bwd).astype(x.dtype)
    hg_gate = jax.nn.silu(hg_g.reshape(B, S, HG_HEADS, HG_DV))
    hg_o = (rms_norm(hg_o, hg_norm_g) * hg_gate).reshape(B, S, HG_WIDTH)

    mkv = (mem @ w_mem_kv).reshape(B, M, 2, MX_HEADS, MX_HEAD_DIM)
    mx_o = memory_attention(mx_q.reshape(B, S, MX_HEADS, MX_HEAD_DIM), mkv[:, :, 0], mkv[:, :, 1])
    mx_o = mx_o.reshape(B, S, MX_WIDTH)

    mix = jnp.concatenate([da_o, hg_o, mx_o], axis=-1) @ w_out
    x = layer_norm_2(DEEPNORM_ALPHA * x + mix, ln1_g, ln1_b)

    u = depthwise_conv_centred(x @ w_up, conv_w, conv_b)
    gate, val = jnp.split(u, 2, axis=-1)
    ffn = (jax.nn.silu(gate) * val) @ w_down
    return layer_norm_2(DEEPNORM_ALPHA * x + ffn, ln2_g, ln2_b)

def second_inputs(seed: int = 0) -> dict:
    key = jax.random.key(seed)
    ks = jax.random.split(key, 24)
    nrm = jax.random.normal
    D = D_MODEL
    x = nrm(ks[0], (BATCH, SEQ, D), jnp.float32)
    mem = nrm(ks[1], (BATCH, N_MEM, D), jnp.float32)
    offsets = jax.random.randint(ks[2], (BATCH, 1), 0, 1024, dtype=jnp.int32)
    positions = (jnp.arange(SEQ, dtype=jnp.int32)[None, :] + offsets).astype(jnp.int32)
    return {
        "x": x,
        "mem": mem,
        "positions": positions,
        "ln_in_g": 1.0 + 0.02 * nrm(ks[3], (D,), jnp.float32),
        "ln_in_b": 0.02 * nrm(ks[4], (D,), jnp.float32),
        "w_in": nrm(ks[5], (DEPTH, D, IN_WIDTH), jnp.float32) * D ** -0.5,
        "da_lambda": 0.1 * nrm(ks[6], (DEPTH, 4, DA_HEAD_DIM), jnp.float32),
        "da_norm_g": 1.0 + 0.02 * nrm(ks[7], (DEPTH, DA_V_DIM), jnp.float32),
        "hg_lb_fwd": 0.5 * nrm(ks[8], (DEPTH, HG_HEADS * HG_DK), jnp.float32),
        "hg_lb_bwd": 0.5 * nrm(ks[9], (DEPTH, HG_HEADS * HG_DK), jnp.float32),
        "hg_norm_g": 1.0 + 0.02 * nrm(ks[10], (DEPTH, HG_DV), jnp.float32),
        "w_mem_kv": nrm(ks[11], (DEPTH, D, 2 * MX_WIDTH), jnp.float32) * D ** -0.5,
        "w_out": nrm(ks[12], (DEPTH, MIX_WIDTH_2, D), jnp.float32) * (MIX_WIDTH_2 ** -0.5 * DEEPNORM_BETA),
        "ln1_g": 1.0 + 0.02 * nrm(ks[13], (DEPTH, D), jnp.float32),
        "ln1_b": 0.02 * nrm(ks[14], (DEPTH, D), jnp.float32),
        "w_up": nrm(ks[15], (DEPTH, D, 2 * D_FF), jnp.float32) * D ** -0.5,
        "conv_w": nrm(ks[16], (DEPTH, CONV_W, 2 * D_FF), jnp.float32) * CONV_W ** -0.5,
        "conv_b": 0.02 * nrm(ks[17], (DEPTH, 2 * D_FF), jnp.float32),
        "w_down": nrm(ks[18], (DEPTH, D_FF, D), jnp.float32) * (D_FF ** -0.5 * DEEPNORM_BETA),
        "ln2_g": 1.0 + 0.02 * nrm(ks[19], (DEPTH, D), jnp.float32),
        "ln2_b": 0.02 * nrm(ks[20], (DEPTH, D), jnp.float32),
    }

def second_block(x, mem, positions, ln_in_g, ln_in_b, w_in, da_lambda, da_norm_g, hg_lb_fwd,
              hg_lb_bwd, hg_norm_g, w_mem_kv, w_out, ln1_g, ln1_b, w_up, conv_w, conv_b,
              w_down, ln2_g, ln2_b):
    inv_freq = ROPE_THETA ** (-jnp.arange(0, ROPE_DIM, 2, dtype=jnp.float32) / ROPE_DIM)
    ang = positions.astype(jnp.float32)[..., None] * inv_freq
    cos = jnp.cos(ang)[:, :, None, None, :].astype(x.dtype)
    sin = jnp.sin(ang)[:, :, None, None, :].astype(x.dtype)

    h = layer_norm_2(x, ln_in_g, ln_in_b)
    for l in range(DEPTH):
        h = hybrid_layer(h, mem, cos, sin, l, w_in[l], da_lambda[l], da_norm_g[l],
                         hg_lb_fwd, hg_lb_bwd, hg_norm_g[l], w_mem_kv[l], w_out[l],
                         ln1_g[l], ln1_b[l], w_up[l], conv_w[l], conv_b[l], w_down[l],
                         ln2_g[l], ln2_b[l])
    return h


def setup_inputs(seed=0):
    out = dict(first_inputs(seed))
    for name, value in second_inputs(seed + 1).items():
        if name != "x":
            out[name + "_2"] = value
    return out


def reference(
    x, c, ada_w, ada_b, ffn_w13, ffn_w2, w_in, w_out, gdn_conv, gdn_a_log, gdn_dt_bias,
    gdn_norm, mlstm_conv, mlstm_i_bias, mlstm_f_bias, mlstm_norm, ln_g, ln_b, mem_2,
    positions_2, ln_in_g_2, ln_in_b_2, w_in_2, da_lambda_2, da_norm_g_2, hg_lb_fwd_2,
    hg_lb_bwd_2, hg_norm_g_2, w_mem_kv_2, w_out_2, ln1_g_2, ln1_b_2, w_up_2, conv_w_2, conv_b_2,
    w_down_2, ln2_g_2, ln2_b_2,
):
    x = first_block(
        x, c, ada_w, ada_b, ffn_w13, ffn_w2, w_in, w_out, gdn_conv, gdn_a_log, gdn_dt_bias,
        gdn_norm, mlstm_conv, mlstm_i_bias, mlstm_f_bias, mlstm_norm, ln_g, ln_b,
    )
    return second_block(
        x, mem_2, positions_2, ln_in_g_2, ln_in_b_2, w_in_2, da_lambda_2, da_norm_g_2,
        hg_lb_fwd_2, hg_lb_bwd_2, hg_norm_g_2, w_mem_kv_2, w_out_2, ln1_g_2, ln1_b_2, w_up_2,
        conv_w_2, conv_b_2, w_down_2, ln2_g_2, ln2_b_2,
    )


_drawn_inputs = setup_inputs


def setup_inputs(seed=0):
    import zlib

    import numpy as np

    out = dict(_drawn_inputs(seed))
    spreads = {}
    factors = {'gdn_norm': 25.454,
     'mlstm_i_bias': 64.0,
     'mlstm_norm': 7.145,
     'da_lambda_2': 3.352,
     'da_norm_g_2': 21.668,
     'hg_lb_fwd_2': 8.0,
     'hg_lb_bwd_2': 23.265,
     'hg_norm_g_2': 29.475,
     'conv_b_2': 6.688,
     'mem_2': 2.938,
     'w_mem_kv_2': 2.975}
    for name, (base, spread) in spreads.items():
        noise = np.random.default_rng([zlib.crc32(name.encode()), seed]).standard_normal(out[name].shape)
        drawn = base * np.exp(spread * noise) if base else spread * noise
        out[name] = __import__('jax').numpy.asarray(drawn.astype(out[name].dtype))
    for name, factor in factors.items():
        out[name] = (out[name] * factor).astype(out[name].dtype)
    return out
```

```python
import math
from contextlib import ExitStack

import numpy as np

import concourse.bass as bass
from concourse import mybir

F32 = mybir.dt.float32
F32R = mybir.dt.float32r
I32 = mybir.dt.int32
ALU = mybir.AluOpType
ACT = mybir.ActivationFunctionType
AX = mybir.AxisListType.X
ADD, SUB, MUL, MAX, MIN = ALU.add, ALU.subtract, ALU.mult, ALU.max, ALU.min

D = 1024
T = 256
FF = 2816
NF = FF // 128
ALPHA = 4 ** 0.25
CH = 2048
NW = 4
NH = 3
NEG = -1e30


def row_index():
    at, n = {}, 0
    for name, rows in (
        ("ada_b", 144), ("ln_g", 48), ("ln_b", 48), ("lin_g", 8), ("lin_b", 8), ("ln1_g", 16), ("ln1_b", 16),
        ("ln2_g", 16), ("ln2_b", 16), ("gconv", 72), ("mconv", 48), ("cw", 264), ("cb", 88), ("lbf", 8), ("lbb", 8),
        ("mnorm", 6), ("gnorm", 2), ("dnorm", 2), ("hnorm", 2),
    ):
        at[name] = n
        n += rows
    return at, n


ROW, NROW = row_index()


def mixer1_cols():
    r = lambda a, b: list(range(a, b))
    fm = [r(128 * i, 128 * i + 128) for i in range(9)]
    fm += [r(2316 + 128 * i, 2316 + 128 * i + 128) for i in range(6)]
    fm += [r(1548 + 128 * i, 1548 + 128 * i + 128) for i in range(4)]
    out = []
    tm = [r(1152, 1164) + r(3468, 3480)]
    tm += [r(1164, 1420), r(1420, 1548) + r(3480, 3608), r(3608, 3864), r(2060, 2316), r(3084, 3340), r(3340, 3468)]
    out += [("tm", tm[0])]
    for i in range(0, 18, 2):
        out.append(("fm", fm[i] + fm[i + 1]))
    out.append(("fm", fm[18]))
    out += [("tm", c) for c in tm[1:]]
    return out


def mixer2_cols():
    r = lambda a, b: list(range(a, b))
    order = [1536, 2048, 2560, 3072, 3584, 0, 512, 1024, 4096]
    return [r(o + h, o + h + 256) for o in order for h in (0, 256)]


def schedule():
    s = []
    ada = lambda l, j, v: [("ada", l, j, v, q) for q in range(4)]

    def ffn(l, i):
        a = []
        for m in range(NF // 2):
            a += [("w13", l, i, 0, m), ("w13", l, i, 1, m)]
        return a

    for l in range(2):
        for j in range(3):
            if l == 0 and j == 0:
                s += ada(0, 0, 0) + ada(0, 0, 1)
            nxt = (l, j + 1) if j < 2 else (l + 1, 0)
            late = ada(*nxt, 0) + ada(*nxt, 1) if nxt[0] < 2 else []
            gate = ada(l, j, 2)
            if j == 1:
                body = [("win", l, n) for n in range(len(mixer1_cols()))]
                tail = [("wout", l, k) for k in range(4)]
                s += weave(body, gate + late) + tail
            else:
                s += weave(ffn(l, j // 2), gate + late)
                s += [("w2", l, j // 2, k) for k in range(NF // 2)]
    for l in range(2):
        s += [("win2", l, n) for n in range(18)]
        s += [("wkv", l, n) for n in range(4)]
        s += [("wout2", l, k) for k in range(6)]
        for m in range(NF // 2):
            s += [("wup", l, 0, m), ("wup", l, 1, m)]
        s += [("wdn", l, k) for k in range(NF // 2)]
    return s


def weave(body, extra):
    out, n = [], 0
    for i, b in enumerate(body):
        out.append(b)
        while n < len(extra) * (i + 1) // len(body):
            out.append(extra[n])
            n += 1
    return out


SCHED = schedule()


def width(c):
    if c[0] == "win":
        return len(mixer1_cols()[c[2]][1])
    return 256


def pack(inp):
    S = np.zeros((len(SCHED), 128, CH), np.float32)
    km = lambda w: w.reshape(-1, 128, w.shape[1]).transpose(1, 0, 2).reshape(128, -1)
    cols1, cols2 = mixer1_cols(), mixer2_cols()
    for n, c in enumerate(SCHED):
        k = c[0]
        if k == "ada":
            _, l, j, v, q = c
            o = (j * 3 + v) * D + q * 256
            w = km(inp["ada_w"][l][:, o:o + 256])
        elif k == "w13":
            _, l, i, h, m = c
            w = km(inp["ffn_w13"][l, i][:, h * FF + m * 256:h * FF + m * 256 + 256])
        elif k == "w2":
            w = km(inp["ffn_w2"][c[1], c[2]][c[3] * 256:c[3] * 256 + 256])
        elif k == "win":
            w = km(inp["w_in"][c[1]][:, cols1[c[2]][1]])
        elif k == "wout":
            w = km(inp["w_out"][c[1]][c[2] * 256:c[2] * 256 + 256])
        elif k == "win2":
            w = km(inp["w_in_2"][c[1]][:, cols2[c[2]]])
        elif k == "wkv":
            w = km(inp["w_mem_kv_2"][c[1]][:, c[2] * 256:c[2] * 256 + 256])
        elif k == "wout2":
            w = km(inp["w_out_2"][c[1]][c[2] * 256:c[2] * 256 + 256])
        elif k == "wup":
            w = km(inp["w_up_2"][c[1]][:, c[2] * FF + c[3] * 256:c[2] * FF + c[3] * 256 + 256])
        else:
            w = km(inp["w_down_2"][c[1]][c[2] * 256:c[2] * 256 + 256])
        S[n, :, :w.shape[1]] = w
    return S


def constants():
    i = np.arange(128)
    s, t = i[:, None], i[None, :]
    same = (s // 64) == (t // 64)
    parts = [
        np.eye(128),
        np.where(same & (s <= t), 0.0, NEG),
        np.where(t <= s, 0.0, NEG),
    ]
    for l in range(6):
        z = 1 << l
        parts.append(((s // (2 * z) == t // (2 * z)) & ((s // z) % 2 == 0) & ((t // z) % 2 == 1)).astype(float))
    for l in range(6):
        z = 1 << l
        parts.append(((s // (2 * z) == t // (2 * z)) & ((s // z) != (t // z))).astype(float))
    parts.append(same.astype(float))
    parts.append(np.tile((np.arange(256) % 64 != 0).astype(float), (128, 1)))
    parts.append(np.tile(500000.0 ** (-np.arange(0, 16, 2) / 16.0), (128, 1)))
    sg = np.ones((128, 1))
    sg[32:64] = -1.0
    parts.append(sg)
    parts.append(np.full((128, 7), -0.5))
    return np.concatenate(parts, 1).astype(np.float32)


CW = dict(ident=(0, 128), neg=(128, 128), causal=(256, 128), lvl=(384, 768), both=(1152, 768), ones64=(1920, 128),
          rmask=(2048, 256), freq=(2304, 8), sgn=(2312, 1), mhalf=(2313, 7))
NCONST = 2320


def layout(inp):
    rows = []
    f = lambda a: rows.append(np.asarray(a, np.float32).reshape(-1, 128))
    for n in ("ada_b", "ln_g", "ln_b", "ln_in_g_2", "ln_in_b_2", "ln1_g_2", "ln1_b_2", "ln2_g_2", "ln2_b_2", "gdn_conv",
              "mlstm_conv", "conv_w_2", "conv_b_2", "hg_lb_fwd_2", "hg_lb_bwd_2", "mlstm_norm"):
        f(inp[n])
    f(np.concatenate([inp["gdn_norm"], inp["gdn_norm"]], 1))
    f(inp["da_norm_g_2"])
    f(inp["hg_norm_g_2"])
    cols = np.concatenate(rows, 0).T
    heads = np.zeros((2, 128, 2), np.float32)
    for l in range(2):
        heads[l, 0:6, 0] = inp["gdn_dt_bias"][l]
        heads[l, 32:38, 0] = inp["mlstm_f_bias"][l]
        heads[l, 96:102, 0] = inp["mlstm_i_bias"][l]
        heads[l, 0:6, 1] = inp["gdn_a_log"][l]
    fm = lambda a: a.reshape(T, 8, 128).transpose(2, 1, 0)
    vec = np.concatenate([a.reshape(-1, D) for a in (
        inp["ada_b"].reshape(2, 3, 3, D)[:, :, 2], inp["ln_g"], inp["ln_b"], inp["ln_in_g_2"][None], inp["ln_in_b_2"][None],
        inp["ln1_g_2"], inp["ln1_b_2"], inp["ln2_g_2"], inp["ln2_b_2"])], 0)
    lam = inp["da_lambda_2"].reshape(2, 256)
    return {
        "stream": pack(inp),
        "cols": cols,
        "cst": constants(),
        "heads": heads.transpose(1, 0, 2).reshape(128, 4),
        "x": inp["x"][0].reshape(2, 128, D),
        "xT": fm(inp["x"][0]),
        "memT": fm(inp["mem_2"][0]),
        "c": inp["c"][0].reshape(8, 128).T,
        "pos": np.asarray(inp["positions_2"][0]).reshape(2, 128).T,
        "vec": vec,
        "lam": lam,
    }


VEC = dict(gate=0, ln_g=6, ln_b=12, lin_g=18, lin_b=19, ln1_g=20, ln1_b=22, ln2_g=24, ln2_b=26)


def flat(x, out):
    if x is None:
        return out
    if isinstance(x, tuple) and len(x) == 2 and isinstance(x[0], str):
        out.append(x)
        return out
    for y in x:
        flat(y, out)
    return out


class Queues:

    def __init__(self, nc, ctx):
        self.nc, self.ctx = nc, ctx
        self.sem, self.cnt, self.seen, self.q = {}, {}, {}, {}
        for e in ("pe", "dve", "act", "pool", "sp"):
            self.sem[e] = ctx.enter_context(nc.semaphore("s_" + e))
            self.cnt[e] = 0
            self.seen[e] = {}
            self.q[e] = []

    def op(self, e, fn, after, inc=True):
        w = []
        for s, v in flat(after, []):
            if self.seen[e].get(s, 0) < v:
                self.seen[e][s] = v
                w = [x for x in w if x[0] != s] + [(s, v)]
        if inc:
            self.cnt[e] += 1
        self.q[e].append((w, fn, (e, 1) if inc else None))
        return (e, self.cnt[e])

    def dma(self, e, sem, out, in_, *after):
        if sem not in self.sem:
            self.sem[sem] = self.ctx.enter_context(self.nc.semaphore("d_" + sem))
            self.cnt[sem] = 0
        self.op(e, lambda g: g.dma_start(out, in_), after, inc=False)
        w, fn, _ = self.q[e][-1]
        self.q[e][-1] = (w, fn, (sem, 16))
        self.cnt[sem] += 16
        return (sem, self.cnt[sem])

    def wait(self, e, *after):
        self.op(e, None, after, inc=False)

    def now(self, *engines):
        return [(e, self.cnt[e]) for e in (engines or ("pe", "dve", "act", "pool")) if self.cnt[e]]

    def play(self, e, eng):
        for w, fn, inc in self.q[e]:
            for s, v in w:
                eng.wait_ge(self.sem[s], v)
            if fn is not None:
                i = fn(eng)
                if inc:
                    i.then_inc(self.sem[inc[0]], inc[1])


class Buf:
    def __init__(self, t, lo, hi, dep):
        self.t, self.lo, self.hi, self.dep = t, lo, hi, dep

    def __getitem__(self, k):
        return self.t[k]


class Mem:

    def __init__(self, nc, lo, hi):
        self.nc, self.free_, self.n = nc, [(lo, hi, [])], 0

    def get(self, shape, dt=F32, high=False):
        size = (int(np.prod(shape[1:])) * 4 + 31) // 32 * 32
        fr = sorted(self.free_)
        runs, i = [], 0
        while i < len(fr):
            j = i
            while j + 1 < len(fr) and fr[j + 1][0] == fr[j][1]:
                j += 1
            if fr[j][1] - fr[i][0] >= size:
                runs.append((fr[i][0], fr[j][1]))
            i = j + 1
        assert runs, ("full", shape, [(a, b - a) for a, b, _ in fr])
        lo = runs[-1][1] - size if high else runs[0][0]
        hi = lo + size
        dep, rest = [], []
        for a, b, t in fr:
            if b <= lo or a >= hi:
                rest.append((a, b, t))
                continue
            dep += t
            if a < lo:
                rest.append((a, lo, t))
            if b > hi:
                rest.append((hi, b, t))
        self.free_ = rest
        self.n += 1
        return Buf(self.nc.alloc_sbuf_tensor_at(f"t{self.n}", list(shape), dt, offset=lo), lo, hi, dep)

    def put(self, buf, *after):
        self.free_.append((buf.lo, buf.hi, flat(after, [])))


def rr(ap, pattern, **k):
    return ap.rearrange(pattern, **k)


def bc(ap, n):
    return ap.unsqueeze(len(ap.shape)).to_broadcast(list(ap.shape) + [n])


class Prog:
    def __init__(self, nc, ctx, dram):
        self.Q = Queues(nc, ctx)
        self.nc, self.dram = nc, dram
        self.M = Mem(nc, (nc.sbuf_base + 31) // 32 * 32, nc.sbuf_usable_end // 32 * 32)
        self.ps = [ctx.enter_context(nc.psum_tensor(f"ps{i}", [128, 512], F32)) for i in range(8)]
        self.pfree = [[] for _ in range(8)]
        self.pn = 0
        self.taps = []
        self.sg_n = 0

    def tt(self, e, out, a, b, o, *after):
        return self.Q.op(e, lambda g: g.tensor_tensor(out, a, b, o), after)

    def ts(self, e, out, a, s1, s2, o1, o2, *after):
        if s2 is None:
            return self.Q.op(e, lambda g: g.tensor_scalar(out, a, s1, None, o1), after)
        return self.Q.op(e, lambda g: g.tensor_scalar(out, a, s1, s2, o1, o2), after)

    def stt(self, out, a, s, b, o1, o2, *after):
        return self.Q.op("dve", lambda g: g.scalar_tensor_tensor(out=out, in0=a, scalar=s, in1=b, op0=o1, op1=o2), after)

    def act(self, out, a, f, *after, **k):
        return self.Q.op("act", lambda g: g.activation(out, a, f, **k), after)

    def cp(self, e, out, a, *after):
        if e == "act":
            return self.Q.op("act", lambda g: g.copy(out, a), after)
        return self.Q.op(e, lambda g: g.tensor_copy(out, a), after)

    def red(self, out, a, o, *after):
        return self.Q.op("dve", lambda g: g.tensor_reduce(out, a, AX, o), after)

    def rcp(self, out, a, *after):
        return self.Q.op("dve", lambda g: g.reciprocal(out, a), after)

    def mset(self, e, out, v, *after):
        return self.Q.op(e, lambda g: g.memset(out, v), after)

    def mm(self, out, l, r, start, stop, *after, inc=False, share=False):
        return self.Q.op("pe", lambda g: g.matmul(out, l, r, start=start, stop=stop, skip_group_check=share), after, inc=inc)

    def tr(self, out, a, *after, inc=False):
        n = a.shape[0]
        return self.Q.op("pe", lambda g: g.transpose(out, a, self.ident[0:n, 0:n]), after, inc=inc)

    def bank(self):
        i = self.pn % 8
        self.pn += 1
        t = self.pfree[i]
        assert t is not None, "a bank in use"
        self.pfree[i] = None
        return i, self.ps[i], t

    def done(self, i, *after):
        assert self.pfree[i] is None
        self.pfree[i] = flat(after, [])

    def tap(self, name, ap, *after):
        if name in self.dram:
            self.xt_ = [self.xt_, self.Q.dma("sp", "tap", self.dram[name], ap, after, self.Q.now())]

    def start(self, first=0, last=None):
        Q, M = self.Q, self.M
        self.C = M.get([128, NCONST])
        self.COL = M.get([128, NROW])
        self.HD = M.get([128, 4])
        self.CV = M.get([128, 8])
        self.SC = M.get([128, 8])
        self.POS = M.get([128, 2], I32)
        self.X = M.get([128, 2, D])
        self.G = [M.get([128, D]) for _ in range(1)]
        self.ones = M.get([128, 128])
        self.AB = M.get([128, 16])
        self.acc = [M.get([128, 256]) for _ in range(2)]
        self.accfree = [[], []]
        self.mod = [M.get([128, 3, 8]) for _ in range(2)]
        self.W = [M.get([128, CH]) for _ in range(NW)]
        self.H = [M.get([128, CH], F32R) for _ in range(NH)]
        self.L = [M.get([128, CH], F32R) for _ in range(NH)]
        const = lambda k: self.C[:, CW[k][0]:CW[k][0] + CW[k][1]]
        self.ident, self.neg, self.causal, self.lvl, self.both = (const(k) for k in ("ident", "neg", "causal", "lvl", "both"))
        self.ones64, self.rmask, self.freq, self.sgn, self.mhalf = (const(k) for k in ("ones64", "rmask", "freq", "sgn", "mhalf"))
        self.tc = Q.dma("act", "c", self.C[:, :], self.dram["cst"])
        self.tc2 = Q.dma("act", "c2", self.COL[:, :], self.dram["cols"])
        self.th = Q.dma("act", "h", self.HD[:, :], self.dram["heads"])
        self.tcv = Q.dma("act", "cv", self.CV[:, :], self.dram["c"])
        self.tpos = Q.dma("act", "pos", self.POS[:, :], self.dram["pos"])
        self.tones = self.mset("pool", self.ones[:, :], 1.0)
        self.S = SCHED[first:last]
        self.first = first
        self.wfree = [[] for _ in range(NW)]
        self.hfree = [[] for _ in range(NH)]
        self.landed, self.ready, self.where = {}, {}, {}
        self.nd = self.np_ = self.nt = self.nh = self.na = 0
        self.pending = []
        self.gate_t = [[], []]
        self.mod_t = [{}, {}]
        self.tsc = self.act(self.SC[:, :], self.CV[:, :], ACT.Silu, self.tcv)
        for _ in range(NW):
            self.load()

    def load(self):
        n = self.nd
        if n >= len(self.S):
            return
        self.nd += 1
        w = n % NW
        sz = 8 * width(self.S[n])
        self.landed[n] = self.Q.dma("sp", f"w{w}", self.W[w][:, 0:sz], self.dram["stream"][self.first + n][:, 0:sz], self.wfree[w])

    def prepare(self):
        n = self.np_
        if n >= len(self.S):
            return
        self.np_ += 1
        w = n % NW
        c = self.S[n]
        if c[0] == "ada":
            self.ada_chunk(n, c, self.W[w])
        else:
            h = self.nh % NH
            self.nh += 1
            sz = 8 * width(c)
            t1 = self.cp("act", self.H[h][:, 0:sz], self.W[w][:, 0:sz], self.landed[n], self.hfree[h])
            t2 = self.tt("dve", self.L[h][:, 0:sz], self.W[w][:, 0:sz], self.H[h][:, 0:sz], SUB, t1)
            self.wfree[w] = [t1, t2]
            self.ready[n] = [t1, t2]
            self.where[n] = h
        self.load()

    def take(self, what):
        pend, self.pending = self.pending, []
        for f in pend:
            f()
        while self.S[self.nt][0] == "ada":
            while self.np_ <= self.nt:
                self.prepare()
            self.nt += 1
        n = self.nt
        assert self.S[n] == what, (self.S[n], what)
        self.nt += 1
        want, k = n, NH - 1
        while k and want + 1 < len(self.S):
            want += 1
            if self.S[want][0] != "ada":
                k -= 1
        while self.np_ <= want:
            if self.np_ < len(self.S) and self.S[self.np_][0] != "ada" and self.nh - self.taken() >= NH:
                break
            if self.np_ >= len(self.S):
                break
            self.prepare()
        return self.where[n], self.H[self.where[n]], self.L[self.where[n]], self.ready[n]

    def taken(self):
        return sum(1 for c in self.S[:self.nt - 1] if c[0] != "ada")

    def flush(self):
        while self.nt < len(self.S) and self.S[self.nt][0] == "ada":
            while self.np_ <= self.nt:
                self.prepare()
            self.nt += 1
        pend, self.pending = self.pending, []
        for f in pend:
            f()

    def ada_chunk(self, n, c, W):
        _, l, j, v, q = c
        s = self.na % 2
        self.na += 1
        A = self.acc[s]
        Wv = rr(W[:, :], "p (k n) -> p k n", k=8)
        t = self.ts("dve", A[:, :], Wv[:, 0, :], self.SC[:, 0:1], None, MUL, None, self.landed[n], self.tsc, self.accfree[s])
        for k in range(1, 8):
            t = self.stt(A[:, :], Wv[:, k, :], self.SC[:, k:k + 1], A[:, :], MUL, ADD, t)
        self.wfree[n % NW] = [t]
        self.accfree[s] = None
        p = (l * 3 + j) % 2

        def finish():
            b, P, f = self.bank()
            if v < 2:
                for i in range(2):
                    u = self.mm(P[:, i:i + 1], A[:, i * 128:i * 128 + 128], self.ones[:, 0:1], True, True, t, f, self.tones, inc=i == 1)
                r = ROW["ada_b"] + l * 72 + (j * 3 + v) * 8 + q * 2
                o = self.mod[p][:, v, q * 2:q * 2 + 2]
                key = (l, j, v)
                x = self.tt("dve", o, P[:, 0:2], self.COL[:, r:r + 2], ADD, u, self.tc2, self.mod_t[p].get("free"))
                if v == 1:
                    x = self.ts("dve", o, o, 1.0, None, ADD, None, x)
                self.mod_t[p][key] = x
            else:
                u = self.mm(P[:, 0:256], self.ones[:, :], A[:, :], True, True, t, f, self.tones, inc=True)
                g = self.G[0]
                x = self.tt("dve", g[:, q * 256:q * 256 + 256], P[:, 0:256], g[:, q * 256:q * 256 + 256], ADD, u, self.tgb)
                a, m = (1.0, 0.5) if j != 1 else (1.0, 1.0)
                x2 = self.ts("dve", g[:, q * 256:q * 256 + 256], g[:, q * 256:q * 256 + 256], a, m, ADD, MUL, x)
                self.gate_t[0] = x2
                self.gkey = (l, j, q)
            self.done(b, x)
            self.accfree[s] = [u]

        if self.pending and len(self.pending) >= 1:
            p0 = self.pending.pop(0)
            p0()
        self.pending.append(finish)

    def gate_bias(self, l, j):
        self.tgb = self.Q.dma("pool", "gb", self.G[0][:, :], self.dram["vec"][VEC["gate"] + l * 3 + j:VEC["gate"] + l * 3 + j + 1, :].to_broadcast([128, D]),
                              self.gate_free)

    def up(self, h, H, L, rd, xh, xl, xt, n, cb):
        Hv = rr(H[:, 0:8 * n], "p (k n) -> p k n", k=8)
        Lv = rr(L[:, 0:8 * n], "p (k n) -> p k n", k=8)
        for m in range(n // 128):
            b, P, f = self.bank()
            w = [rd, xt, f]
            for k in range(8):
                o = slice(m * 128, m * 128 + 128)
                self.mm(P[:, 0:T], Hv[:, k, o], xh[:, k, :], k == 0, False, w)
                self.mm(P[:, 0:T], Hv[:, k, o], xl[:, k, :], False, False)
                t = self.mm(P[:, 0:T], Lv[:, k, o], xh[:, k, :], False, k == 7, inc=k == 7)
                w = []
            self.done(b, cb(m, P, t))
        self.hfree[h] = [t]
        return t

    def tokmajor(self, h, H, L, rd, xh, xl, xt, n, cb):
        Hv = rr(H[:, 0:8 * n], "p (k n) -> p k n", k=8)
        Lv = rr(L[:, 0:8 * n], "p (k n) -> p k n", k=8)
        for a in range(2):
            b, P, f = self.bank()
            w = [rd, xt, f]
            for k in range(8):
                o = slice(a * 128, a * 128 + 128)
                self.mm(P[:, 0:n], xh[:, k, o], Hv[:, k, :], k == 0, False, w)
                self.mm(P[:, 0:n], xh[:, k, o], Lv[:, k, :], False, False)
                t = self.mm(P[:, 0:n], xl[:, k, o], Hv[:, k, :], False, k == 7, inc=k == 7)
                w = []
            self.done(b, cb(a, P, t))
        self.hfree[h] = [t]
        return t

    def down(self, keys, nk, hh, hl, ht):
        B = [self.bank() for _ in range(4)]
        w = {i: B[i][2] for i in range(4)}
        for c, key in enumerate(keys):
            h, H, L, rd = self.take(key)
            Hv = rr(H[:, :], "p (k n) -> p k n", k=2)
            Lv = rr(L[:, :], "p (k n) -> p k n", k=2)
            for a in range(2):
                for kk in range(2):
                    k = 2 * c + kk
                    xh, xl = hh[:, k, a * 128:a * 128 + 128], hl[:, k, a * 128:a * 128 + 128]
                    for n in range(2):
                        P = B[2 * a + n][1]
                        s = slice(n * 512, n * 512 + 512)
                        self.mm(P[:, :], xh, Hv[:, kk, s], k == 0, False, rd, ht(k), w[2 * a + n])
                        self.mm(P[:, :], xh, Lv[:, kk, s], False, False)
                        t = self.mm(P[:, :], xl, Hv[:, kk, s], False, k == nk - 1, inc=(k == nk - 1) or (kk == 1 and n == 1))
                        if k == nk - 1:
                            w[2 * a + n] = t
            self.hfree[h] = [t]
        return [(B[i][0], B[i][1], w[i]) for i in range(4)]

    def stats(self, r, st, a, *after):
        t = []
        for i in range(2):
            t.append(self.Q.op("dve", lambda g, i=i: g.bn_stats(st[:, a, 4 + 6 * i:10 + 6 * i], r[:, a, i * 512:i * 512 + 512]), after))
        t = self.Q.op("dve", lambda g: g.bn_aggr(st[:, a, 0:2], st[:, a, 4:16]), t)
        t = self.ts("pool", st[:, a, 2:3], st[:, a, 1:2], 1e-5, None, ADD, None, t)
        return self.tt("pool", st[:, a, 3:4], st[:, a, 2:3], self.mhalf[:, 0:1], ALU.pow, t, self.tc)

    def norm(self, r, st, a, tr, g, b, tgb, last=False):
        t = self.ts("dve", r[:, a, :], r[:, a, :], st[:, a, 0:1], st[:, a, 3:4], SUB, MUL, tr)
        e = "dve" if last else "pool"
        t1 = self.tt(e, self.X[:, a, :], r[:, a, :], g, MUL, t, tgb, self.xfree)
        t2 = self.tt(e, self.X[:, a, :], self.X[:, a, :], b, ADD, t1)
        return t, t2

    def fold(self, cols):
        A, B = self.AB[:, 0:8], self.AB[:, 8:16]
        g, b, mod = cols
        w = self.abfree
        if mod is None:
            t1 = self.cp("dve", A, g, self.tc2, w)
            t2 = self.cp("dve", B, b, self.tc2, w)
            return [t1, t2]
        p, l, j = mod
        m = self.mod[p]
        tm = [v for k, v in self.mod_t[p].items()]
        t1 = self.tt("dve", A, g, m[:, 1, :], MUL, tm, self.tc2, w)
        t2 = self.tt("dve", B, b, m[:, 1, :], MUL, tm, self.tc2, w)
        t2 = self.tt("dve", B, B, m[:, 0, :], ADD, t2)
        self.mod_t[p] = {"free": [t1, t2]}
        return [t1, t2]

    def to_cols(self, r, tr, tab):
        tmp = self.M.get([128, 2, T])
        self.XH = self.M.get([128, 8, T], F32R, high=True)
        self.XL = self.M.get([128, 8, T], F32R, high=True)
        tf = [tmp.dep, tmp.dep]
        out = []
        for f in range(8):
            b, P, fr = self.bank()
            for a in range(2):
                u = self.tr(P[:, a * 128:a * 128 + 128], r[:, a, f * 128:f * 128 + 128], tr[a], fr, self.tc, inc=a == 1)
            s = f % 2
            A, B = self.AB[:, f:f + 1], self.AB[:, 8 + f:9 + f]
            t1 = self.act(self.XH[:, f, :], P[:, 0:T], ACT.Identity, u, tab, self.XH.dep, scale=A, bias=B)
            t2 = self.ts("dve", tmp[:, s, :], P[:, 0:T], A, B, MUL, ADD, u, tab, tf[s], t1)
            t3 = self.tt("dve", self.XL[:, f, :], tmp[:, s, :], self.XH[:, f, :], SUB, t2, t1, self.XL.dep)
            tf[s] = t3
            self.done(b, t1, t2)
            out += [t1, t3]
        self.abfree = out
        self.M.put(tmp, out)
        return out

    def post(self, banks, gate, rows, cols, last=False):
        Q, M = self.Q, self.M
        R = M.get([128, 2, D])
        GB = M.get([128, 2, D])
        st = M.get([128, 2, 16])
        tg = [Q.dma("pool", "lg", GB[:, i, :], self.dram["vec"][rows[i]:rows[i] + 1, :].to_broadcast([128, D]), GB.dep, Q.now("dve")) for i in range(2)]
        ts_ = []
        for i, (b, P, t) in enumerate(banks):
            a, n = divmod(i, 2)
            s = slice(n * 512, n * 512 + 512)
            if gate:
                t = self.tt("dve", R[:, a, s], P[:, :], self.G[0][:, s], MUL, t, self.gate_t[0], R.dep)
                self.done(b, t)
                t = self.stt(R[:, a, s], self.X[:, a, s], ALPHA, R[:, a, s], MUL, ADD, t, self.xt_)
            else:
                t = self.stt(R[:, a, s], self.X[:, a, s], ALPHA, P[:, :], MUL, ADD, t, self.xt_, R.dep)
                self.done(b, t)
            ts_.append(t)
            if n == 1:
                ts_.append(self.stats(R, st, a, ts_, st.dep))
        self.gate_free = ts_
        self.xfree = ts_
        tn, tx = [], []
        if cols is not None:
            tab = self.fold(cols)
        for a in range(2):
            t1, t2 = self.norm(R, st, a, ts_, GB[:, 0, :], GB[:, 1, :], tg, last=last)
            tn.append(t1)
            tx.append(t2)
        self.xt_ = tx
        out = None
        if cols is not None:
            out = self.to_cols(R, tn, tab)
        M.put(R, Q.now())
        M.put(GB, Q.now())
        M.put(st, Q.now())
        return out

    def ffn1(self, l, i, xt):
        M = self.M
        self.gate_bias(l, 2 * i)
        hh = M.get([128, NF, T], F32R)
        hl = M.get([128, NF, T], F32R)
        sa = M.get([128, 4, T])
        hf = M.get([128, 2, T])
        ht = {}
        sfree = [sa.dep] * 4
        hfr = [hf.dep] * 2
        for m in range(NF // 2):
            sil = {}

            def on_a(k, P, t):
                s = (2 * m + k) % 4
                sil[k] = self.act(sa[:, s, :], P[:, 0:T], ACT.Silu, t, sfree[s])
                return sil[k]

            def on_b(k, P, t):
                f = 2 * m + k
                s, u = f % 4, f % 2
                t1 = self.tt("dve", hf[:, u, :], P[:, 0:T], sa[:, s, :], MUL, t, sil[k], hfr[u])
                t2 = self.cp("act", hh[:, f, :], hf[:, u, :], t1, hh.dep)
                t3 = self.tt("dve", hl[:, f, :], hf[:, u, :], hh[:, f, :], SUB, t2, hl.dep)
                sfree[s] = t1
                hfr[u] = t3
                ht[f] = [t2, t3]
                return t1

            h, H, L, rd = self.take(("w13", l, i, 0, m))
            self.up(h, H, L, rd, self.XH, self.XL, xt, 256, on_a)
            h, H, L, rd = self.take(("w13", l, i, 1, m))
            t = self.up(h, H, L, rd, self.XH, self.XL, xt, 256, on_b)
        M.put(self.XH, t)
        M.put(self.XL, t)
        banks = self.down([("w2", l, i, k) for k in range(NF // 2)], NF, hh, hl, lambda k: ht[k])
        for b in (hh, hl, sa, hf):
            M.put(b, self.Q.now())
        return banks

    def ffn2(self, l, xt):
        M = self.M
        hh = M.get([128, NF, T], F32R)
        hl = M.get([128, NF, T], F32R)
        ya = M.get([128, 4, T])
        yb = M.get([128, 2, T])
        hf = M.get([128, 2, T])
        ht = {}
        afree, bfree, hfr = [ya.dep] * 4, [yb.dep] * 2, [hf.dep] * 2

        def conv(y, P, r, t, fr):
            c = lambda tap: self.COL[:, ROW["cw"] + (l * 3 + tap) * 44 + r:ROW["cw"] + (l * 3 + tap) * 44 + r + 1]
            bb = self.COL[:, ROW["cb"] + l * 44 + r:ROW["cb"] + l * 44 + r + 1]
            t1 = self.act(y, P[:, 0:T], ACT.Identity, t, fr, self.tc2, scale=c(1), bias=bb)
            t2 = self.stt(y[:, 1:T], P[:, 0:T - 1], c(0), y[:, 1:T], MUL, ADD, t1)
            return self.stt(y[:, 0:T - 1], P[:, 1:T], c(2), y[:, 0:T - 1], MUL, ADD, t2)

        for m in range(NF // 2):
            sil = {}

            def on_a(k, P, t):
                f = 2 * m + k
                y = ya[:, f % 4, :]
                t1 = conv(y, P, f, t, afree[f % 4])
                sil[k] = self.act(y, y, ACT.Silu, t1)
                return t1

            def on_b(k, P, t):
                f = 2 * m + k
                u = f % 2
                y = yb[:, u, :]
                t1 = conv(y, P, 22 + f, t, bfree[u])
                t2 = self.tt("dve", hf[:, u, :], y, ya[:, f % 4, :], MUL, t1, sil[k], hfr[u])
                afree[f % 4] = bfree[u] = t2
                t3 = self.cp("act", hh[:, f, :], hf[:, u, :], t2, hh.dep)
                t4 = self.tt("dve", hl[:, f, :], hf[:, u, :], hh[:, f, :], SUB, t3, hl.dep)
                hfr[u] = t4
                ht[f] = [t3, t4]
                return t1

            h, H, L, rd = self.take(("wup", l, 0, m))
            self.up(h, H, L, rd, self.XH, self.XL, xt, 256, on_a)
            h, H, L, rd = self.take(("wup", l, 1, m))
            t = self.up(h, H, L, rd, self.XH, self.XL, xt, 256, on_b)
        M.put(self.XH, t)
        M.put(self.XL, t)
        banks = self.down([("wdn", l, k) for k in range(NF // 2)], NF, hh, hl, lambda k: ht[k])
        for b in (hh, hl, ya, yb, hf):
            M.put(b, self.Q.now())
        return banks

    def mixer1(self, l, xt):
        Q, M = self.Q, self.M
        COL = self.COL
        self.gate_bias(l, 1)
        cols = mixer1_cols()
        gt = M.get([128, 2, 128])
        gq = M.get([128, 9, T])
        cq = M.get([128, 6, T])
        mq = M.get([128, 4, T])
        zs = M.get([128, 2, 384])
        so = M.get([128, 2, 384])
        mv = M.get([128, 2, 256])
        vx = M.get([128, 2, 6, 65])
        t0 = self.mset("pool", gt[:, :, :], 0.0, gt.dep)
        t1 = self.mset("pool", vx[:, :, :, :], 1.0, vx.dep)
        tg = {}
        ready = {}

        def gates(a, P, t):
            o = []
            for src, dst in ((0, 0), (6, 64), (12, 96), (18, 32)):
                o.append(self.cp("dve", gt[:, a, dst:dst + 6], P[:, src:src + 6], t, t0))
            tg[a] = o
            return o

        def fm(g, P, t):
            if g < 15:
                y = gq[:, g, :] if g < 9 else cq[:, g - 9, :]
                dep = gq.dep if g < 9 else cq.dep
                r = ROW["gconv"] + l * 36 + g if g < 9 else ROW["mconv"] + l * 24 + g - 9
                n = 9 if g < 9 else 6
                w = [COL[:, r + tap * n:r + tap * n + 1] for tap in range(4)]
                u = self.act(y, P[:, 0:T], ACT.Identity, t, dep, self.tc2, scale=w[3])
                for j in range(1, 4):
                    u = self.stt(y[:, j:T], P[:, 0:T - j], w[3 - j], y[:, j:T], MUL, ADD, u)
                ready[g] = self.act(y, y, ACT.Silu, u)
                return u
            ready[g] = self.cp("act", mq[:, g - 15, :], P[:, 0:T], t, mq.dep)
            return ready[g]

        for n, (kind, c) in enumerate(cols):
            h, H, L, rd = self.take(("win", l, n))
            w = len(c)
            if n == 0:
                te = self.tokmajor(h, H, L, rd, self.XH, self.XL, xt, w, gates)
                rows = self.gate_rows(l, gt, tg)
            elif kind == "fm":
                te = self.up(h, H, L, rd, self.XH, self.XL, xt, w, lambda m, P, t, n=n: fm(2 * (n - 1) + m, P, t))
            else:
                def tmcb(a, P, t, n=n, w=w):
                    o = []
                    if n == 11:
                        o.append(self.act(zs[:, a, 0:256], P[:, 0:256], ACT.Silu, t, zs.dep))
                    elif n == 12:
                        o.append(self.act(zs[:, a, 256:384], P[:, 0:128], ACT.Silu, t, zs.dep))
                        o.append(self.act(so[:, a, 0:128], P[:, 128:256], ACT.Sigmoid, t, so.dep))
                    elif n == 13:
                        o.append(self.act(so[:, a, 128:384], P[:, 0:256], ACT.Sigmoid, t, so.dep))
                    elif n == 14:
                        o.append(self.cp("act", mv[:, a, :], P[:, 0:256], t, mv.dep))
                    elif n == 15:
                        o.append(self.cp("act", vx[:, a, 0:4, 0:64], rr(P[:, 0:256], "p (h d) -> p h d", h=4), t, t1))
                    else:
                        o.append(self.cp("act", vx[:, a, 4:6, 0:64], rr(P[:, 0:128], "p (h d) -> p h d", h=2), t, t1))
                    ready[("tm", n, a)] = o
                    return o
                te = self.tokmajor(h, H, L, rd, self.XH, self.XL, xt, w, tmcb)
        M.put(self.XH, te)
        M.put(self.XL, te)
        tz = [ready[("tm", n, a)] for n in (11, 12) for a in range(2)]
        tso = [ready[("tm", n, a)] for n in (12, 13) for a in range(2)]
        tmv = [ready[("tm", 14, a)] for a in range(2)]
        tvx = [ready[("tm", n, a)] for n in (15, 16) for a in range(2)]
        RT, RB, RC, DC, trt, trb, trc, tdc = rows

        mh = M.get([128, 8, T], F32R, high=True)
        ml = M.get([128, 8, T], F32R, high=True)
        tm = {}
        self.gdn(l, gq, [ready[g] for g in range(9)], zs, tz, RT, RB, RC, trt, trb, trc, mh, ml, tm)
        self.moba(mq, [ready[g] for g in range(15, 19)], mv, tmv, mh, ml, tm)
        self.mlstm(l, cq, [ready[g] for g in range(9, 15)], vx, tvx, so, tso, RT, RB, RC, DC, trt, trb, trc, tdc, mh, ml, tm)
        for b in (RT, RB, RC, DC, gt, self.PSEL):
            M.put(b, Q.now())
        banks = self.down([("wout", l, k) for k in range(4)], 8, mh, ml, lambda k: tm[k])
        M.put(mh, Q.now("pe"))
        M.put(ml, Q.now("pe"))
        return banks

    def gate_rows(self, l, gt, tg):
        Q, M = self.Q, self.M
        z = []
        mk = lambda s: M.get(s)
        RT, RB, RC, DC = mk([128, 2, 2, 128]), mk([128, T]), mk([128, T]), mk([128, 4])
        self.PSEL = mk([128, 9, 128])
        for i in range(9):
            r = 32 * (i // 3) + 2 * (i % 3)
            z.append(self.cp("pool", rr(self.PSEL[:, i, :], "p (a b) -> p a b", a=2), bc(self.ident[:, r:r + 2], 64), self.tc, self.PSEL.dep))
        A, B, y, e, gl, G, Mx, ir, dd = (mk([128, T + 1]) for _ in range(9))
        for t in (RB, RC, DC, A, B, y, Mx, ir):
            z.append(self.mset("pool", t[:, :], 0.0, t.dep))
        b, P, f = self.bank()
        for a in range(2):
            tp = self.tr(P[:, a * 128:a * 128 + 128], gt[:, a, :], tg[a], f, self.tc, inc=a == 1)
        q0, q1, q2, q3, q01 = slice(0, 32), slice(32, 64), slice(64, 96), slice(96, 128), slice(0, 64)
        hb = self.HD[:, 2 * l:2 * l + 1]
        w = slice(0, T)
        t = self.ts("dve", y[q01, w], P[q01, 0:T], hb[q01], self.sgn[q01], ADD, MUL, tp, z, self.th, self.tc)
        ti = self.ts("dve", ir[q3, w], P[q3, 0:T], hb[q3], None, ADD, None, tp, z, self.th)
        ti = self.cp("dve", ir[q1, w], ir[q3, w], ti)
        tb = self.act(A[q2, w], P[q2, 0:T], ACT.Exp, tp, z, t, ti, scale=-1.0)
        self.done(b, t, ti, tb)
        te = self.act(e[q01, w], y[q01, w], ACT.Abs, t, e.dep)
        te = self.act(e[q01, w], e[q01, w], ACT.Exp, te, scale=-1.0)
        te = self.act(e[q01, w], e[q01, w], ACT.Ln, te, bias=1.0)
        cf = self.act(dd[q01, 0:1], self.HD[q01, 2 * l + 1:2 * l + 2], ACT.Exp, self.th, dd.dep)
        cf = self.ts("dve", dd[q01, 1:2], dd[q01, 0:1], -1.0, None, MUL, None, cf)
        tb = self.ts("dve", A[q2, w], A[q2, w], 1.0, None, ADD, None, tb)
        tb = self.rcp(A[q2, w], A[q2, w], tb)
        t = self.stt(gl[q01, w], y[q01, w], 0.0, e[q01, w], MAX, ADD, te, gl.dep)
        t = self.ts("dve", gl[q01, w], gl[q01, w], dd[q01, 1:2], None, MUL, None, t, cf)
        tG = Q.op("dve", lambda g: g.tensor_tensor_scan(G[q01, w], self.rmask[q01, :], gl[q01, w], 0.0, MUL, ADD), [t, G.dep])
        tM = Q.op("dve", lambda g: g.tensor_tensor_scan(Mx[q1, 1:T + 1], gl[q1, w], ir[q1, w], 0.0, ADD, MAX), [t, ti])
        c4 = lambda ap: rr(ap, "p (c s) -> p c s", c=4)
        glast = lambda q: c4(G[q, w])[:, :, 63:64]
        td = self.tt("dve", c4(dd[q01, w]), glast(q01).to_broadcast([64, 4, 64]), c4(G[q01, w]), SUB, tG)
        o = [self.ts("dve", A[q0, w], G[q0, w], -1.0, None, MUL, None, tG)]
        o.append(self.tt("dve", A[q1, w], ir[q1, w], G[q1, w], SUB, tG))
        mL = c4(Mx[q1, 1:T + 1])[:, :, 63:64]
        mP = c4(Mx[q1, 0:T])[:, :, 0:1]
        t = self.tt("dve", e[q1, w], dd[q1, w], ir[q1, w], ADD, td, te)
        t = self.tt("dve", c4(e[q1, w]), c4(e[q1, w]), mL.to_broadcast([32, 4, 64]), SUB, t, tM)
        o.append(self.act(A[q3, w], e[q1, w], ACT.Exp, t))
        r = [self.cp("dve", RB[q0, :], G[q0, w], tG)]
        tr1 = self.tt("dve", RB[q1, :], G[q1, w], Mx[q1, 1:T + 1], SUB, tM)
        r.append(tr1)
        t = self.tt("dve", c4(gl[q1, w]), c4(RB[q1, :]), mP.to_broadcast([32, 4, 64]), ADD, tr1, tM)
        c = [self.act(RC[q1, :], gl[q1, w], ACT.Exp, t)]
        c.append(self.act(RC[q0, :], G[q0, w], ACT.Exp, tG))
        c.append(self.cp("dve", RC[q2, :], A[q2, w], tb))
        o.append(self.act(B[q0, w], dd[q0, w], ACT.Exp, td))
        o.append(self.act(B[q1, w], Mx[q1, 1:T + 1], ACT.Exp, tM, scale=-1.0))
        t = self.act(y[q2, w], G[q0, w], ACT.Exp, tG)
        o.append(self.tt("dve", B[q2, w], y[q2, w], A[q2, w], MUL, t, tb))
        g4 = G[q1, w][:, 63:T:64]
        t = self.tt("dve", ir[q1, 0:4], g4, Mx[q1, 0:T:64], ADD, r, o)
        t = self.tt("dve", ir[q1, 4:8], ir[q1, 0:4], Mx[q1, 64:T + 1:64], SUB, t)
        tdc = self.act(DC[q1, :], ir[q1, 4:8], ACT.Exp, t)
        b, P, f = self.bank()
        for i, S in enumerate((A, B)):
            for a in range(2):
                t = self.tr(P[:, (2 * i + a) * 128:(2 * i + a) * 128 + 128], S[:, a * 128:a * 128 + 128], o, f, inc=i + a == 2)
        trt = self.cp("act", rr(RT[:, :, :, :], "p i a c -> p (i a c)"), P[:, :], t, RT.dep)
        self.done(b, trt)
        for x in (A, B, y, e, gl, G, Mx, ir, dd):
            M.put(x, Q.now())
        return RT, RB, RC, DC, trt, [r, z], [c, z], [tdc, z]

    def sel(self, K, r, n):
        if n == 1:
            return self.ident[0:K, r:r + 1].to_broadcast([K, 128])
        return self.PSEL[0:K, (r // 32) * 3 + (r % 32) // 2, :]

    def decays(self, q, RT, RB, trt, trb):
        Dk = self.M.get([128, 12, 128])
        out = []
        for g in range(4):
            b, P, f = self.bank()
            for j in range(3):
                u = 3 * g + j
                h, a = 2 * ((u % 6) // 2) + u // 6, u % 2
                t = self.mm(P[:, j * 128:j * 128 + 128], self.sel(64, 32 * q + h, 1), RB[0:64, a * 128:a * 128 + 128], True, True, trb, f, inc=j == 2)
            o = []
            for j in range(3):
                u = 3 * g + j
                h, a = 2 * ((u % 6) // 2) + u // 6, u % 2
                o.append(self.stt(Dk[:, u, :], P[:, j * 128:j * 128 + 128], RT[:, 0, a, 32 * q + h:32 * q + h + 1], self.neg, ADD, ADD, t, trt, Dk.dep))
            self.done(b, o)
            out.append(self.act(Dk[:, 3 * g:3 * g + 3, :], Dk[:, 3 * g:3 * g + 3, :], ACT.Exp, o))
        return Dk, out

    def units(self, lT, rT, tin, cb):
        for g in range(4):
            b, P, f = self.bank()
            for j in range(3):
                u = 3 * g + j
                par, pr, a = u // 6, (u % 6) // 2, u % 2
                rs, cs = slice(64 * par, 64 * par + 64), slice(a * 128, a * 128 + 128)
                t = self.mm(P[:, j * 128:j * 128 + 128], lT[rs, pr, cs], rT[rs, pr, cs], True, True, tin, f, inc=j == 2)
            self.done(b, cb(g, P, t))

    def pairs(self, K, q, R, tr, cb):
        for p in range(3):
            b, P, f = self.bank()
            t = self.mm(P[:, 0:T], self.sel(K, 32 * q + 2 * p, 2), R[0:K, :], True, True, tr, f, inc=True)
            self.done(b, cb(p, P, t))

    def tok(self, src, tin, cb):
        for a in range(2):
            b, P, f = self.bank()
            for p in range(3):
                t = self.tr(P[:, p * 128:p * 128 + 128], src[:, p, a * 128:a * 128 + 128], tin, f, inc=p == 2)
            self.done(b, cb(a, P, t))

    def to_mix(self, src, tin, k, col, mh, ml, tm, tiles):
        tmp = self.M.get([128, T])
        tf = tmp.dep
        for i in range(tiles):
            b, P, f = self.bank()
            for a in range(2):
                t = self.tr(P[:, a * 128:a * 128 + 128], src[:, a, i * 128:i * 128 + 128], tin, f, inc=a == 1)
            c = col(i)
            t1 = self.act(mh[:, k + i, :], P[:, 0:T], ACT.Identity, t, mh.dep, self.tc2, scale=c)
            t2 = self.ts("dve", tmp[:, :], P[:, 0:T], c, None, MUL, None, t, tf, t1)
            self.done(b, t1, t2)
            tf = self.tt("dve", ml[:, k + i, :], tmp[:, :], mh[:, k + i, :], SUB, t2, t1, ml.dep)
            tm[k + i] = [t1, tf]
        self.M.put(tmp, tf)

    def gdn(self, l, gq, tq, zs, tz, RT, RB, RC, trt, trb, trc, mh, ml, tm):
        Q, M = self.Q, self.M
        h6 = lambda ap: rr(ap, "p (h d) -> p h d", h=6)
        rs = M.get([128, 6, T])
        tn = []
        for i in range(3):
            s = slice(2 * i, 2 * i + 2)
            t = self.act(rs[:, s, :], gq[:, s, :], ACT.Square, tq, rs.dep)
            b, P, f = self.bank()
            t = self.mm(P[:, :], self.ones64, rs[:, s, :], True, True, t, f, self.tc, inc=True)
            t = self.act(rs[:, s, :], P[:, :], ACT.Ln, t, bias=1e-6)
            self.done(b, t)
            t = self.act(rs[:, s, :], rs[:, s, :], ACT.Exp, t, scale=-0.5)
            for k in (2 * i, 2 * i + 1):
                tn.append(self.stt(gq[:, k, :], gq[:, k, :], 0.125 if k < 3 else 1.0, rs[:, k, :], MUL, MUL, t, tq))
        M.put(rs, Q.now("dve", "act"))
        qn, kn, vn_ = gq[:, 0:3, :], gq[:, 3:6, :], gq[:, 6:9, :]
        Dk, td = self.decays(0, RT, RB, trt, trb)
        kb = M.get([128, 3, T])
        qd = M.get([128, 3, T])
        GLc = M.get([128, 3, 4])
        tkb, tqd, tgl = [], [], []

        def on_beta(p, P, t):
            tkb.append(self.tt("dve", kb[:, p, :], kn[:, p, :], P[:, 0:T], MUL, t, tn, kb.dep))
            return tkb[-1]

        def on_g(p, P, t):
            tqd.append(self.tt("dve", qd[:, p, :], qn[:, p, :], P[:, 0:T], MUL, t, tn, qd.dep))
            tgl.append(self.cp("dve", GLc[:, p, :], P[:, 63:T:64], t, GLc.dep))
            return [tqd[-1], tgl[-1]]

        self.pairs(128, 2, RC, trc, on_beta)
        self.pairs(128, 0, RC, trc, on_g)
        AT = M.get([128, 12, 128])
        ta = [None] * 4

        def on_a(g, P, t):
            s = slice(3 * g, 3 * g + 3)
            ta[g] = self.tt("dve", rr(AT[:, s, :], "p u t -> p (u t)"), P[:, 0:384], rr(Dk[:, s, :], "p u t -> p (u t)"), MUL, t, td[g], AT.dep)
            return ta[g]

        tat = [None] * 4

        def on_q(g, P, t):
            s = slice(3 * g, 3 * g + 3)
            d = rr(Dk[:, s, :], "p u t -> p (u t)")
            tat[g] = self.tt("dve", d, P[:, 0:384], d, MUL, t, ta[g])
            return tat[g]

        self.units(kn, kb, [tn, tkb], on_a)
        self.units(kn, qn, tn, on_q)
        M.put(kb, Q.now("pe"))
        Xb = M.get([128, 12, 128])
        XT = M.get([128, 12, 128])
        Ub = M.get([128, 12, 128])
        Al = M.get([128, 12, 128])
        fl = lambda b, g: rr(b[:, 3 * g:3 * g + 3, :], "p u t -> p (u t)")
        idb = self.ident.unsqueeze(1).to_broadcast([128, 3, 128])
        tX, tXT, tU, tA, rA, rU = ([None] * 4 for _ in range(6))
        for lv in range(6):
            mk = self.lvl[:, lv * 128:lv * 128 + 128].unsqueeze(1).to_broadcast([128, 3, 128])
            for g in range(4):
                tA[g] = self.tt("dve" if g % 2 else "pool", Al[:, 3 * g:3 * g + 3, :], AT[:, 3 * g:3 * g + 3, :], mk, MUL, ta[g], rA[g], Al.dep)
            for g in range(4):
                b, P, f = self.bank()
                for j in range(3):
                    u = 3 * g + j
                    t = self.mm(P[:, j * 128:j * 128 + 128], Al[:, u, :], self.ident if lv == 0 else Xb[:, u, :], True, True, tA[g], tX[g], f, inc=j == 2)
                rA[g] = t
                if lv == 0:
                    tX[g] = self.tt("dve", Xb[:, 3 * g:3 * g + 3, :], idb, rr(P[:, 0:384], "p (u t) -> p u t", u=3), SUB, t, Xb.dep)
                    tXT[g] = self.tt("dve", XT[:, 3 * g:3 * g + 3, :], idb, Al[:, 3 * g:3 * g + 3, :], SUB, tA[g], XT.dep)
                    rA[g] = [t, tXT[g]]
                    self.done(b, tX[g])
                else:
                    tU[g] = self.cp("act", fl(Ub, g), P[:, 0:384], t, Ub.dep, rU[g])
                    self.done(b, tU[g])
            if lv == 0:
                continue
            for g in range(4):
                if lv < 5:
                    b, P, f = self.bank()
                    for j in range(3):
                        u = 3 * g + j
                        t = self.mm(P[:, j * 128:j * 128 + 128], XT[:, u, :], Ub[:, u, :], True, True, tU[g], tXT[g], f, inc=j == 2)
                    tX[g] = self.tt("dve", fl(Xb, g), fl(Xb, g), P[:, 0:384], SUB, t, tX[g])
                    self.done(b, tX[g])
                b, P, f = self.bank()
                for j in range(3):
                    u = 3 * g + j
                    t = self.mm(P[:, j * 128:j * 128 + 128], Ub[:, u, :], XT[:, u, :], True, True, tU[g], tXT[g], f, inc=j == 2)
                rU[g] = t
                tXT[g] = self.tt("dve", fl(XT, g), fl(XT, g), P[:, 0:384], SUB, t, tXT[g])
                self.done(b, tXT[g])
        for b in (Xb, Ub, Al, AT):
            M.put(b, Q.now())
        kd = M.get([128, 2, 384])
        kg = M.get([128, 2, 384])
        vb = M.get([128, 2, 384])
        colv = lambda i, a, q: bc(RT[:, i, a, 32 * q:32 * q + 6], 64)
        tkd, tvb = [None] * 2, [None] * 2

        def on_k(a, P, t):
            t1 = self.tt("dve", h6(kd[:, a, :]), h6(P[:, 0:384]), colv(1, a, 0), MUL, t, trt, kd.dep)
            t2 = self.tt("dve", h6(kg[:, a, :]), h6(P[:, 0:384]), colv(1, a, 2), MUL, t, trt, kg.dep)
            tkd[a] = [t1, t2]
            return [t1, t2]

        def on_v(a, P, t):
            tvb[a] = self.tt("dve", h6(vb[:, a, :]), h6(P[:, 0:384]), colv(0, a, 2), MUL, t, trt, vb.dep)
            return tvb[a]

        self.tok(kn, tn, on_k)
        self.tok(vn_, tq, on_v)
        un = lambda h, a: (h % 2) * 6 + (h // 2) * 2 + a
        us = M.get([128, 2, 384])
        wT = M.get([128, 3, T])
        tu, tw = [], []
        for a in range(2):
            b, P, f = self.bank()
            for h in range(6):
                t = self.mm(P[:, h * 64:h * 64 + 64], XT[:, un(h, a), :], vb[:, a, h * 64:h * 64 + 64], True, True, tvb[a], tXT, f, inc=h == 5)
            tu.append(self.cp("act", us[:, a, :], P[:, 0:384], t, us.dep))
            self.done(b, tu[-1])
        for p in range(3):
            b, P, f = self.bank()
            for h in (2 * p, 2 * p + 1):
                for a in range(2):
                    t = self.mm(P[64 * (h % 2):64 * (h % 2) + 64, a * 128:a * 128 + 128], kg[:, a, h * 64:h * 64 + 64], XT[:, un(h, a), :], True, True, tkd, tXT, f, inc=(h % 2 == 1 and a == 1))
            tw.append(self.cp("act", wT[:, p, :], P[:, 0:T], t, wT.dep))
            self.done(b, tw[-1])
        M.put(XT, Q.now("pe"))
        M.put(vb, Q.now("pe"))
        M.put(kg, Q.now("pe"))
        S2 = M.get([128, 3, 128])
        vn = M.get([128, 2, 384])
        os_ = M.get([128, 2, 384])
        ts_ = self.mset("pool", S2[:, :, :], 0.0, S2.dep)
        to = []
        for a in range(2):
            bo, Po, fo = self.bank()
            tvn = []
            for n in (2 * a, 2 * a + 1):
                o = 64 * (n % 2)
                r, c = slice(o, o + 64), slice(64 * n, 64 * n + 64)
                b, P, f = self.bank()
                for p in range(3):
                    t = self.mm(P[r, p * 128:p * 128 + 128], wT[:, p, c], S2[:, p, :], True, True, ts_, tw, f, inc=p == 2)
                tv = self.tt("dve", vn[r, a, :], us[r, a, :], P[r, 0:384], SUB, t, tu, vn.dep)
                self.done(b, tv)
                tvn.append(tv)
                for p in range(3):
                    tq_ = self.mm(Po[r, p * 128:p * 128 + 128], qd[:, p, c], S2[:, p, :], p == 0, False, ts_, tqd, fo, inc=p == 2, share=True)
                if n == 3:
                    continue
                b, P, f = self.bank()
                for p in range(3):
                    t = self.mm(P[:, p * 128:p * 128 + 128], kd[r, a, p * 128:p * 128 + 128], vn[r, a, p * 128:p * 128 + 128], True, True, tv, tkd, f, inc=p == 2)
                ts_ = []
                for p in range(3):
                    for e in range(2):
                        q = slice(64 * e, 64 * e + 64)
                        qq = slice(p * 128 + 64 * e, p * 128 + 64 * e + 64)
                        ts_.append(self.stt(S2[q, p, q], S2[q, p, q], GLc[q, p, n:n + 1], P[q, qq], MUL, ADD, t, tq_, tgl))
                self.done(b, ts_)
            for h in range(6):
                t = self.mm(Po[:, h * 64:h * 64 + 64], Dk[:, un(h, a), :], vn[:, a, h * 64:h * 64 + 64], False, h == 5, tvn, tat, inc=h == 5, share=True)
            to.append(self.cp("act", os_[:, a, :], Po[:, 0:384], t, os_.dep))
            self.done(bo, to[-1])
        for b in (S2, vn, us, wT, kd, qd, Dk, GLc, gq):
            M.put(b, Q.now())
        sq = M.get([128, 2, 384])
        ms = M.get([128, 4, 6])
        tf = []
        for a in range(2):
            t = self.act(sq[:, a, :], os_[:, a, :], ACT.Square, to[a], sq.dep)
            t = self.red(ms[:, a, :], h6(sq[:, a, :]), ADD, t, ms.dep)
            t = self.ts("pool", ms[:, a, :], ms[:, a, :], 1 / 64, 1e-6, MUL, ADD, t)
            t = self.tt("pool", ms[:, 2 + a, :], ms[:, a, :], self.mhalf[:, 0:6], ALU.pow, t)
            t = self.tt("dve", h6(os_[:, a, :]), h6(os_[:, a, :]), bc(ms[:, 2 + a, :], 64), MUL, t)
            tf.append(self.tt("dve", os_[:, a, :], os_[:, a, :], zs[:, a, :], MUL, t, tz))
        self.to_mix(os_, tf, 0, lambda i: self.COL[:, ROW["gnorm"] + l:ROW["gnorm"] + l + 1], mh, ml, tm, 3)
        for b in (sq, ms, os_, zs):
            M.put(b, Q.now())

    def moba(self, mq, tq, mv, tv, mh, ml, tm):
        Q, M = self.Q, self.M
        S = M.get([128, 4, 384])
        PT = M.get([128, 4, 384])
        mx = M.get([128, 4, 8])
        tp = {}
        for h in (0, 2, 1, 3):
            r = slice(64 * (h % 2), 64 * (h % 2) + 64)
            b, P, f = self.bank()
            for a in range(2):
                n = 128 * (a + 1)
                t = self.mm(P[:, 128 * a:128 * a + n], mq[r, h // 2, a * 128:a * 128 + 128], mq[r, 2 + h // 2, 0:n], True, True, tq, f, inc=a == 1)
            c = [self.stt(S[:, h, 0:128], P[:, 0:128], 0.125, self.causal, MUL, ADD, t, S.dep),
                 self.stt(S[:, h, 256:384], P[:, 256:384], 0.125, self.causal, MUL, ADD, t, S.dep),
                 self.ts("dve", S[:, h, 128:256], P[:, 128:256], 0.125, None, MUL, None, t, S.dep)]
            self.done(b, c)
            for a in range(2):
                s = slice(0, 128) if a == 0 else slice(128, 384)
                t = self.Q.op("dve", lambda g, h=h, a=a, s=s: g.tensor_reduce(mx[:, h, a:a + 1], S[:, h, s], AX, MAX), [c, mx.dep])
                t = self.ts("dve", mx[:, h, 2 + a:3 + a], mx[:, h, a:a + 1], -1.0, None, MUL, None, t)
                t = self.act(S[:, h, s], S[:, h, s], ACT.Exp, t, bias=mx[:, h, 2 + a:3 + a], accum_out=mx[:, h, 4 + a:5 + a])
                t = self.rcp(mx[:, h, 6 + a:7 + a], mx[:, h, 4 + a:5 + a], t)
                tp[h, a] = self.ts("dve", S[:, h, s], S[:, h, s], mx[:, h, 6 + a:7 + a], None, MUL, None, t)
        tpt = {}
        for h in range(4):
            b, P, f = self.bank()
            for i in range(3):
                t = self.tr(P[:, i * 128:i * 128 + 128], S[:, h, i * 128:i * 128 + 128], tp[h, 0], tp[h, 1], f, inc=i == 2)
            tpt[h] = self.cp("act", PT[:, h, :], P[:, 0:384], t, PT.dep)
            self.done(b, tpt[h])
        for p in range(2):
            b, P, f = self.bank()
            for h in (2 * p, 2 * p + 1):
                r = slice(64 * (h % 2), 64 * (h % 2) + 64)
                d = slice(64 * h, 64 * h + 64)
                self.mm(P[r, 0:256], mv[:, 0, d], PT[:, h, 0:256], True, False, tpt[h], tv, f)
                t = self.mm(P[r, 128:256], mv[:, 1, d], PT[:, h, 256:384], False, True, inc=h % 2 == 1)
            t1 = self.cp("act", mh[:, 3 + p, :], P[:, 0:T], t, mh.dep)
            t2 = self.tt("dve", ml[:, 3 + p, :], P[:, 0:T], mh[:, 3 + p, :], SUB, t1, ml.dep)
            self.done(b, t1, t2)
            tm[3 + p] = [t1, t2]
        for b in (S, PT, mx, mq, mv):
            M.put(b, Q.now())

    def mlstm(self, l, cq, tq, vx, tvx, so, tso, RT, RB, RC, DC, trt, trb, trc, tdc, mh, ml, tm):
        Q, M = self.Q, self.M
        h6 = lambda ap: rr(ap, "p (h d) -> p h d", h=6)
        q, k = cq[:, 0:3, :], cq[:, 3:6, :]
        Dk, td = self.decays(1, RT, RB, trt, trb)
        qa = M.get([128, 3, T])
        DCc = M.get([128, 3, 4])
        tqa, tpp = [], [None] * 4

        def on_a(p, P, t):
            tqa.append(self.stt(qa[:, p, :], q[:, p, :], 0.125, P[:, 0:T], MUL, MUL, t, tq, qa.dep))
            return tqa[-1]

        self.pairs(128, 1, RC, trc, on_a)
        b, P, f = self.bank()
        for p in range(3):
            t = self.mm(P[:, 4 * p:4 * p + 4], self.sel(64, 32 + 2 * p, 2), DC[0:64, :], True, True, tdc, f, inc=p == 2)
        tdc = self.cp("dve", rr(DCc[:, :, :], "p a b -> p (a b)"), P[:, 0:12], t, DCc.dep)
        self.done(b, tdc)

        def on_p(g, P, t):
            d = rr(Dk[:, 3 * g:3 * g + 3, :], "p u t -> p (u t)")
            tpp[g] = self.stt(d, P[:, 0:384], 0.125, d, MUL, MUL, t, td[g])
            return tpp[g]

        self.units(k, q, tq, on_p)
        ks = M.get([128, 2, 384])
        tks = [None] * 2

        def on_k(a, P, t):
            tks[a] = self.tt("dve", h6(ks[:, a, :]), h6(P[:, 0:384]), bc(RT[:, 0, a, 96:102], 64), MUL, t, trt, ks.dep)
            return tks[a]

        self.tok(k, tq, on_k)
        un = lambda h, a: (h % 2) * 6 + (h // 2) * 2 + a
        Cx = M.get([128, 3, 130])
        nd = M.get([128, 2, 6, 65])
        ts_ = self.mset("pool", Cx[:, :, :], 0.0, Cx.dep)
        tn = []
        for a in range(2):
            bo, Po, fo = self.bank()
            for n in (2 * a, 2 * a + 1):
                o = 64 * (n % 2)
                r, c = slice(o, o + 64), slice(64 * n, 64 * n + 64)
                for p in range(3):
                    tq_ = self.mm(Po[r, p * 130:p * 130 + 130], qa[:, p, c], Cx[:, p, :], p == 0, False, ts_, tqa, fo, inc=p == 2, share=True)
                if n == 3:
                    continue
                b, P, f = self.bank()
                for p in range(3):
                    t = self.mm(P[:, p * 130:p * 130 + 130], ks[r, a, p * 128:p * 128 + 128], rr(vx[r, a, 2 * p:2 * p + 2, :], "p h d -> p (h d)"), True, True, tks, tvx, f, inc=p == 2)
                ts_ = []
                for p in range(3):
                    for e in range(2):
                        q_, cc = slice(64 * e, 64 * e + 64), slice(65 * e, 65 * e + 65)
                        ts_.append(self.stt(Cx[q_, p, cc], Cx[q_, p, cc], DCc[q_, p, n:n + 1], P[q_, p * 130 + 65 * e:p * 130 + 65 * e + 65], MUL, ADD, t, tq_, tdc))
                self.done(b, ts_)
            for h in range(6):
                t = self.mm(Po[:, h * 65:h * 65 + 65], Dk[:, un(h, a), :], vx[:, a, h, :], False, h == 5, tpp, tvx, inc=h == 5, share=True)
            tn.append(self.cp("act", rr(nd[:, a, :, :], "p h d -> p (h d)"), Po[:, 0:390], t, nd.dep))
            self.done(bo, tn[-1])
        for b in (Cx, ks, qa, Dk, DCc, cq, vx):
            M.put(b, Q.now())
        hc = M.get([128, 2, 384])
        sq = M.get([128, 2, 384])
        s = M.get([128, 2, 8, 6])
        tf = []
        for a in range(2):
            w = [tn[a], s.dep]
            t = self.ts("dve", s[:, a, 0, :], nd[:, a, :, 64], -1.0, None, MUL, None, w)
            t = self.tt("dve", s[:, a, 0, :], s[:, a, 0, :], nd[:, a, :, 64], MAX, t)
            t = self.tt("dve", s[:, a, 1, :], s[:, a, 0, :], RT[:, 1, a, 32:38], MAX, t, trt)
            t = self.rcp(s[:, a, 2, :], s[:, a, 1, :], t)
            t = self.tt("dve", h6(hc[:, a, :]), nd[:, a, :, 0:64], bc(s[:, a, 2, :], 64), MUL, t, hc.dep)
            t = self.tt("dve", hc[:, a, :], hc[:, a, :], so[:, a, :], MUL, t, tso)
            t = self.red(s[:, a, 3, :], h6(hc[:, a, :]), ADD, t)
            t = self.ts("dve", s[:, a, 3, :], s[:, a, 3, :], 1 / 64, None, MUL, None, t)
            tc = self.tt("dve", h6(hc[:, a, :]), h6(hc[:, a, :]), bc(s[:, a, 3, :], 64), SUB, t)
            t = self.act(sq[:, a, :], hc[:, a, :], ACT.Square, tc, sq.dep)
            t = self.red(s[:, a, 4, :], h6(sq[:, a, :]), ADD, t)
            t = self.ts("pool", s[:, a, 5, :], s[:, a, 4, :], 1 / 64, 1e-6, MUL, ADD, t)
            t = self.tt("pool", s[:, a, 6, :], s[:, a, 5, :], self.mhalf[:, 0:6], ALU.pow, t)
            tf.append(self.tt("dve", h6(hc[:, a, :]), h6(hc[:, a, :]), bc(s[:, a, 6, :], 64), MUL, t))
        self.to_mix(hc, tf, 5, lambda i: self.COL[:, ROW["mnorm"] + 3 * l + i:ROW["mnorm"] + 3 * l + i + 1], mh, ml, tm, 3)
        for b in (nd, hc, sq, s, so):
            M.put(b, Q.now())

    def mixer2(self, l, xt):
        Q, M = self.Q, self.M
        XH, XL = self.XH, self.XL
        qs = M.get([128, 4, T])
        K2 = M.get([128, 2, 4, T])
        B2 = M.get([128, 2, 4, T])
        hv = M.get([128, 2, 512])
        hg = M.get([128, 2, 512])
        dqk = M.get([128, 2, 1024])
        dv = M.get([128, 2, 512])
        xq = M.get([128, 4, T])
        R = {}
        lb = self.lower_bounds(l)

        def fm(n, m, P, t):
            i = 2 * (n % 2) + m
            if n < 2:
                R["q", i] = self.act(qs[:, i, :], P[:, 0:T], ACT.Silu, t, qs.dep)
                return R["q", i]
            if n < 6:
                d = (n - 2) // 2
                R["f", d, i] = self.act(K2[:, d, i, :], P[:, 0:T], ACT.Sigmoid, t, K2.dep)
                return R["f", d, i]
            R["x", i] = self.cp("act", xq[:, i, :], P[:, 0:T], t, xq.dep)
            return R["x", i]

        def tm(n, a, P, t):
            s = slice((n % 2) * 256, (n % 2) * 256 + 256)
            if n < 8:
                R["v", a, n % 2] = self.cp("act", hv[:, a, s], P[:, 0:256], t, hv.dep)
                return R["v", a, n % 2]
            if n < 10:
                R["g", a, n % 2] = self.act(hg[:, a, s], P[:, 0:256], ACT.Silu, t, hg.dep)
                return R["g", a, n % 2]
            if n < 14:
                o = (n - 10) * 256
                R["dqk", a, n] = self.cp("act", dqk[:, a, o:o + 256], P[:, 0:256], t, dqk.dep)
                return R["dqk", a, n]
            R["dv", a, n] = self.cp("act", dv[:, a, s], P[:, 0:256], t, dv.dep)
            return R["dv", a, n]

        def got(k):
            return [v for kk, v in R.items() if kk[0] == k]

        steps = None
        for n in range(18):
            h, H, L, rd = self.take(("win2", l, n))
            if n < 6 or n >= 16:
                te = self.up(h, H, L, rd, XH, XL, xt, 256, lambda m, P, t, n=n: fm(n, m, P, t))
            else:
                te = self.tokmajor(h, H, L, rd, XH, XL, xt, 256, lambda a, P, t, n=n: tm(n, a, P, t))
            if n == 5:
                steps = self.hg_levels(l, lb, qs, K2, B2, got("q"), got("f"), R)
            if steps:
                next(steps, None)
        M.put(XH, te)
        M.put(XL, te)
        mf = M.get([128, 8, T])
        eh = M.get([128, 8, T], F32R)
        el = M.get([128, 8, T], F32R)
        t = Q.dma("pool", "mem", mf[:, :, :], self.dram["memT"], mf.dep)
        fl = lambda b: rr(b[:, :, :], "p k t -> p (k t)")
        t1 = self.cp("act", fl(eh), fl(mf), t, eh.dep)
        t2 = self.tt("dve", fl(el), fl(mf), fl(eh), SUB, t1, el.dep)
        M.put(mf, t1, t2)
        mk = M.get([128, 4, T])
        mv = M.get([128, 2, 512])

        def mkc(n, m, P, t):
            R["mk", 2 * n + m] = self.cp("act", mk[:, 2 * n + m, :], P[:, 0:T], t, mk.dep)
            return R["mk", 2 * n + m]

        def mvc(n, a, P, t):
            s = slice((n % 2) * 256, (n % 2) * 256 + 256)
            R["mv", a, n] = self.cp("act", mv[:, a, s], P[:, 0:256], t, mv.dep)
            return R["mv", a, n]

        for n in range(4):
            h, H, L, rd = self.take(("wkv", l, n))
            if n < 2:
                te = self.up(h, H, L, rd, eh, el, [t1, t2], 256, lambda m, P, t, n=n: mkc(n, m, P, t))
            else:
                te = self.tokmajor(h, H, L, rd, eh, el, [t1, t2], 256, lambda a, P, t, n=n: mvc(n, a, P, t))
            next(steps, None)
        M.put(eh, te)
        M.put(el, te)
        for _ in steps:
            pass
        self.hgp = R["attn"]
        mh = M.get([128, 12, T], F32R, high=True)
        ml = M.get([128, 12, T], F32R, high=True)
        tmx = {}
        self.hgrn(l, qs, K2, B2, hv, got("v"), hg, got("g"), R, mh, ml, tmx)
        self.diff(l, dqk, got("dqk"), dv, got("dv"), mh, ml, tmx)
        self.memory(xq, got("x"), mk, got("mk"), mv, got("mv"), mh, ml, tmx)
        banks = self.down([("wout2", l, k) for k in range(6)], 12, mh, ml, lambda k: tmx[k])
        M.put(mh, Q.now("pe"))
        M.put(ml, Q.now("pe"))
        return banks

    def lower_bounds(self, l):
        if l == 0:
            return None
        Q, M = self.Q, self.M
        z = M.get([128, 2, 8, 4])
        t_ = []
        for d, name in enumerate(("lbf", "lbb")):
            c = [self.COL[:, ROW[name] + 4 * i:ROW[name] + 4 * i + 4] for i in range(2)]
            t = self.tt("dve", z[:, d, 0, :], c[0], c[1], MAX, z.dep, self.tc2)
            a = [self.tt("dve", z[:, d, 1 + i, :], c[i], z[:, d, 0, :], SUB, t) for i in range(2)]
            a = [self.act(z[:, d, 1 + i, :], z[:, d, 1 + i, :], ACT.Exp, a[i]) for i in range(2)]
            t = self.tt("dve", z[:, d, 3, :], z[:, d, 1, :], z[:, d, 2, :], ADD, a)
            t = self.rcp(z[:, d, 3, :], z[:, d, 3, :], t)
            a = [self.tt("dve", z[:, d, 1 + i, :], z[:, d, 1 + i, :], z[:, d, 3, :], MUL, t) for i in range(2)]
            t = self.tt("dve", z[:, d, 4, :], z[:, d, 1, :], z[:, d, 2, :], ADD, a)
            t = self.tt("dve", z[:, d, 4, :], z[:, d, 4, :], z[:, d, 1, :], SUB, t)
            t_.append(self.ts("dve", z[:, d, 5, :], z[:, d, 4, :], -1.0, 1.0, MUL, ADD, t))
        return z, t_

    def hg_levels(self, l, lb, qs, K2, B2, tq, tf, R):
        Q, M = self.Q, self.M
        lo = 2.0 ** -63
        E = M.get([128, 2, 4, T])
        fl = lambda x: rr(x, "p h t -> p (h t)")
        tk, tb = [], []
        for d in range(2):
            f = fl(K2[:, d, :, :])
            if lb is None:
                t = self.ts("dve", f, f, 1e-20, None, MAX, None, tf)
            else:
                z, tz = lb
                ts_ = [self.ts("dve", K2[:, d, h, :], K2[:, d, h, :], z[:, d, 5, h:h + 1], z[:, d, 4, h:h + 1], MUL, ADD, tf, tz) for h in range(4)]
                t = self.ts("dve", f, f, 1e-20, None, MAX, None, ts_)
            g, g2 = fl(B2[:, d, :, :]), fl(E[:, d, :, :])
            t1 = self.ts("dve", g, f, lo, None, MAX, None, t, B2.dep)
            t2 = self.ts("dve", g2, f, lo, 1 / lo, MIN, MUL, t, E.dep)
            t1 = self.act(g, g, ACT.Ln, t1)
            t2 = self.act(g2, g2, ACT.Ln, t2)
            tg = self.tt("dve", g2, g, g2, ADD, t1, t2)
            tk.append(self.ts("dve", f, f, -1.0, 1.0, MUL, ADD, t1, t2))
            for h in range(4):
                s = slice(None) if d == 0 else slice(T - 1, None, -1)
                tb.append(Q.op("dve", lambda g_, h=h, s=s, d=d: g_.tensor_tensor_scan(B2[:, d, h, s], self.rmask, E[:, d, h, s], 0.0, MUL, ADD), [tg]))
        if lb is not None:
            M.put(lb[0], Q.now("dve"))
        A = M.get([128, 8, 128])
        ta = self.mset("pool", A[:, :, :], 0.0, A.dep)
        KL = [M.get([128, 4, T]) for _ in range(2)]
        QL = [M.get([128, 4, T]) for _ in range(2)]
        kfree = [[x.dep, y.dep] for x, y in zip(KL, QL)]
        efree = tb
        todo = []

        def meet(Kl, Ql, mask, tin, s):
            nonlocal ta
            for g in range(2):
                b, P, f = self.bank()
                for j in range(4):
                    u = 4 * g + j
                    h, a = u // 2, u % 2
                    c = slice(a * 128, a * 128 + 128)
                    t = self.mm(P[:, j * 128:j * 128 + 128], Kl[:, h, c], Ql[:, h, c], True, True, tin, f, inc=j == 3)
                mb = mask.bitcast(I32).unsqueeze(1).to_broadcast([128, 4, 128])
                ta = Q.op("dve", lambda e, g=g, P=P, mb=mb: e.copy_predicated(A[:, 4 * g:4 * g + 4, :], mb, rr(P[:, :], "p (u t) -> p u t", u=4)), [t, ta])
                self.done(b, ta)
            if s is not None:
                kfree[s] = t

        t = self.tt("pool", fl(KL[1][:, :, :]), fl(K2[:, 0, :, :]), fl(K2[:, 1, :, :]), ADD, tk, kfree[1])
        todo.append(lambda t=t: meet(KL[1], qs, self.ident, [t, tq], 1))
        yield
        for lv in range(6):
            z = 1 << lv
            s = lv % 2
            v = lambda x: rr(fl(x), "p (n z) -> p n z", z=2 * z)
            te = []
            for d in range(2):
                b, e = v(B2[:, d, :, :]), v(E[:, d, :, :])
                ref = b[:, :, z - 1 + d:z + d].to_broadcast([128, 512 // z, z])
                lw, up = slice(0, z), slice(z, 2 * z)
                x, y = (lw, up) if d == 0 else (up, lw)
                te.append(self.tt("pool", e[:, :, x], ref, b[:, :, x], SUB, tb, efree))
                te.append(self.tt("pool", e[:, :, y], b[:, :, y], ref, SUB, tb, efree))
            t = self.act(rr(E[:, :, :, :], "p d h t -> p (d h t)"), rr(E[:, :, :, :], "p d h t -> p (d h t)"), ACT.Exp, te)
            w = []
            for o, src, x, y in ((KL[s], (K2[:, 0, :, :], K2[:, 1, :, :]), slice(0, z), slice(z, 2 * z)),
                                 (QL[s], (qs[:, :, :], qs[:, :, :]), slice(z, 2 * z), slice(0, z))):
                w.append(self.tt("dve", v(o[:, :, :])[:, :, x], v(src[0])[:, :, x], v(E[:, 0, :, :])[:, :, x], MUL, t, tk, tq, kfree[s]))
                w.append(self.tt("dve", v(o[:, :, :])[:, :, y], v(src[1])[:, :, y], v(E[:, 1, :, :])[:, :, y], MUL, t, tk, tq, kfree[s]))
            efree = w
            todo.append(lambda lv=lv, s=s, w=w: meet(KL[s], QL[s], self.both[:, lv * 128:lv * 128 + 128], w, s))
            todo.pop(0)()
            yield
        todo.pop(0)()
        for x in (*KL, *QL):
            M.put(x, Q.now("pe"))
        R["attn"] = (A, ta, tk, tb, E)
        yield

    def hgrn(self, l, qs, K2, B2, hv, tv, hg, tg, R, mh, ml, tmx):
        Q, M = self.Q, self.M
        A, ta, tk, tb, E = R["attn"]
        tq = [v for k, v in R.items() if k[0] == "q"]
        fl = lambda x: rr(x, "p h t -> p (h t)")
        c4 = lambda x: rr(fl(x), "p (n s) -> p n s", s=64)
        kt = M.get([128, 2, 2, 512])
        dc = M.get([128, 2, 16])
        tkt = {}
        for d in range(2):
            b = c4(B2[:, d, :, :])
            end = 63 if d == 0 else 0
            last = b[:, :, end:end + 1].to_broadcast([128, 16, 64])
            t = self.tt("dve", c4(E[:, d, :, :]), last, b, SUB, tb, Q.now("dve"))
            t = self.act(fl(E[:, d, :, :]), fl(E[:, d, :, :]), ACT.Exp, t)
            tkd = self.tt("dve", fl(E[:, d, :, :]), fl(E[:, d, :, :]), fl(K2[:, d, :, :]), MUL, t, tk)
            for a in range(2):
                bb, P, f = self.bank()
                for h in range(4):
                    t = self.tr(P[:, h * 128:h * 128 + 128], E[:, d, h, a * 128:a * 128 + 128], tkd, f, inc=h == 3)
                tkt[d, a] = self.cp("act", kt[:, d, a, :], P[:, :], t, kt.dep)
                self.done(bb, tkt[d, a])
            x = fl(B2[:, d, :, :])
            t = self.act(x, x, ACT.Exp, tkd, tb, tkt[d, 1])
            td = self.cp("dve", dc[:, d, :], c4(B2[:, d, :, :])[:, :, end], t, dc.dep)
            R["qe", d] = self.tt("dve", x, x, fl(qs[:, :, :]), MUL, td, tq)
            R["dc", d] = td
        M.put(E, Q.now("pe"))
        M.put(K2, Q.now("dve"))
        ST = [M.get([128, 512]) for _ in range(6)]
        tst = {}
        for d in range(2):
            prev = None
            for i in range(3):
                n = i if d == 0 else 3 - i
                a, o = n // 2, 64 * (n % 2)
                b, P, f = self.bank()
                for h in range(4):
                    c = slice(h * 128, h * 128 + 128)
                    t = self.mm(P[:, c], kt[o:o + 64, d, a, c], hv[o:o + 64, a, c], True, True, tkt[d, a], tv, f, inc=h == 3)
                if i == 0:
                    w = self.cp("act", ST[3 * d][:, :], P[:, :], t, ST[3 * d].dep)
                else:
                    w = [self.stt(ST[3 * d + i][:, h * 128:h * 128 + 128], ST[3 * d + i - 1][:, h * 128:h * 128 + 128],
                                  dc[:, d, 4 * h + n:4 * h + n + 1], P[:, h * 128:h * 128 + 128], MUL, ADD, t, prev, R["dc", d], ST[3 * d + i].dep) for h in range(4)]
                self.done(b, w)
                tst[d, i] = prev = w
        for x in (kt, dc, qs):
            M.put(x, Q.now())
        o_ = M.get([128, 2, 512])
        sq = M.get([128, 2, 512])
        ms = M.get([128, 4, 4])
        h4 = lambda ap: rr(ap, "p (h d) -> p h d", h=4)
        tf = []
        for a in range(2):
            b, P, f = self.bank()
            for h in range(4):
                c = slice(h * 128, h * 128 + 128)
                self.mm(P[:, c], A[:, 2 * h + a, :], hv[:, a, c], h == 0, False, ta, tv, f, share=True)
            for n in (2 * a, 2 * a + 1):
                r = slice(64 * (n % 2), 64 * (n % 2) + 64)
                for d in range(2):
                    i = n - 1 if d == 0 else 2 - n
                    if i < 0:
                        continue
                    for h in range(4):
                        c = slice(h * 128, h * 128 + 128)
                        t = self.mm(P[r, c], B2[:, d, h, 64 * n:64 * n + 64], ST[3 * d + i][:, c], False, n == 2 * a + 1 and h == 3 and (d == 1 or n == 3), R["qe", d], tst[d, i],
                                    inc=n == 2 * a + 1 and h == 3, share=True)
            t = self.cp("act", o_[:, a, :], P[:, :], t, o_.dep)
            self.done(b, t)
            tf.append(self.head_rms(o_, sq, ms, a, t, 1.0))
            tf[-1] = self.tt("dve", o_[:, a, :], o_[:, a, :], hg[:, a, :], MUL, tf[-1], tg)
        self.to_mix(o_, tf, 4, lambda i: self.COL[:, ROW["hnorm"] + l:ROW["hnorm"] + l + 1], mh, ml, tmx, 4)
        for x in (A, B2, *ST, o_, sq, ms, hv, hg):
            M.put(x, Q.now())

    def head_rms(self, o, sq, ms, a, tin, k):
        h4 = lambda ap: rr(ap, "p (h d) -> p h d", h=4)
        t = self.act(sq[:, a, :], o[:, a, :], ACT.Square, tin, sq.dep)
        t = self.red(ms[:, a, :], h4(sq[:, a, :]), ADD, t, ms.dep)
        t = self.ts("pool", ms[:, a, :], ms[:, a, :], 1 / 128, 1e-6, MUL, ADD, t)
        t = self.tt("pool", ms[:, 2 + a, :], ms[:, a, :], self.mhalf[:, 0:4], ALU.pow, t)
        if k != 1.0:
            t = self.ts("pool", ms[:, 2 + a, :], ms[:, 2 + a, :], k, None, MUL, None, t)
        return self.tt("dve", h4(o[:, a, :]), h4(o[:, a, :]), bc(ms[:, 2 + a, :], 128), MUL, t)

    def rotary(self):
        Q, M = self.Q, self.M
        self.CS = M.get([128, 2, 2, 8])
        z = M.get([128, 2, 4, 8])
        p = M.get([128, 2])
        t = self.cp("dve", p[:, :], self.POS[:, :], self.tpos, p.dep)
        out = []
        c1 = 6.28125
        c2 = float(np.float32(np.round((2 * math.pi - c1) * 2 ** 20) / 2 ** 20))
        c3 = 2 * math.pi - c1 - c2
        big = 1.5 * 2 ** 23
        for a in range(2):
            x, k, r, y = (z[:, a, i, :] for i in range(4))
            t1 = self.ts("dve", x, self.freq, p[:, a:a + 1], None, MUL, None, t, self.tc, z.dep)
            t2 = self.ts("dve", k, x, 1 / (2 * math.pi), None, MUL, None, t1)
            t2 = self.ts("dve", k, k, big, None, ADD, None, t2)
            t2 = self.ts("dve", k, k, -big, None, ADD, None, t2)
            t2 = self.stt(r, k, -c1, x, MUL, ADD, t2)
            t2 = self.stt(r, k, -c2, r, MUL, ADD, t2)
            t2 = self.stt(r, k, -c3, r, MUL, ADD, t2)
            t2 = self.ts("dve", r, r, 3.1415925, -3.1415925, MIN, MAX, t2)
            out.append(self.act(self.CS[:, 1, a, :], r, ACT.Sin, t2, self.CS.dep))
            t3 = self.ts("dve", y, r, -1.0, None, MUL, None, t2)
            t3 = self.tt("dve", y, y, r, MAX, t3)
            t3 = self.ts("dve", y, y, -1.0, math.pi / 2, MUL, ADD, t3)
            out.append(self.act(self.CS[:, 0, a, :], y, ACT.Sin, t3, self.CS.dep))
        M.put(z, out)
        M.put(p, out)
        self.tcs = out

    def soft(self, P, w, scale, mx, out, *after):
        P3 = rr(P, "p (a k) -> p a k", a=2)
        t = self.red(mx[:, 0:2], P3, MAX, after)
        t = self.ts("dve", mx[:, 2:4], mx[:, 0:2], -scale, None, MUL, None, t)
        o = [self.act(out[:, a, :], P3[:, a, :], ACT.Exp, t, bias=mx[:, 2 + a:3 + a], scale=scale, accum_out=mx[:, 4 + a:5 + a]) for a in range(2)]
        return o, self.rcp(mx[:, 6:8], mx[:, 4:6], o)

    def diff(self, l, dqk, tqk, dv, tdv, mh, ml, tmx):
        Q, M = self.Q, self.M
        lam0 = 0.8 - 0.6 * math.exp(-0.3 * l)
        LM = M.get([128, 256])
        lm = M.get([128, 8])
        t = Q.dma("pool", "lam", LM[:, :], self.dram["lam"][l:l + 1, :].to_broadcast([128, 256]), LM.dep)
        L4 = rr(LM[:, :], "p (a b d) -> p a b d", a=2, b=2)
        t = self.tt("dve", L4[:, :, 0, :], L4[:, :, 0, :], L4[:, :, 1, :], MUL, t)
        t = self.red(lm[:, 0:2], L4[:, :, 0, :], ADD, t, lm.dep)
        t = self.act(lm[:, 2:4], lm[:, 0:2], ACT.Exp, t)
        t = self.tt("dve", lm[:, 4:5], lm[:, 3:4], lm[:, 2:3], SUB, t)
        tl = self.ts("dve", lm[:, 5:6], lm[:, 4:5], -lam0, None, ADD, None, t)
        tm = M.get([128, 2, 4, 16, 8])
        qT = M.get([128, 8, T])
        tr_ = []
        for a in range(2):
            v = rr(dqk[:, a, :], "p (g d) -> p g d", g=16)
            x1, x2 = v[:, :, 0:8], v[:, :, 8:16]
            c, s = (self.CS[:, i, a, :].unsqueeze(1).to_broadcast([128, 16, 8]) for i in range(2))
            u = [self.tt("dve", tm[:, a, i, :, :], x, y, MUL, tqk, self.tcs, tm.dep) for i, (x, y) in enumerate(((x1, c), (x2, s), (x2, c), (x1, s)))]
            tr_.append(self.tt("dve", x1, tm[:, a, 0, :, :], tm[:, a, 1, :, :], SUB, u))
            tr_.append(self.tt("dve", x2, tm[:, a, 2, :, :], tm[:, a, 3, :, :], ADD, u))
        tT = []
        for i in range(4):
            b, P, f = self.bank()
            for j in range(2):
                for a in range(2):
                    k = 2 * i + j
                    t = self.tr(P[:, j * 256 + a * 128:j * 256 + a * 128 + 128], dqk[:, a, k * 128:k * 128 + 128], tr_, f, inc=j + a == 2)
            tT.append(self.cp("act", rr(qT[:, 2 * i:2 * i + 2, :], "p k t -> p (k t)"), P[:, :], t, qT.dep))
            self.done(b, tT[-1])
        M.put(tm, Q.now("dve"))
        pp = M.get([128, 2, 2, 2, T])
        mx = M.get([128, 8, 8])
        aT = M.get([128, 4, 2, T])
        pfr = [pp.dep] * 2
        taT = {}
        back = []
        for h in range(4):
            s = h % 2
            tt_ = []
            for c in range(2):
                r = slice(64 * c, 64 * c + 64)
                b, P, f = self.bank()
                for a in range(2):
                    t = self.mm(P[:, a * 256:a * 256 + 256], qT[r, h, a * 128:a * 128 + 128], qT[r, 4 + h, :], True, True, tT, f, inc=a == 1)
                m = mx[:, 2 * h + c, :]
                o, tr1 = self.soft(P[:, :], 256, 0.125, m, pp[:, s, c, :, :], t, pfr[s], mx.dep)
                self.done(b, o)
                tt_.append(tr1)
            m0, m1 = mx[:, 2 * h, :], mx[:, 2 * h + 1, :]
            t = self.ts("dve", m1[:, 0:2], m1[:, 6:8], lm[:, 5:6], None, MUL, None, tt_, tl)
            o = []
            for a in range(2):
                t1 = self.ts("dve", pp[:, s, 0, a, :], pp[:, s, 0, a, :], m0[:, 6 + a:7 + a], None, MUL, None, tt_)
                o.append(self.stt(pp[:, s, 0, a, :], pp[:, s, 1, a, :], m1[:, a:a + 1], pp[:, s, 0, a, :], MUL, ADD, t, t1))

            def turn(h=h, s=s, o=o):
                b, P, f = self.bank()
                for kk in range(2):
                    for a in range(2):
                        t = self.tr(P[:, kk * 256 + a * 128:kk * 256 + a * 128 + 128], pp[:, s, 0, a, kk * 128:kk * 128 + 128], o, f, inc=kk + a == 2)
                pfr[s] = t
                taT[h] = self.cp("act", rr(aT[:, h, :, :], "p k t -> p (k t)"), P[:, :], t, aT.dep)
                self.done(b, taT[h])

            back.append(turn)
            if h:
                back.pop(0)()
        back.pop(0)()
        M.put(pp, Q.now())
        o_ = M.get([128, 2, 512])
        sq = M.get([128, 2, 512])
        ms = M.get([128, 4, 4])
        tf = []
        for a in range(2):
            b, P, f = self.bank()
            for h in range(4):
                c = slice(h * 128, h * 128 + 128)
                for kk in range(2):
                    t = self.mm(P[:, c], aT[:, h, kk, a * 128:a * 128 + 128], dv[:, kk, c], kk == 0, kk == 1, taT[h], tdv, f, inc=h == 3 and kk == 1)
            t = self.cp("act", o_[:, a, :], P[:, :], t, o_.dep)
            self.done(b, t)
            tf.append(self.head_rms(o_, sq, ms, a, t, 1.0 - lam0))
        self.to_mix(o_, tf, 0, lambda i: self.COL[:, ROW["dnorm"] + l:ROW["dnorm"] + l + 1], mh, ml, tmx, 4)
        for x in (LM, lm, qT, mx, aT, o_, sq, ms, dqk, dv):
            M.put(x, Q.now())

    def memory(self, xq, tx, mk, tk, mv, tv, mh, ml, tmx):
        Q, M = self.Q, self.M
        pp = M.get([128, 2, 2, T])
        mx = M.get([128, 4, 8])
        pT = M.get([128, 2, 2, T])
        pfr, tfr = [pp.dep] * 2, [pT.dep] * 2
        back = []
        for h in range(4):
            s = h % 2
            b, P, f = self.bank()
            for a in range(2):
                t = self.mm(P[:, a * 256:a * 256 + 256], xq[:, h, a * 128:a * 128 + 128], mk[:, h, :], True, True, tx, tk, f, inc=a == 1)
            m = mx[:, h, :]
            o, t = self.soft(P[:, :], 256, 128 ** -0.5, m, pp[:, s, :, :], t, pfr[s], mx.dep)
            self.done(b, o)
            o = [self.ts("dve", pp[:, s, a, :], pp[:, s, a, :], m[:, 6 + a:7 + a], None, MUL, None, t) for a in range(2)]

            def turn(h=h, s=s, o=o):
                b, P, f = self.bank()
                for kk in range(2):
                    for a in range(2):
                        t = self.tr(P[:, kk * 256 + a * 128:kk * 256 + a * 128 + 128], pp[:, s, a, kk * 128:kk * 128 + 128], o, f, inc=kk + a == 2)
                pfr[s] = t
                t = self.cp("act", rr(pT[:, s, :, :], "p k t -> p (k t)"), P[:, :], t, tfr[s])
                self.done(b, t)
                b, P, f = self.bank()
                for kk in range(2):
                    u = self.mm(P[:, 0:T], mv[:, kk, h * 128:h * 128 + 128], pT[:, s, kk, :], kk == 0, kk == 1, t, tv, f, inc=kk == 1)
                tfr[s] = u
                t1 = self.cp("act", mh[:, 8 + h, :], P[:, 0:T], u, mh.dep)
                t2 = self.tt("dve", ml[:, 8 + h, :], P[:, 0:T], mh[:, 8 + h, :], SUB, t1, ml.dep)
                self.done(b, t1, t2)
                tmx[8 + h] = [t1, t2]

            back.append(turn)
            if h:
                back.pop(0)()
        back.pop(0)()
        for x in (pp, mx, pT, xq, mk, mv):
            M.put(x, Q.now())

    def first_input(self, p, l, j):
        Q, M = self.Q, self.M
        xf = M.get([128, 8, T])
        tmp = M.get([128, 2, T])
        self.XH = M.get([128, 8, T], F32R, high=True)
        self.XL = M.get([128, 8, T], F32R, high=True)
        tx = Q.dma("act", "xf", xf[:, :, :], self.dram["xT"], xf.dep)
        self.xt_ = [Q.dma("act", "x", self.X[:, a, :], self.dram["x"][a]) for a in range(2)][-1:]
        tm = [v for k, v in self.mod_t[p].items() if k != "free"]
        A, B = self.mod[p][:, 1, :], self.mod[p][:, 0, :]
        tf = [tmp.dep] * 2
        out = []
        for f in range(8):
            s = f % 2
            a, b = A[:, f:f + 1], B[:, f:f + 1]
            t1 = self.act(self.XH[:, f, :], xf[:, f, :], ACT.Identity, tx, tm, self.XH.dep, scale=a, bias=b)
            t2 = self.ts("dve", tmp[:, s, :], xf[:, f, :], a, b, MUL, ADD, tx, tm, tf[s])
            t3 = self.tt("dve", self.XL[:, f, :], tmp[:, s, :], self.XH[:, f, :], SUB, t2, t1, self.XL.dep)
            tf[s] = t3
            out += [t1, t3]
        self.mod_t[p] = {"free": out}
        M.put(xf, out)
        M.put(tmp, out)
        return out

    def renorm(self, cols):
        Q, M = self.Q, self.M
        R = M.get([128, 2, D])
        GB = M.get([128, 2, D])
        st = M.get([128, 2, 16])
        v = VEC["lin_g"]
        tg = [Q.dma("pool", "lg", GB[:, i, :], self.dram["vec"][v + i:v + i + 1, :].to_broadcast([128, D]), GB.dep) for i in range(2)]
        tab = self.fold(cols)
        tn, tx = [], []
        for a in range(2):
            ts_ = self.stats(self.X, st, a, self.xt_, st.dep)
            t = self.ts("dve", R[:, a, :], self.X[:, a, :], st[:, a, 0:1], st[:, a, 3:4], SUB, MUL, ts_, R.dep)
            t1 = self.tt("pool", self.X[:, a, :], R[:, a, :], GB[:, 0, :], MUL, t, tg)
            tx.append(self.tt("pool", self.X[:, a, :], self.X[:, a, :], GB[:, 1, :], ADD, t1))
            tn.append(t)
        self.xt_ = tx
        out = self.to_cols(R, tn, tab)
        for b in (R, GB, st):
            M.put(b, Q.now())
        return out

    def rowsof(self, n, i):
        return [VEC[n + "_g"] + i, VEC[n + "_b"] + i]

    def colsof(self, n, i):
        g, b = ROW[n + "_g"] + 8 * i, ROW[n + "_b"] + 8 * i
        return self.COL[:, g:g + 8], self.COL[:, b:b + 8]

    def run(self, until=None):
        Q = self.Q
        self.gate_free = self.xfree = self.abfree = None
        self.start()
        self.flush()
        xt = self.first_input(0, 0, 0)
        for l in range(2):
            banks = self.ffn1(l, 0, xt)
            xt = self.post(banks, True, self.rowsof("ln", 3 * l), (*self.colsof("ln", 3 * l), ((3 * l + 1) % 2, l, 1)))
            self.tap(f"x{3 * l}", self.X[:, :, :], self.xt_)
            banks = self.mixer1(l, xt)
            xt = self.post(banks, True, self.rowsof("ln", 3 * l + 1), (*self.colsof("ln", 3 * l + 1), ((3 * l + 2) % 2, l, 2)))
            self.tap(f"x{3 * l + 1}", self.X[:, :, :], self.xt_)
            banks = self.ffn1(l, 1, xt)
            cols = (*self.colsof("ln", 3 * l + 2), (1, 1, 0)) if l == 0 else None
            xt = self.post(banks, True, self.rowsof("ln", 3 * l + 2), cols)
            self.tap(f"x{3 * l + 2}", self.X[:, :, :], self.xt_)
        self.rotary()
        xt = self.renorm((*self.colsof("lin", 0), None))
        for l in range(2):
            banks = self.mixer2(l, xt)
            xt = self.post(banks, False, self.rowsof("ln1", l), (*self.colsof("ln1", l), None))
            self.tap(f"y{2 * l}", self.X[:, :, :], self.xt_)
            banks = self.ffn2(l, xt)
            xt = self.post(banks, False, self.rowsof("ln2", l), (*self.colsof("ln2", l), None) if l == 0 else None, last=l == 1)
            self.tap(f"y{2 * l + 1}", self.X[:, :, :], self.xt_)
        for a in range(2):
            t = Q.dma("sp", "out", self.dram["out"][a], self.X[:, a, :], self.xt_)
        Q.wait("sp", t)


def build(nc, dram):
    ctx = ExitStack()
    with ctx:
        p = Prog(nc, ctx, dram)
        p.run()
        for n in ("tap",):
            if n in p.Q.cnt:
                p.Q.wait("sp", (n, p.Q.cnt[n]))
        block = ctx.enter_context(nc.Block())

        @block.sync
        def _(e):
            p.Q.play("sp", e)

        @block.tensor
        def _(e):
            p.Q.play("pe", e)

        @block.vector
        def _(e):
            p.Q.play("dve", e)

        @block.scalar
        def _(e):
            p.Q.play("act", e)

        @block.gpsimd
        def _(e):
            p.Q.play("pool", e)


def kernel(**inputs):
    import numpy as _np
    import concourse.bacc as _bacc
    from concourse import mybir as _mybir
    from concourse.bass_utils import run_bass_kernel_spmd as _run

    a = {k: _np.asarray(v) for k, v in inputs.items()}
    arrays = {"in_" + k: _np.ascontiguousarray(v) for k, v in layout(a).items()}
    nc = _bacc.Bacc("TRN2", target_bir_lowering=False, num_devices=1)
    dram = {k[3:]: nc.dram_tensor(k, v.shape, _mybir.dt.from_np(v.dtype), kind="ExternalInput").ap() for k, v in arrays.items()}
    out = nc.dram_tensor("out_0", (2, 128, D), F32, kind="ExternalOutput").ap()
    dram["out"] = out
    build(nc, dram)
    r = _run(nc, [arrays], core_ids=[0])
    return r.results[0]["out_0"].reshape(1, T, D)
```

```python
import math
from contextlib import ExitStack

import numpy as np

import concourse.bass as bass
from concourse import mybir

F32 = mybir.dt.float32
F32R = mybir.dt.float32r
I32 = mybir.dt.int32
ALU = mybir.AluOpType
ACT = mybir.ActivationFunctionType
AX = mybir.AxisListType.X
ADD, SUB, MUL, MAX, MIN = ALU.add, ALU.subtract, ALU.mult, ALU.max, ALU.min

D = 1024
T = 256
FF = 2816
NF = FF // 128
ALPHA = 4 ** 0.25
CH = 2048
NW = 4
NH = 3
NEG = -1e30


def row_index():
    at, n = {}, 0
    for name, rows in (
        ("ada_b", 144), ("ln_g", 48), ("ln_b", 48), ("lin_g", 8), ("lin_b", 8), ("ln1_g", 16), ("ln1_b", 16),
        ("ln2_g", 16), ("ln2_b", 16), ("gconv", 72), ("mconv", 48), ("cw", 264), ("cb", 88), ("lbf", 8), ("lbb", 8),
        ("mnorm", 6), ("gnorm", 2), ("dnorm", 2), ("hnorm", 2),
    ):
        at[name] = n
        n += rows
    return at, n


ROW, NROW = row_index()


def mixer1_cols():
    r = lambda a, b: list(range(a, b))
    fm = [r(128 * i, 128 * i + 128) for i in range(9)]
    fm += [r(2316 + 128 * i, 2316 + 128 * i + 128) for i in range(6)]
    fm += [r(1548 + 128 * i, 1548 + 128 * i + 128) for i in range(4)]
    out = []
    tm = [r(1152, 1164) + r(3468, 3480)]
    tm += [r(1164, 1420), r(1420, 1548) + r(3480, 3608), r(3608, 3864), r(2060, 2316), r(3084, 3340), r(3340, 3468)]
    out += [("tm", tm[0])]
    for i in range(0, 18, 2):
        out.append(("fm", fm[i] + fm[i + 1]))
    out.append(("fm", fm[18]))
    out += [("tm", c) for c in tm[1:]]
    return out


def mixer2_cols():
    r = lambda a, b: list(range(a, b))
    order = [1536, 2048, 2560, 0, 512, 1024, 3072, 3584, 4096]
    return [r(o + h, o + h + 256) for o in order for h in (0, 256)]


ADA = {(0, 0): [(0, 1), (0, 2)], (0, 1): [], (0, 2): [(1, 0), (1, 1)], (1, 0): [(1, 2)], (1, 1): [], (1, 2): []}


MIX1 = [0, 9, 10, 14, 1, 2, 3, 4, 5, 8, 6, 7, 15, 16, 11, 12, 13]
EARLY = [1, 2, 2, 1, 1, 1, 0, 0]
WOUT1 = [3, 2, 1, 0]
WOUT2 = [0, 1, 4, 5, 2, 3]


def schedule():
    s = []
    ada = lambda l, j, v: [("ada", l, j, v, q) for q in range(4)]

    def ffn(l, i):
        a = []
        for m in range(NF // 2):
            a += [("w13", l, i, 0, m), ("w13", l, i, 1, m)]
        return a

    wkv = [("wkv", l, n) for l in range(2) for n in range(4)]
    first = ada(0, 0, 0) + ada(0, 0, 1)
    n = 0
    for i, k in enumerate(EARLY):
        s += [wkv[i]] + first[n:n + k]
        n += k
    for l in range(2):
        for j in range(3):
            extra = ada(l, j, 2)
            for nl, nj in ADA[l, j]:
                extra += ada(nl, nj, 0) + ada(nl, nj, 1)
            if j == 1:
                body = [("win", l, n) for n in MIX1]
                s += weave(body, extra) + [("wout", l, k) for k in WOUT1]
            else:
                w2 = [("w2", l, j // 2, k) for k in range(NF // 2)]
                n = len(extra) * 2 // 3
                s += weave(ffn(l, j // 2), extra[:n]) + weave(w2[:8], extra[n:]) + w2[8:]
    for l in range(2):
        s += [("win2", l, n) for n in range(18)]
        s += [("wout2", l, k) for k in WOUT2]
        for m in range(NF // 2):
            s += [("wup", l, 0, m), ("wup", l, 1, m)]
        s += [("wdn", l, k) for k in range(NF // 2)]
    return s


def weave(body, extra):
    out, n = [], 0
    for i, b in enumerate(body):
        out.append(b)
        while n < len(extra) * (i + 1) // len(body):
            out.append(extra[n])
            n += 1
    return out


SCHED = schedule()


def width(c):
    if c[0] == "win":
        return len(mixer1_cols()[c[2]][1])
    return 256


def pack(inp):
    S = np.zeros((len(SCHED), 128, CH), np.float32)
    km = lambda w: w.reshape(-1, 128, w.shape[1]).transpose(1, 0, 2).reshape(128, -1)
    cols1, cols2 = mixer1_cols(), mixer2_cols()
    for n, c in enumerate(SCHED):
        k = c[0]
        if k == "ada":
            _, l, j, v, q = c
            o = (j * 3 + v) * D
            w = km(inp["ada_w"][l][q * 256:q * 256 + 256, o:o + D])
        elif k == "w13":
            _, l, i, h, m = c
            w = km(inp["ffn_w13"][l, i][:, h * FF + m * 256:h * FF + m * 256 + 256])
        elif k == "w2":
            w = km(inp["ffn_w2"][c[1], c[2]][c[3] * 256:c[3] * 256 + 256])
        elif k == "win":
            w = km(inp["w_in"][c[1]][:, cols1[c[2]][1]])
        elif k == "wout":
            w = km(inp["w_out"][c[1]][c[2] * 256:c[2] * 256 + 256])
        elif k == "win2":
            w = km(inp["w_in_2"][c[1]][:, cols2[c[2]]])
        elif k == "wkv":
            w = km(inp["w_mem_kv_2"][c[1]][:, c[2] * 256:c[2] * 256 + 256])
        elif k == "wout2":
            w = km(inp["w_out_2"][c[1]][c[2] * 256:c[2] * 256 + 256])
        elif k == "wup":
            w = km(inp["w_up_2"][c[1]][:, c[2] * FF + c[3] * 256:c[2] * FF + c[3] * 256 + 256])
        else:
            w = km(inp["w_down_2"][c[1]][c[2] * 256:c[2] * 256 + 256])
        S[n, :, :w.shape[1]] = w
    return S


def constants():
    i = np.arange(128)
    s, t = i[:, None], i[None, :]
    same = (s // 64) == (t // 64)
    parts = [
        np.eye(128),
        np.where(same & (s <= t), 0.0, NEG),
        np.where(t <= s, 0.0, NEG),
    ]
    for l in range(6):
        z = 1 << l
        parts.append(((s // (2 * z) == t // (2 * z)) & ((s // z) % 2 == 0) & ((t // z) % 2 == 1)).astype(float))
    for l in range(6):
        z = 1 << l
        parts.append(((s // (2 * z) == t // (2 * z)) & ((s // z) != (t // z))).astype(float))
    parts.append(same.astype(float))
    parts.append(np.tile((np.arange(256) % 64 != 0).astype(float), (128, 1)))
    parts.append(np.tile(500000.0 ** (-np.arange(0, 16, 2) / 16.0), (128, 1)))
    sg = np.ones((128, 1))
    sg[32:64] = -1.0
    parts.append(sg)
    parts.append(np.full((128, 7), -0.5))
    return np.concatenate(parts, 1).astype(np.float32)


CW = dict(ident=(0, 128), neg=(128, 128), causal=(256, 128), lvl=(384, 768), both=(1152, 768), ones64=(1920, 128),
          rmask=(2048, 256), freq=(2304, 8), sgn=(2312, 1), mhalf=(2313, 7))
NCONST = 2320


def layout(inp):
    rows = []
    f = lambda a: rows.append(np.asarray(a, np.float32).reshape(-1, 128))
    for n in ("ada_b", "ln_g", "ln_b", "ln_in_g_2", "ln_in_b_2", "ln1_g_2", "ln1_b_2", "ln2_g_2", "ln2_b_2", "gdn_conv",
              "mlstm_conv", "conv_w_2", "conv_b_2", "hg_lb_fwd_2", "hg_lb_bwd_2", "mlstm_norm"):
        f(inp[n])
    f(np.concatenate([inp["gdn_norm"], inp["gdn_norm"]], 1))
    f(inp["da_norm_g_2"])
    f(inp["hg_norm_g_2"])
    cols = np.concatenate(rows, 0).T
    heads = np.zeros((2, 128, 2), np.float32)
    for l in range(2):
        heads[l, 0:6, 0] = inp["gdn_dt_bias"][l]
        heads[l, 32:38, 0] = inp["mlstm_f_bias"][l]
        heads[l, 96:102, 0] = inp["mlstm_i_bias"][l]
        heads[l, 0:6, 1] = inp["gdn_a_log"][l]
    fm = lambda a: a.reshape(T, 8, 128).transpose(2, 1, 0)
    vec = np.concatenate([a.reshape(-1, D) for a in (
        inp["ada_b"].reshape(2, 3, 3, D)[:, :, 2], inp["ln_g"], inp["ln_b"], inp["ln_in_g_2"][None], inp["ln_in_b_2"][None],
        inp["ln1_g_2"], inp["ln1_b_2"], inp["ln2_g_2"], inp["ln2_b_2"])], 0)
    lam = inp["da_lambda_2"].reshape(2, 256)
    return {
        "stream": pack(inp),
        "cols": cols,
        "cst": constants(),
        "heads": heads.transpose(1, 0, 2).reshape(128, 4),
        "x": inp["x"][0].reshape(2, 128, D),
        "xT": fm(inp["x"][0]),
        "memT": fm(inp["mem_2"][0]),
        "c": inp["c"][0].reshape(8, 128).T,
        "pos": np.asarray(inp["positions_2"][0]).reshape(2, 128).T,
        "vec": vec,
        "lam": lam,
    }


VEC = dict(gate=0, ln_g=6, ln_b=12, lin_g=18, lin_b=19, ln1_g=20, ln1_b=22, ln2_g=24, ln2_b=26)


def flat(x, out):
    if x is None:
        return out
    if isinstance(x, tuple) and len(x) == 2 and isinstance(x[0], str):
        out.append(x)
        return out
    for y in x:
        flat(y, out)
    return out


class Queues:

    def __init__(self, nc, ctx):
        self.nc, self.ctx = nc, ctx
        self.sem, self.cnt, self.seen, self.q = {}, {}, {}, {}
        for e in ("pe", "dve", "act", "pool", "sp"):
            self.sem[e] = ctx.enter_context(nc.semaphore("s_" + e))
            self.cnt[e] = 0
            self.seen[e] = {}
            self.q[e] = []

    def op(self, e, fn, after, inc=True):
        w = []
        for s, v in flat(after, []):
            if self.seen[e].get(s, 0) < v:
                self.seen[e][s] = v
                w = [x for x in w if x[0] != s] + [(s, v)]
        if inc:
            self.cnt[e] += 1
        self.q[e].append((w, fn, (e, 1) if inc else None))
        return (e, self.cnt[e])

    def dma(self, e, sem, out, in_, *after):
        if sem not in self.sem:
            self.sem[sem] = self.ctx.enter_context(self.nc.semaphore("d_" + sem))
            self.cnt[sem] = 0
        self.op(e, lambda g: g.dma_start(out, in_), after, inc=False)
        w, fn, _ = self.q[e][-1]
        self.q[e][-1] = (w, fn, (sem, 16))
        self.cnt[sem] += 16
        return (sem, self.cnt[sem])

    def wait(self, e, *after):
        self.op(e, None, after, inc=False)

    def now(self, *engines):
        return [(e, self.cnt[e]) for e in (engines or ("pe", "dve", "act", "pool")) if self.cnt[e]]

    def play(self, e, eng):
        for w, fn, inc in self.q[e]:
            for s, v in w:
                eng.wait_ge(self.sem[s], v)
            if fn is not None:
                i = fn(eng)
                if inc:
                    i.then_inc(self.sem[inc[0]], inc[1])


class Buf:
    def __init__(self, t, lo, hi, dep):
        self.t, self.lo, self.hi, self.dep = t, lo, hi, dep

    def __getitem__(self, k):
        return self.t[k]


class Mem:

    def __init__(self, nc, lo, hi):
        self.nc, self.free_, self.n = nc, [(lo, hi, [])], 0

    def get(self, shape, dt=F32, high=False):
        size = (int(np.prod(shape[1:])) * 4 + 31) // 32 * 32
        fr = sorted(self.free_)
        runs, i = [], 0
        while i < len(fr):
            j = i
            while j + 1 < len(fr) and fr[j + 1][0] == fr[j][1]:
                j += 1
            if fr[j][1] - fr[i][0] >= size:
                runs.append((fr[i][0], fr[j][1]))
            i = j + 1
        assert runs, ("full", shape, [(a, b - a) for a, b, _ in fr])
        lo = runs[-1][1] - size if high else runs[0][0]
        hi = lo + size
        dep, rest = [], []
        for a, b, t in fr:
            if b <= lo or a >= hi:
                rest.append((a, b, t))
                continue
            dep += t
            if a < lo:
                rest.append((a, lo, t))
            if b > hi:
                rest.append((hi, b, t))
        self.free_ = rest
        self.n += 1
        return Buf(self.nc.alloc_sbuf_tensor_at(f"t{self.n}", list(shape), dt, offset=lo), lo, hi, dep)

    def fits(self, shape):
        size = (int(np.prod(shape[1:])) * 4 + 31) // 32 * 32
        end, run = None, 0
        for a, b, _ in sorted(self.free_):
            run = run + b - a if a == end else b - a
            end = b
            if run >= size:
                return True
        return False

    def put(self, buf, *after):
        self.free_.append((buf.lo, buf.hi, flat(after, [])))


def rr(ap, pattern, **k):
    return ap.rearrange(pattern, **k)


def bc(ap, n):
    return ap.unsqueeze(len(ap.shape)).to_broadcast(list(ap.shape) + [n])


class Prog:
    def __init__(self, nc, ctx, dram):
        self.Q = Queues(nc, ctx)
        self.nc, self.dram = nc, dram
        self.M = Mem(nc, (nc.sbuf_base + 31) // 32 * 32, nc.sbuf_usable_end // 32 * 32)
        self.ps = [ctx.enter_context(nc.psum_tensor(f"ps{i}", [128, 512], F32)) for i in range(8)]
        self.pfree = [[] for _ in range(8)]
        self.pn = 0

    def tt(self, e, out, a, b, o, *after):
        return self.Q.op(e, lambda g: g.tensor_tensor(out, a, b, o), after)

    def ts(self, e, out, a, s1, s2, o1, o2, *after):
        if s2 is None:
            return self.Q.op(e, lambda g: g.tensor_scalar(out, a, s1, None, o1), after)
        return self.Q.op(e, lambda g: g.tensor_scalar(out, a, s1, s2, o1, o2), after)

    def stt(self, out, a, s, b, o1, o2, *after):
        return self.Q.op("dve", lambda g: g.scalar_tensor_tensor(out=out, in0=a, scalar=s, in1=b, op0=o1, op1=o2), after)

    def act(self, out, a, f, *after, **k):
        return self.Q.op("act", lambda g: g.activation(out, a, f, **k), after)

    def cp(self, e, out, a, *after):
        if e == "act":
            return self.Q.op("act", lambda g: g.copy(out, a), after)
        return self.Q.op(e, lambda g: g.tensor_copy(out, a), after)

    def red(self, out, a, o, *after):
        return self.Q.op("dve", lambda g: g.tensor_reduce(out, a, AX, o), after)

    def rcp(self, out, a, *after):
        return self.Q.op("dve", lambda g: g.reciprocal(out, a), after)

    def mset(self, e, out, v, *after):
        return self.Q.op(e, lambda g: g.memset(out, v), after)

    def mm(self, out, l, r, start, stop, *after, inc=False, share=False):
        return self.Q.op("pe", lambda g: g.matmul(out, l, r, start=start, stop=stop, skip_group_check=share), after, inc=inc)

    def tr(self, out, a, *after, inc=False):
        n = a.shape[0]
        return self.Q.op("pe", lambda g: g.transpose(out, a, self.ident[0:n, 0:n]), after, inc=inc)

    def bank(self):
        i = next(i % 8 for i in range(self.pn, self.pn + 8) if self.pfree[i % 8] is not None)
        self.pn = i + 1
        t = self.pfree[i]
        self.pfree[i] = None
        return i, self.ps[i], t

    def done(self, i, *after):
        assert self.pfree[i] is None
        self.pfree[i] = flat(after, [])


    def start(self, first=0, last=None):
        Q, M = self.Q, self.M
        self.C = M.get([128, NCONST])
        self.COL = M.get([128, NROW])
        self.HD = M.get([128, 4])
        self.CV = M.get([128, 8])
        self.SC = M.get([128, 8])
        self.POS = M.get([128, 2], I32)
        self.X = M.get([128, 2, D])
        self.G = [M.get([128, D]) for _ in range(1)]
        self.ones = M.get([128, 128])
        self.AB = M.get([128, 16])
        self.acc = M.get([128, D])
        self.accfree = self.acct = None
        self.mod = [M.get([128, 3, 8]) for _ in range(2)]
        self.W = [M.get([128, CH]) for _ in range(NW)]
        self.H = [M.get([128, CH], F32R) for _ in range(NH)]
        self.L = [M.get([128, CH], F32R) for _ in range(NH)]
        const = lambda k: self.C[:, CW[k][0]:CW[k][0] + CW[k][1]]
        self.ident, self.neg, self.causal, self.lvl, self.both = (const(k) for k in ("ident", "neg", "causal", "lvl", "both"))
        self.ones64, self.rmask, self.freq, self.sgn, self.mhalf = (const(k) for k in ("ones64", "rmask", "freq", "sgn", "mhalf"))
        self.tcv = Q.dma("act", "cv", self.CV[:, :], self.dram["c"])
        self.memf = M.get([128, 8, T])
        self.xf = M.get([128, 8, T])
        self.tmf = Q.dma("sp", "mem", self.memf[:, :, :], self.dram["memT"])
        self.tc2 = Q.dma("act", "c2", self.COL[:, :], self.dram["cols"])
        self.tc = None
        self.th = Q.dma("pool", "h", self.HD[:, :], self.dram["heads"])
        self.tpos = Q.dma("pool", "pos", self.POS[:, :], self.dram["pos"])
        self.tones = self.mset("pool", self.ones[:, :], 1.0)
        self.S = SCHED[first:last]
        self.first = first
        self.wfree = [[] for _ in range(NW)]
        self.hfree = [[] for _ in range(NH)]
        self.landed, self.ready, self.where = {}, {}, {}
        self.nd = self.np_ = self.nt = self.nh = self.rel = 0
        self.tasks = []
        self.lows = []
        self.pending = []
        self.gate_t = [[], []]
        self.mod_t = [{}, {}]
        self.tsc = self.act(self.SC[:, :], self.CV[:, :], ACT.Silu, self.tcv)
        for _ in range(NW):
            self.load()

    def load(self):
        n = self.nd
        if n >= len(self.S):
            return
        self.nd += 1
        w = n % NW
        sz = 8 * width(self.S[n])
        self.landed[n] = self.Q.dma("sp", f"w{w}", self.W[w][:, 0:sz], self.dram["stream"][self.first + n][:, 0:sz], self.wfree[w])

    def prepare(self):
        n = self.np_
        if n >= len(self.S):
            return
        self.np_ += 1
        self.low()
        w = n % NW
        c = self.S[n]
        if c[0] == "ada":
            self.ada_chunk(n, c, self.W[w])
        else:
            h = self.nh % NH
            self.nh += 1
            sz = 8 * width(c)
            t1 = self.cp("act", self.H[h][:, 0:sz], self.W[w][:, 0:sz], self.landed[n], self.hfree[h])
            self.where[n] = h

            def low(e):
                t2 = self.tt(e, self.L[h][:, 0:sz], self.W[w][:, 0:sz], self.H[h][:, 0:sz], SUB, t1)
                self.wfree[w] = [t1, t2]
                self.ready[n] = [t1, t2]
                self.load()

            self.lows.append(low)
            return
        self.load()

    def low(self, e="dve"):
        while self.lows:
            self.lows.pop(0)(e)

    def take(self, what):
        self.settle(2)
        while self.S[self.nt][0] == "ada":
            while self.np_ <= self.nt:
                self.prepare()
            self.nt += 1
        n = self.nt
        assert self.S[n] == what, (self.S[n], what)
        self.nt += 1
        self.low()
        self.ahead(n, NH - 1)
        if n not in self.ready:
            self.low()
        return self.where[n], self.H[self.where[n]], self.L[self.where[n]], self.ready[n]

    def ahead(self, n, k):
        want = n
        while k and want + 1 < len(self.S):
            want += 1
            if self.S[want][0] != "ada":
                k -= 1
        while self.np_ <= min(want, len(self.S) - 1):
            if self.S[self.np_][0] != "ada" and self.nh - self.rel >= NH:
                assert self.np_ > n
                break
            self.prepare()

    def release(self, h, t):
        self.hfree[h] = [t]
        self.rel += 1

    def beside(self, n=1):
        idle = 0
        while n and self.tasks and idle < len(self.tasks):
            g = self.tasks.pop(0)
            had = list(self.M.free_)
            r = next(g, "end")
            if r == "end":
                idle = 0
                continue
            self.tasks.append(g)
            if r == "wait":
                idle = idle + 1 if had == self.M.free_ else 0
            else:
                idle = 0
                n -= 1
        return idle == 0

    def need(self, made):
        def of(k):
            while k not in made:
                assert self.beside()
            return made[k]
        return of

    def once(self, first, fin):
        def run(banks):
            first()
            return fin(banks)
        return run

    def finish_tasks(self):
        while self.tasks:
            assert self.beside() or not self.tasks

    def room(self, shape, dt=F32, **k):
        while not self.M.fits(shape):
            yield "wait"
        return self.M.get(shape, dt, **k)

    def settle(self, age=0):
        pend, self.pending = self.pending, []
        for n, f in pend:
            if n + 1 >= age:
                f()
            else:
                self.pending.append((n + 1, f))

    def flush(self):
        while self.nt < len(self.S) and self.S[self.nt][0] == "ada":
            while self.np_ <= self.nt:
                self.prepare()
            self.nt += 1
        self.settle()

    def ada_chunk(self, n, c, W):
        _, l, j, v, q = c
        A = self.acc
        Wv = rr(W[:, :], "p (k n) -> p k n", k=2)
        t = None
        for i in range(2):
            k = 2 * q + i
            if k == 0:
                self.settle()
                t = self.ts("dve", A[:, :], Wv[:, i, :], self.SC[:, 0:1], None, MUL, None, self.landed[n], self.tsc, self.accfree)
            else:
                t = self.stt(A[:, :], Wv[:, i, :], self.SC[:, k:k + 1], A[:, :], MUL, ADD, t or self.acct, self.landed[n])
        self.acct = t
        self.wfree[n % NW] = [t]
        if q < 3:
            return
        p = (l * 3 + j) % 2

        def columns():
            b, P, f = self.bank()
            for i in range(8):
                u = self.mm(P[:, i:i + 1], A[:, i * 128:i * 128 + 128], self.ones[:, 0:1], True, True, t, f, self.tones, inc=i == 7)
            r = ROW["ada_b"] + l * 72 + (j * 3 + v) * 8
            o = self.mod[p][:, v, :]
            x = self.tt("dve", o, P[:, 0:8], self.COL[:, r:r + 8], ADD, u, self.tc2, self.mod_t[p].get("free"))
            if v == 1:
                x = self.ts("dve", o, o, 1.0, None, ADD, None, x)
            self.mod_t[p][(l, j, v)] = x
            self.done(b, x)
            self.accfree = [u]

        def spread():
            xs = []
            for i in range(2):
                b, P, f = self.bank()
                s = slice(i * 512, i * 512 + 512)
                u = self.mm(P[:, :], self.ones[:, :], A[:, s], True, True, t, f, self.tones, inc=True)
                x = self.tt("dve", self.G[0][:, s], P[:, :], self.G[0][:, s], ADD, u, self.tgb)
                self.done(b, x)
                xs.append(self.ts("dve", self.G[0][:, s], self.G[0][:, s], 1.0, 0.5 if j != 1 else 1.0, ADD, MUL, x))
            self.gate_t[0] = xs
            self.accfree = [u]

        self.pending.append((0, columns if v < 2 else spread))

    def gate_bias(self, l, j):
        self.tgb = self.Q.dma("pool", "gb", self.G[0][:, :], self.dram["vec"][VEC["gate"] + l * 3 + j:VEC["gate"] + l * 3 + j + 1, :].to_broadcast([128, D]),
                              self.gate_free)

    def up(self, h, H, L, rd, xh, xl, xt, n, cb):
        Hv = rr(H[:, 0:8 * n], "p (k n) -> p k n", k=8)
        Lv = rr(L[:, 0:8 * n], "p (k n) -> p k n", k=8)
        for m in range(n // 128):
            b, P, f = self.bank()
            w = [rd, f]
            for k in range(8):
                w = [w, xt[k]]
                o = slice(m * 128, m * 128 + 128)
                self.mm(P[:, 0:T], Hv[:, k, o], xh[:, k, :], k == 0, False, w)
                self.mm(P[:, 0:T], Hv[:, k, o], xl[:, k, :], False, False)
                t = self.mm(P[:, 0:T], Lv[:, k, o], xh[:, k, :], False, k == 7, inc=k == 7)
                w = []
            self.done(b, cb(m, P, t))
            self.low()
            if m < n // 128 - 1:
                self.beside()
        self.release(h, t)
        self.beside()
        return t

    def tokmajor(self, h, H, L, rd, xh, xl, xt, n, cb):
        Hv = rr(H[:, 0:8 * n], "p (k n) -> p k n", k=8)
        Lv = rr(L[:, 0:8 * n], "p (k n) -> p k n", k=8)
        for a in range(2):
            b, P, f = self.bank()
            w = [rd, f]
            for k in range(8):
                w = [w, xt[k]]
                o = slice(a * 128, a * 128 + 128)
                self.mm(P[:, 0:n], xh[:, k, o], Hv[:, k, :], k == 0, False, w)
                self.mm(P[:, 0:n], xh[:, k, o], Lv[:, k, :], False, False)
                t = self.mm(P[:, 0:n], xl[:, k, o], Hv[:, k, :], False, k == 7, inc=k == 7)
                w = []
            self.done(b, cb(a, P, t))
            self.low()
            if a == 0:
                self.beside()
        self.release(h, t)
        self.beside()
        return t

    def down(self, keys, ks, hh, hl, ht, fin, tail=NH):
        B = [list(self.bank()) for _ in range(4)]
        last = max(0, len(keys) - tail)
        groups = [[c] for c in range(last)] + [list(range(last, len(keys)))]
        k0, k1 = ks[0], ks[-1]
        for group in groups:
            got = [self.take(keys[c]) for c in group]
            for a in range(2):
                for i, (c, (h, H, L, rd)) in enumerate(zip(group, got)):
                    Hv = rr(H[:, :], "p (k n) -> p k n", k=2)
                    Lv = rr(L[:, :], "p (k n) -> p k n", k=2)
                    for n, kk in ((0, 0), (0, 1), (1, 0), (1, 1)):
                        k = ks[2 * c + kk]
                        xh, xl = hh[:, k, a * 128:a * 128 + 128], hl[:, k, a * 128:a * 128 + 128]
                        P = B[2 * a + n][1]
                        s = slice(n * 512, n * 512 + 512)
                        self.mm(P[:, :], xh, Hv[:, kk, s], k == k0, False, rd, ht(k), B[2 * a + n][2] if k == k0 else None)
                        self.mm(P[:, :], xh, Lv[:, kk, s], False, False)
                        t = self.mm(P[:, :], xl, Hv[:, kk, s], False, k == k1, inc=(k == k1) or (kk == 1 and n == 1))
                        if k == k1:
                            B[2 * a + n][2] = t
                    if a == 1:
                        self.release(h, t)
                    if len(group) > 1 and a == 1 and i < len(group) - 1:
                        if i == len(group) - 2:
                            next(fin)
                        if i == 0:
                            self.ahead(self.np_ - 1, 1)
                            if len(group) > 2:
                                self.low("pool")
                if len(group) > 1 and a == 0:
                    fin = fin(B)
                    next(fin)
                if len(group) == 1:
                    self.low()
        for out in fin:
            pass
        self.ahead(self.np_ - 1, 1)
        return out

    def half_stats(self, r, st, a, i, *after):
        return self.Q.op("dve", lambda g: g.bn_stats(st[:, a, 4 + 6 * i:10 + 6 * i], r[:, a, i * 512:i * 512 + 512]), after)

    def stats(self, st, a, t):
        t = self.Q.op("dve", lambda g: g.bn_aggr(st[:, a, 0:2], st[:, a, 4:16]), t)
        t = self.ts("pool", st[:, a, 2:3], st[:, a, 1:2], 1e-5, None, ADD, None, t)
        return self.tt("pool", st[:, a, 3:4], st[:, a, 2:3], self.mhalf[:, 0:1], ALU.pow, t, self.tc)

    def fold(self, cols):
        A, B = self.AB[:, 0:8], self.AB[:, 8:16]
        g, b, mod = cols
        w = self.abfree
        if mod is None:
            t1 = self.cp("dve", A, g, self.tc2, w)
            t2 = self.cp("dve", B, b, self.tc2, w)
            return [t1, t2]
        p, l, j = mod
        m = self.mod[p]
        tm = [v for k, v in self.mod_t[p].items()]
        t1 = self.tt("dve", A, g, m[:, 1, :], MUL, tm, self.tc2, w)
        t2 = self.tt("dve", B, b, m[:, 1, :], MUL, tm, self.tc2, w)
        t2 = self.tt("dve", B, B, m[:, 0, :], ADD, t2)
        self.mod_t[p] = {"free": [t1, t2]}
        return [t1, t2]

    def to_cols(self, r, a, tr, tab, out):
        tmp, XH, XL = self.tmp, self.XH, self.XL
        c = slice(a * 128, a * 128 + 128)
        for f in range(0, 8, 2):
            b, P, fr = self.bank()
            for i in range(2):
                u = self.tr(P[:, i * 128:i * 128 + 128], r[:, a, (f + i) * 128:(f + i) * 128 + 128], tr, fr, self.tc, inc=i == 1)
            s = f // 2 % 2
            t1, t2 = [], []
            for i in range(2):
                A, B = self.AB[:, f + i:f + i + 1], self.AB[:, 8 + f + i:9 + f + i]
                t1.append(self.act(XH[:, f + i, c], P[:, i * 128:i * 128 + 128], ACT.Identity, u, tab, XH.dep, scale=A, bias=B))
            for i in range(2):
                A, B = self.AB[:, f + i:f + i + 1], self.AB[:, 8 + f + i:9 + f + i]
                p = P[:, i * 128:i * 128 + 128]
                if a == 0:
                    t2.append(self.act(self.tmp0[:, f + i, :], p, ACT.Identity, u, tab, self.tmp0.dep, scale=A, bias=B))
                else:
                    t2.append(self.ts("dve", tmp[:, s, i, :], p, A, B, MUL, ADD, t1, u, tab, tmp.dep, self.tmpf[s]))
            self.done(b, t1, t2)

            def low(f=f, s=s, t1=t1, t2=t2):
                src = self.tmp0[:, f:f + 2, :] if a == 0 else tmp[:, s, :, :]
                t3 = self.tt("dve", XL[:, f:f + 2, c], src, XH[:, f:f + 2, c], SUB, t2, t1, XL.dep)
                self.tmpf[s] = t3
                for i in range(2):
                    out[f + i] += [t1, t3]

            if a == 0:
                self.xlows.append(low)
            else:
                low()

    def half_norm(self, R, src, st, a, ts_, dep):
        t1 = self.ts("dve", st[:, a, 2:3], st[:, a, 0:1], st[:, a, 3:4], -1.0, MUL, MUL, ts_)
        t1 = self.act(R[:, a, 0:512], src[:, a, 0:512], ACT.Identity, t1, dep, scale=st[:, a, 3:4], bias=st[:, a, 2:3])
        t2 = self.ts("dve", R[:, a, 512:D], src[:, a, 512:D], st[:, a, 0:1], st[:, a, 3:4], SUB, MUL, ts_, dep)
        return [t1, t2]

    def post(self, gate, rows, cols, again=None):
        Q, M = self.Q, self.M

        def run(banks):
            self.settle()
            R = M.get([128, 2, D])
            n_gb = 4 if again else 2
            GB = M.get([128, n_gb, D])
            st = M.get([128, 2, 16])
            rws = rows + (again or [])
            tg = [Q.dma("pool", "lg", GB[:, i, :], self.dram["vec"][r:r + 1, :].to_broadcast([128, D]), GB.dep, Q.now("dve")) for i, r in enumerate(rws)]
            out = [[] for _ in range(8)]
            if cols is not None:
                tab = self.fold(cols)
                self.tmp = M.get([128, 2, 2, 128])
                self.tmpf = [None, None]
                self.tmp0 = M.get([128, 8, 128])
                self.xlows = []
                self.XH = M.get([128, 8, T], F32R, high=True)
                self.XL = M.get([128, 8, T], F32R, high=True)
            X, xt, free, last = self.X, [], [], []
            for a in range(2):
                ts_ = []
                for n in range(2):
                    b, P, t = banks[2 * a + n]
                    s = slice(n * 512, n * 512 + 512)
                    if gate:
                        t = self.tt("dve", R[:, a, s], P[:, :], self.G[0][:, s], MUL, t, self.gate_t[0], R.dep)
                        self.done(b, t)
                        t = self.stt(R[:, a, s], X[:, a, s], ALPHA, R[:, a, s], MUL, ADD, t, self.xt_)
                    else:
                        t = self.stt(R[:, a, s], X[:, a, s], ALPHA, P[:, :], MUL, ADD, t, self.xt_, R.dep)
                        self.done(b, t)
                    free.append(t)
                    ts_.append(self.half_stats(R, st, a, n, t, st.dep))
                ts_ = self.stats(st, a, ts_)
                while a == 1 and cols is not None and self.xlows:
                    self.xlows.pop(0)()
                self.low()
                tn = self.half_norm(R, R, st, a, ts_, None)
                e = "dve" if again or cols is None else "pool"
                if e == "dve":
                    t = self.tt(e, X[:, a, :], R[:, a, :], GB[:, 0, :], MUL, tn, tg)
                    t = self.tt(e, X[:, a, :], X[:, a, :], GB[:, 1, :], ADD, t)
                if again:
                    ts_ = self.stats(st, a, [self.half_stats(X, st, a, i, t, tn) for i in range(2)])
                    tn = self.half_norm(R, X, st, a, ts_, t)
                if again or e == "pool":
                    t = None
                    last.append((a, tn))
                xt.append(t)
                if a == 0:
                    yield
                if cols is not None:
                    self.to_cols(R, a, tn, tab, out)
                if a == 0:
                    yield
            for a, tn in last:
                i = 2 if again else 0
                t = self.tt("pool", X[:, a, :], R[:, a, :], GB[:, i, :], MUL, tn, tg)
                xt.append(self.tt("pool", X[:, a, :], X[:, a, :], GB[:, i + 1, :], ADD, t))
            self.gate_free = free
            self.xt_ = xt
            if cols is not None:
                self.abfree = out
                M.put(self.tmp, out)
                M.put(self.tmp0, out)
            for b in (R, GB, st):
                M.put(b, Q.now())
            yield out

        return run

    def ffn1(self, l, i, xt, fin):
        M = self.M
        self.gate_bias(l, 2 * i)
        hh = M.get([128, NF, T], F32R)
        hl = M.get([128, NF, T], F32R)
        sa = M.get([128, 4, T])
        hf = M.get([128, 2, T])
        ht = {}
        sfree = [sa.dep] * 4
        hfr = [hf.dep] * 2
        late = []

        def flush():
            while late:
                late.pop(0)()

        for m in range(NF // 2):
            sil = {}

            def on_a(k, P, t):
                s = (2 * m + k) % 4
                sil[k] = self.act(sa[:, s, :], P[:, 0:T], ACT.Silu, t, sfree[s])
                flush()
                return sil[k]

            def on_b(k, P, t):
                f = 2 * m + k
                s, u = f % 4, f % 2
                t1 = self.tt("dve", hf[:, u, :], P[:, 0:T], sa[:, s, :], MUL, t, sil[k], hfr[u])
                sfree[s] = t1
                flush()

                def split():
                    t2 = self.cp("act", hh[:, f, :], hf[:, u, :], t1, hh.dep)
                    t3 = self.tt("dve", hl[:, f, :], hf[:, u, :], hh[:, f, :], SUB, t2, hl.dep)
                    hfr[u] = t3
                    ht[f] = [t2, t3]

                late.append(split)
                return t1

            h, H, L, rd = self.take(("w13", l, i, 0, m))
            self.up(h, H, L, rd, self.XH, self.XL, xt, 256, on_a)
            h, H, L, rd = self.take(("w13", l, i, 1, m))
            t = self.up(h, H, L, rd, self.XH, self.XL, xt, 256, on_b)
        flush()
        M.put(self.XH, t)
        M.put(self.XL, t)
        out = self.down([("w2", l, i, k) for k in range(NF // 2)], range(NF), hh, hl, lambda k: ht[k], fin)
        for b in (hh, hl, sa, hf):
            M.put(b, self.Q.now())
        return out

    def ffn2(self, l, xt, fin):
        M = self.M
        hh = M.get([128, NF, T], F32R)
        hl = M.get([128, NF, T], F32R)
        ya = M.get([128, 4, T])
        yb = M.get([128, 2, T])
        hf = M.get([128, 2, T])
        ht = {}
        afree, bfree, hfr = [ya.dep] * 4, [yb.dep] * 2, [hf.dep] * 2

        late = []

        def flush():
            while late:
                late.pop(0)()

        def conv(y, P, r, t, fr):
            c = lambda tap: self.COL[:, ROW["cw"] + (l * 3 + tap) * 44 + r:ROW["cw"] + (l * 3 + tap) * 44 + r + 1]
            bb = self.COL[:, ROW["cb"] + l * 44 + r:ROW["cb"] + l * 44 + r + 1]
            t1 = self.act(y, P[:, 0:T], ACT.Identity, t, fr, self.tc2, scale=c(1), bias=bb)
            flush()
            t2 = self.stt(y[:, 1:T], P[:, 0:T - 1], c(0), y[:, 1:T], MUL, ADD, t1)
            return self.stt(y[:, 0:T - 1], P[:, 1:T], c(2), y[:, 0:T - 1], MUL, ADD, t2)

        for m in range(NF // 2):
            sil = {}

            def on_a(k, P, t):
                f = 2 * m + k
                y = ya[:, f % 4, :]
                t1 = conv(y, P, f, t, afree[f % 4])

                def silu():
                    sil[k] = self.act(y, y, ACT.Silu, t1)

                late.append(silu)
                return t1

            def on_b(k, P, t):
                f = 2 * m + k
                u = f % 2
                y = yb[:, u, :]
                t1 = conv(y, P, 22 + f, t, bfree[u])
                t2 = self.tt("dve", hf[:, u, :], y, ya[:, f % 4, :], MUL, t1, sil[k], hfr[u])
                afree[f % 4] = bfree[u] = t2

                def split():
                    t3 = self.cp("act", hh[:, f, :], hf[:, u, :], t2, hh.dep)
                    t4 = self.tt("dve", hl[:, f, :], hf[:, u, :], hh[:, f, :], SUB, t3, hl.dep)
                    hfr[u] = t4
                    ht[f] = [t3, t4]

                late.append(split)
                return t1

            h, H, L, rd = self.take(("wup", l, 0, m))
            self.up(h, H, L, rd, self.XH, self.XL, xt, 256, on_a)
            h, H, L, rd = self.take(("wup", l, 1, m))
            t = self.up(h, H, L, rd, self.XH, self.XL, xt, 256, on_b)
        flush()
        M.put(self.XH, t)
        M.put(self.XL, t)
        out = self.down([("wdn", l, k) for k in range(NF // 2)], range(NF), hh, hl, lambda k: ht[k], fin)
        for b in (hh, hl, ya, yb, hf):
            M.put(b, self.Q.now())
        return out

    def mixer1(self, l, xt, fin):
        Q, M = self.Q, self.M
        COL = self.COL
        self.gate_bias(l, 1)
        cols = mixer1_cols()
        gt = M.get([128, 2, 128])
        gq = M.get([128, 9, T])
        cq = M.get([128, 6, T])
        mq = M.get([128, 4, T])
        zs = M.get([128, 2, 384])
        so = M.get([128, 2, 384])
        mv = M.get([128, 2, 256])
        vx = M.get([128, 2, 6, 65])
        t0 = self.mset("pool", gt[:, :, :], 0.0, gt.dep)
        t1 = self.mset("pool", vx[:, :, :, :], 1.0, vx.dep)
        tg = {}
        ready = {}

        def gates(a, P, t):
            o = []
            for src, dst in ((0, 0), (6, 64), (12, 96), (18, 32)):
                o.append(self.cp("dve", gt[:, a, dst:dst + 6], P[:, src:src + 6], t, t0))
            tg[a] = o
            return o

        def fm(g, P, t):
            if g < 15:
                y = gq[:, g, :] if g < 9 else cq[:, g - 9, :]
                dep = gq.dep if g < 9 else cq.dep
                r = ROW["gconv"] + l * 36 + g if g < 9 else ROW["mconv"] + l * 24 + g - 9
                n = 9 if g < 9 else 6
                w = [COL[:, r + tap * n:r + tap * n + 1] for tap in range(4)]
                u = self.act(y, P[:, 0:T], ACT.Identity, t, dep, self.tc2, scale=w[3])
                flush()
                for j in range(1, 4):
                    u = self.stt(y[:, j:T], P[:, 0:T - j], w[3 - j], y[:, j:T], MUL, ADD, u)

                def silu():
                    ready[g] = self.act(y, y, ACT.Silu, u)

                late.append(silu)
                return u
            flush()
            ready[g] = self.cp("act", mq[:, g - 15, :], P[:, 0:T], t, mq.dep)
            return ready[g]

        tm, mix, rows = {}, [], []
        late = []

        def flush():
            while late:
                late.pop(0)()

        def gdn_task():
            r = yield from self.gate_rows(l, gt, tg)
            rows.append(r)
            while any(g not in ready for g in range(9)):
                yield "wait"
            yield from self.gdn(l, gq, [ready[g] for g in range(9)], zs, ready, rows[0], mix, tm)

        def mlstm_task():
            while not rows or any(g not in ready for g in range(9, 15)) or ("tm", 16, 1) not in ready or "inv" not in ready:
                yield "wait"
            yield from self.mlstm(l, cq, [ready[g] for g in range(9, 15)], vx, so, ready, rows[0], mix, tm)

        def moba_task():
            while any(g not in ready for g in range(15, 19)) or ("tm", 14, 1) not in ready:
                yield "wait"
            yield from self.moba(mq, [ready[g] for g in range(15, 19)], mv, [ready["tm", 14, a] for a in range(2)], mix, tm)

        for n in MIX1:
            kind, c = cols[n]
            h, H, L, rd = self.take(("win", l, n))
            w = len(c)
            if n == 0:
                te = self.tokmajor(h, H, L, rd, self.XH, self.XL, xt, w, gates)
                g = gdn_task()
                self.tasks += [g, mlstm_task(), moba_task()]
            elif kind == "fm":
                te = self.up(h, H, L, rd, self.XH, self.XL, xt, w, lambda m, P, t, n=n: fm(2 * (n - 1) + m, P, t))
            else:
                def tmcb(a, P, t, n=n, w=w):
                    flush()
                    o = []
                    if n == 11:
                        o.append(self.act(zs[:, a, 0:256], P[:, 0:256], ACT.Silu, t, zs.dep))
                    elif n == 12:
                        o.append(self.act(zs[:, a, 256:384], P[:, 0:128], ACT.Silu, t, zs.dep))
                        o.append(self.act(so[:, a, 0:128], P[:, 128:256], ACT.Sigmoid, t, so.dep))
                    elif n == 13:
                        o.append(self.act(so[:, a, 128:384], P[:, 0:256], ACT.Sigmoid, t, so.dep))
                    elif n == 14:
                        o.append(self.cp("act", mv[:, a, :], P[:, 0:256], t, mv.dep))
                    elif n == 15:
                        o.append(self.cp("act", vx[:, a, 0:4, 0:64], rr(P[:, 0:256], "p (h d) -> p h d", h=4), t, t1))
                    else:
                        o.append(self.cp("act", vx[:, a, 4:6, 0:64], rr(P[:, 0:128], "p (h d) -> p h d", h=2), t, t1))
                    ready[("tm", n, a)] = o
                    return o
                te = self.tokmajor(h, H, L, rd, self.XH, self.XL, xt, w, tmcb)
        M.put(self.XH, te)
        M.put(self.XL, te)
        mh = M.get([128, 8, T], F32R, high=True)
        ml = M.get([128, 8, T], F32R, high=True)
        mix += [mh, ml]
        ks = [2 * k + i for k in WOUT1 for i in range(2)]
        while ks[1] not in tm:
            assert self.beside()

        def end():
            self.finish_tasks()
            for b in (*rows[0][:4], gt, self.PSEL):
                M.put(b, Q.now())

        out = self.down([("wout", l, k) for k in WOUT1], ks, mh, ml, self.need(tm), self.once(end, fin), 2)
        M.put(mh, Q.now("pe"))
        M.put(ml, Q.now("pe"))
        return out

    def gate_rows(self, l, gt, tg):
        Q, M = self.Q, self.M
        z = []
        mk = lambda s: M.get(s)
        RT, RB, RC, DC = mk([128, 2, 2, 128]), mk([128, T]), mk([128, T]), mk([128, 4])
        self.PSEL = mk([128, 9, 128])
        for i in range(9):
            r = 32 * (i // 3) + 2 * (i % 3)
            z.append(self.cp("pool", rr(self.PSEL[:, i, :], "p (a b) -> p a b", a=2), bc(self.ident[:, r:r + 2], 64), self.tc, self.PSEL.dep))
        A, B, y, e, gl, G, Mx, ir, dd = (mk([128, T + 1]) for _ in range(9))
        for t in (RB, RC, DC, A, B, y, Mx, ir):
            z.append(self.mset("pool", t[:, :], 0.0, t.dep))
        b, P, f = self.bank()
        for a in range(2):
            tp = self.tr(P[:, a * 128:a * 128 + 128], gt[:, a, :], tg[a], f, self.tc, inc=a == 1)
        q0, q1, q2, q3, q01 = slice(0, 32), slice(32, 64), slice(64, 96), slice(96, 128), slice(0, 64)
        hb = self.HD[:, 2 * l:2 * l + 1]
        w = slice(0, T)
        t = self.ts("dve", y[q01, w], P[q01, 0:T], hb[q01], self.sgn[q01], ADD, MUL, tp, z, self.th, self.tc)
        ti = self.ts("dve", ir[q3, w], P[q3, 0:T], hb[q3], None, ADD, None, tp, z, self.th)
        ti = self.cp("dve", ir[q1, w], ir[q3, w], ti)
        tb = self.act(A[q2, w], P[q2, 0:T], ACT.Exp, tp, z, t, ti, scale=-1.0)
        self.done(b, t, ti, tb)
        yield
        te = self.act(e[q01, w], y[q01, w], ACT.Abs, t, e.dep)
        te = self.act(e[q01, w], e[q01, w], ACT.Exp, te, scale=-1.0)
        te = self.act(e[q01, w], e[q01, w], ACT.Ln, te, bias=1.0)
        yield
        cf = self.act(dd[q01, 0:1], self.HD[q01, 2 * l + 1:2 * l + 2], ACT.Exp, self.th, dd.dep)
        cf = self.ts("dve", dd[q01, 1:2], dd[q01, 0:1], -1.0, None, MUL, None, cf)
        tb = self.ts("dve", A[q2, w], A[q2, w], 1.0, None, ADD, None, tb)
        tb = self.rcp(A[q2, w], A[q2, w], tb)
        yield
        t = self.stt(gl[q01, w], y[q01, w], 0.0, e[q01, w], MAX, ADD, te, gl.dep)
        t = self.ts("dve", gl[q01, w], gl[q01, w], dd[q01, 1:2], None, MUL, None, t, cf)
        yield
        tG = Q.op("dve", lambda g: g.tensor_tensor_scan(G[q01, w], self.rmask[q01, :], gl[q01, w], 0.0, MUL, ADD), [t, G.dep])
        tM = Q.op("dve", lambda g: g.tensor_tensor_scan(Mx[q1, 1:T + 1], gl[q1, w], ir[q1, w], 0.0, ADD, MAX), [t, ti])
        c4 = lambda ap: rr(ap, "p (c s) -> p c s", c=4)
        glast = lambda q: c4(G[q, w])[:, :, 63:64]
        td = self.tt("dve", c4(dd[q01, w]), glast(q01).to_broadcast([64, 4, 64]), c4(G[q01, w]), SUB, tG)
        yield
        o = [self.ts("dve", A[q0, w], G[q0, w], -1.0, None, MUL, None, tG)]
        o.append(self.tt("dve", A[q1, w], ir[q1, w], G[q1, w], SUB, tG))
        mL = c4(Mx[q1, 1:T + 1])[:, :, 63:64]
        mP = c4(Mx[q1, 0:T])[:, :, 0:1]
        yield
        t = self.tt("dve", e[q1, w], dd[q1, w], ir[q1, w], ADD, td, te)
        t = self.tt("dve", c4(e[q1, w]), c4(e[q1, w]), mL.to_broadcast([32, 4, 64]), SUB, t, tM)
        o.append(self.act(A[q3, w], e[q1, w], ACT.Exp, t))
        yield
        r = [self.cp("dve", RB[q0, :], G[q0, w], tG)]
        tr1 = self.tt("dve", RB[q1, :], G[q1, w], Mx[q1, 1:T + 1], SUB, tM)
        r.append(tr1)
        t = self.tt("dve", c4(gl[q1, w]), c4(RB[q1, :]), mP.to_broadcast([32, 4, 64]), ADD, tr1, tM)
        yield
        c = [self.act(RC[q1, :], gl[q1, w], ACT.Exp, t)]
        c.append(self.act(RC[q0, :], G[q0, w], ACT.Exp, tG))
        c.append(self.cp("dve", RC[q2, :], A[q2, w], tb))
        o.append(self.act(B[q0, w], dd[q0, w], ACT.Exp, td))
        o.append(self.act(B[q1, w], Mx[q1, 1:T + 1], ACT.Exp, tM, scale=-1.0))
        yield
        t = self.act(y[q2, w], G[q0, w], ACT.Exp, tG)
        o.append(self.tt("dve", B[q2, w], y[q2, w], A[q2, w], MUL, t, tb))
        yield
        g4 = G[q1, w][:, 63:T:64]
        t = self.tt("dve", ir[q1, 0:4], g4, Mx[q1, 0:T:64], ADD, r, o)
        t = self.tt("dve", ir[q1, 4:8], ir[q1, 0:4], Mx[q1, 64:T + 1:64], SUB, t)
        tdc = self.act(DC[q1, :], ir[q1, 4:8], ACT.Exp, t)
        yield
        yield
        b, P, f = self.bank()
        for i, S in enumerate((A, B)):
            for a in range(2):
                t = self.tr(P[:, (2 * i + a) * 128:(2 * i + a) * 128 + 128], S[:, a * 128:a * 128 + 128], o, f, inc=i + a == 2)
        trt = self.cp("act", rr(RT[:, :, :, :], "p i a c -> p (i a c)"), P[:, :], t, RT.dep)
        self.done(b, trt)
        for x in (A, B, y, e, gl, G, Mx, ir, dd):
            M.put(x, Q.now())
        return RT, RB, RC, DC, trt, [r, z], [c, z], [tdc, z]

    def sel(self, K, r, n):
        if n == 1:
            return self.ident[0:K, r:r + 1].to_broadcast([K, 128])
        return self.PSEL[0:K, (r // 32) * 3 + (r % 32) // 2, :]

    def decays(self, q, RT, RB, trt, trb):
        Dk = yield from self.room([128, 12, 128])
        out = []
        for g in range(4):
            b, P, f = self.bank()
            for j in range(3):
                u = 3 * g + j
                h, a = 2 * ((u % 6) // 2) + u // 6, u % 2
                t = self.mm(P[:, j * 128:j * 128 + 128], self.sel(64, 32 * q + h, 1), RB[0:64, a * 128:a * 128 + 128], True, True, trb, f, inc=j == 2)
            o = []
            for j in range(3):
                u = 3 * g + j
                h, a = 2 * ((u % 6) // 2) + u // 6, u % 2
                o.append(self.stt(Dk[:, u, :], P[:, j * 128:j * 128 + 128], RT[:, 0, a, 32 * q + h:32 * q + h + 1], self.neg, ADD, ADD, t, trt, Dk.dep))
            self.done(b, o)
            out.append(self.act(Dk[:, 3 * g:3 * g + 3, :], Dk[:, 3 * g:3 * g + 3, :], ACT.Exp, o))
            if g % 2:
                yield
        return Dk, out

    def units(self, lT, rT, tin, cb):
        for g in range(4):
            b, P, f = self.bank()
            for j in range(3):
                u = 3 * g + j
                par, pr, a = u // 6, (u % 6) // 2, u % 2
                rs, cs = slice(64 * par, 64 * par + 64), slice(a * 128, a * 128 + 128)
                t = self.mm(P[:, j * 128:j * 128 + 128], lT[rs, pr, cs], rT[rs, pr, cs], True, True, tin, f, inc=j == 2)
            self.done(b, cb(g, P, t))
            if g % 2:
                yield

    def pairs(self, K, q, R, tr, cb):
        for p in range(3):
            b, P, f = self.bank()
            t = self.mm(P[:, 0:T], self.sel(K, 32 * q + 2 * p, 2), R[0:K, :], True, True, tr, f, inc=True)
            self.done(b, cb(p, P, t))
        yield

    def tok(self, src, tin, cb):
        for a in range(2):
            b, P, f = self.bank()
            for p in range(3):
                t = self.tr(P[:, p * 128:p * 128 + 128], src[:, p, a * 128:a * 128 + 128], tin, f, inc=p == 2)
            self.done(b, cb(a, P, t))
        yield

    def to_mix(self, src, tin, k, col, mh, ml, tm, tiles):
        tmp = yield from self.room([128, T])
        tf = tmp.dep
        for i in range(tiles):
            b, P, f = self.bank()
            for a in range(2):
                t = self.tr(P[:, a * 128:a * 128 + 128], src[:, a, i * 128:i * 128 + 128], tin, f, inc=a == 1)
            c = col(i)
            t1 = self.act(mh[:, k + i, :], P[:, 0:T], ACT.Identity, t, mh.dep, self.tc2, scale=c)
            t2 = self.ts("dve", tmp[:, :], P[:, 0:T], c, None, MUL, None, t, tf, t1)
            self.done(b, t1, t2)
            tf = self.tt("dve", ml[:, k + i, :], tmp[:, :], mh[:, k + i, :], SUB, t2, t1, ml.dep)
            tm[k + i] = [t1, tf]
        self.M.put(tmp, tf)
        yield

    def gdn(self, l, gq, tq, zs, ready, rows, mix, tm):
        Q, M = self.Q, self.M
        RT, RB, RC, DC, trt, trb, trc, tdc = rows
        h6 = lambda ap: rr(ap, "p (h d) -> p h d", h=6)
        rs = yield from self.room([128, 6, T])
        tn = []
        tsq = [self.act(rs[:, 2 * i:2 * i + 2, :], gq[:, 2 * i:2 * i + 2, :], ACT.Square, tq[2 * i:2 * i + 2], rs.dep) for i in range(3)]
        yield
        for i in range(3):
            s = slice(2 * i, 2 * i + 2)
            b, P, f = self.bank()
            t = self.mm(P[:, :], self.ones64, rs[:, s, :], True, True, tsq[i], f, self.tc, inc=True)
            t = self.act(rs[:, s, :], P[:, :], ACT.Ln, t, bias=1e-6)
            self.done(b, t)
            t = self.act(rs[:, s, :], rs[:, s, :], ACT.Exp, t, scale=-0.5)
            for k in (2 * i, 2 * i + 1):
                tn.append(self.stt(gq[:, k, :], gq[:, k, :], 0.125 if k < 3 else 1.0, rs[:, k, :], MUL, MUL, t, tq))
            yield
        M.put(rs, Q.now("dve", "act"))
        qn, kn, vn_ = gq[:, 0:3, :], gq[:, 3:6, :], gq[:, 6:9, :]
        Dk, td = yield from self.decays(0, RT, RB, trt, trb)
        kb = yield from self.room([128, 3, T])
        qd = yield from self.room([128, 3, T])
        GLc = yield from self.room([128, 3, 4])
        tkb, tqd, tgl = [], [], []

        def on_beta(p, P, t):
            tkb.append(self.tt("dve", kb[:, p, :], kn[:, p, :], P[:, 0:T], MUL, t, tn, kb.dep))
            return tkb[-1]

        def on_g(p, P, t):
            tqd.append(self.tt("dve", qd[:, p, :], qn[:, p, :], P[:, 0:T], MUL, t, tn, qd.dep))
            tgl.append(self.cp("dve", GLc[:, p, :], P[:, 63:T:64], t, GLc.dep))
            return [tqd[-1], tgl[-1]]

        yield from self.pairs(128, 2, RC, trc, on_beta)
        yield from self.pairs(128, 0, RC, trc, on_g)
        AT = yield from self.room([128, 12, 128])
        ta = [None] * 4

        def on_a(g, P, t):
            s = slice(3 * g, 3 * g + 3)
            ta[g] = self.tt("dve", rr(AT[:, s, :], "p u t -> p (u t)"), P[:, 0:384], rr(Dk[:, s, :], "p u t -> p (u t)"), MUL, t, td[g], AT.dep)
            return ta[g]

        tat = [None] * 4

        def on_q(g, P, t):
            s = slice(3 * g, 3 * g + 3)
            d = rr(Dk[:, s, :], "p u t -> p (u t)")
            tat[g] = self.tt("dve", d, P[:, 0:384], d, MUL, t, ta[g])
            return tat[g]

        yield from self.units(kn, kb, [tn, tkb], on_a)
        yield from self.units(kn, qn, tn, on_q)
        M.put(kb, Q.now("pe"))
        Xb = yield from self.room([128, 12, 128])
        XT = yield from self.room([128, 12, 128])
        Ub = yield from self.room([128, 12, 128])
        Al = yield from self.room([128, 12, 128])
        fl = lambda b, g: rr(b[:, 3 * g:3 * g + 3, :], "p u t -> p (u t)")
        idb = self.ident.unsqueeze(1).to_broadcast([128, 3, 128])
        tX, tXT, tU, tA, rA, rU = ([None] * 4 for _ in range(6))

        def part(lv, g):
            mk = self.lvl[:, lv * 128:lv * 128 + 128].unsqueeze(1).to_broadcast([128, 3, 128])
            tA[g] = self.tt("dve" if g % 2 else "pool", Al[:, 3 * g:3 * g + 3, :], AT[:, 3 * g:3 * g + 3, :], mk, MUL, ta[g], rA[g], Al.dep)

        for g in range(4):
            part(0, g)
        yield
        for lv in range(6):
            for g in range(4):
                b, P, f = self.bank()
                for j in range(3):
                    u = 3 * g + j
                    t = self.mm(P[:, j * 128:j * 128 + 128], Al[:, u, :], self.ident if lv == 0 else Xb[:, u, :], True, True, tA[g], tX[g], f, inc=j == 2)
                rA[g] = t
                if lv == 0:
                    tX[g] = self.tt("dve", Xb[:, 3 * g:3 * g + 3, :], idb, rr(P[:, 0:384], "p (u t) -> p u t", u=3), SUB, t, Xb.dep)
                    tXT[g] = self.tt("dve", XT[:, 3 * g:3 * g + 3, :], idb, Al[:, 3 * g:3 * g + 3, :], SUB, tA[g], XT.dep)
                    rA[g] = [t, tXT[g]]
                    self.done(b, tX[g])
                else:
                    tU[g] = self.cp("act", fl(Ub, g), P[:, 0:384], t, Ub.dep, rU[g])
                    self.done(b, tU[g])
            if lv < 5:
                for g in range(4):
                    part(lv + 1, g)
            yield
            if lv == 0:
                continue
            for g in range(4):
                if lv < 5:
                    b, P, f = self.bank()
                    for j in range(3):
                        u = 3 * g + j
                        t = self.mm(P[:, j * 128:j * 128 + 128], XT[:, u, :], Ub[:, u, :], True, True, tU[g], tXT[g], f, inc=j == 2)
                    tX[g] = self.tt("dve", fl(Xb, g), fl(Xb, g), P[:, 0:384], SUB, t, tX[g])
                    self.done(b, tX[g])
                b, P, f = self.bank()
                for j in range(3):
                    u = 3 * g + j
                    t = self.mm(P[:, j * 128:j * 128 + 128], Ub[:, u, :], XT[:, u, :], True, True, tU[g], tXT[g], f, inc=j == 2)
                rU[g] = t
                tXT[g] = self.tt("dve", fl(XT, g), fl(XT, g), P[:, 0:384], SUB, t, tXT[g])
                self.done(b, tXT[g])
                if g % 2:
                    yield
        ready["inv"] = True
        for b in (Xb, Ub, Al, AT):
            M.put(b, Q.now())
        kd = yield from self.room([128, 2, 384])
        kg = yield from self.room([128, 2, 384])
        vb = yield from self.room([128, 2, 384])
        colv = lambda i, a, q: bc(RT[:, i, a, 32 * q:32 * q + 6], 64)
        tkd, tvb = [None] * 2, [None] * 2

        def on_k(a, P, t):
            t1 = self.tt("dve", h6(kd[:, a, :]), h6(P[:, 0:384]), colv(1, a, 0), MUL, t, trt, kd.dep)
            t2 = self.tt("dve", h6(kg[:, a, :]), h6(P[:, 0:384]), colv(1, a, 2), MUL, t, trt, kg.dep)
            tkd[a] = [t1, t2]
            return [t1, t2]

        def on_v(a, P, t):
            tvb[a] = self.tt("dve", h6(vb[:, a, :]), h6(P[:, 0:384]), colv(0, a, 2), MUL, t, trt, vb.dep)
            return tvb[a]

        yield from self.tok(kn, tn, on_k)
        yield from self.tok(vn_, tq, on_v)
        un = lambda h, a: (h % 2) * 6 + (h // 2) * 2 + a
        us = yield from self.room([128, 2, 384])
        wT = yield from self.room([128, 3, T])
        tu, tw = [], []
        for a in range(2):
            b, P, f = self.bank()
            for h in range(6):
                t = self.mm(P[:, h * 64:h * 64 + 64], XT[:, un(h, a), :], vb[:, a, h * 64:h * 64 + 64], True, True, tvb[a], tXT, f, inc=h == 5)
            tu.append(self.cp("act", us[:, a, :], P[:, 0:384], t, us.dep))
            self.done(b, tu[-1])
        yield
        for p in range(3):
            b, P, f = self.bank()
            for h in (2 * p, 2 * p + 1):
                for a in range(2):
                    t = self.mm(P[64 * (h % 2):64 * (h % 2) + 64, a * 128:a * 128 + 128], kg[:, a, h * 64:h * 64 + 64], XT[:, un(h, a), :], True, True, tkd, tXT, f, inc=(h % 2 == 1 and a == 1))
            tw.append(self.cp("act", wT[:, p, :], P[:, 0:T], t, wT.dep))
            self.done(b, tw[-1])
        yield
        M.put(XT, Q.now("pe"))
        M.put(vb, Q.now("pe"))
        M.put(kg, Q.now("pe"))
        S2 = yield from self.room([128, 3, 128])
        vn = yield from self.room([128, 2, 384])
        os_ = yield from self.room([128, 2, 384])
        ts_ = self.mset("pool", S2[:, :, :], 0.0, S2.dep)
        to = []
        for a in range(2):
            bo, Po, fo = self.bank()
            tvn = []
            for n in (2 * a, 2 * a + 1):
                o = 64 * (n % 2)
                r, c = slice(o, o + 64), slice(64 * n, 64 * n + 64)
                b, P, f = self.bank()
                for p in range(3):
                    t = self.mm(P[r, p * 128:p * 128 + 128], wT[:, p, c], S2[:, p, :], True, True, ts_, tw, f, inc=p == 2)
                tv = self.tt("dve", vn[r, a, :], us[r, a, :], P[r, 0:384], SUB, t, tu, vn.dep)
                self.done(b, tv)
                tvn.append(tv)
                yield
                for p in range(3):
                    tq_ = self.mm(Po[r, p * 128:p * 128 + 128], qd[:, p, c], S2[:, p, :], p == 0, False, ts_, tqd, fo, inc=p == 2, share=True)
                if n == 3:
                    continue
                b, P, f = self.bank()
                for p in range(3):
                    t = self.mm(P[:, p * 128:p * 128 + 128], kd[r, a, p * 128:p * 128 + 128], vn[r, a, p * 128:p * 128 + 128], True, True, tv, tkd, f, inc=p == 2)
                ts_ = []
                for p in range(3):
                    for e in range(2):
                        q = slice(64 * e, 64 * e + 64)
                        qq = slice(p * 128 + 64 * e, p * 128 + 64 * e + 64)
                        ts_.append(self.stt(S2[q, p, q], S2[q, p, q], GLc[q, p, n:n + 1], P[q, qq], MUL, ADD, t, tq_, tgl))
                self.done(b, ts_)
                yield
            for h in range(6):
                t = self.mm(Po[:, h * 64:h * 64 + 64], Dk[:, un(h, a), :], vn[:, a, h * 64:h * 64 + 64], False, h == 5, tvn, tat, inc=h == 5, share=True)
            to.append(self.cp("act", os_[:, a, :], Po[:, 0:384], t, os_.dep))
            self.done(bo, to[-1])
            yield
        for b in (S2, vn, us, wT, kd, qd, Dk, GLc, gq):
            M.put(b, Q.now())
        while any(("tm", n, 1) not in ready for n in (11, 12)) or not mix:
            yield "wait"
        tz = [ready["tm", n, a] for n in (11, 12) for a in range(2)]
        mh, ml = mix
        sq = yield from self.room([128, 2, 384])
        ms = yield from self.room([128, 4, 6])
        two = lambda f: [f(a, t[a]) for a in range(2)]
        t = [[to[a], ms.dep] for a in range(2)]
        t = two(lambda a, t: self.act(sq[:, a, :], os_[:, a, :], ACT.Square, t, sq.dep))
        yield
        t = two(lambda a, t: self.red(ms[:, a, :], h6(sq[:, a, :]), ADD, t))
        t = two(lambda a, t: self.ts("pool", ms[:, a, :], ms[:, a, :], 1 / 64, 1e-6, MUL, ADD, t))
        t = two(lambda a, t: self.tt("pool", ms[:, 2 + a, :], ms[:, a, :], self.mhalf[:, 0:6], ALU.pow, t))
        yield
        t = two(lambda a, t: self.tt("dve", h6(os_[:, a, :]), h6(os_[:, a, :]), bc(ms[:, 2 + a, :], 64), MUL, t))
        tf = two(lambda a, t: self.tt("dve", os_[:, a, :], os_[:, a, :], zs[:, a, :], MUL, t, tz))
        yield
        yield from self.to_mix(os_, tf, 0, lambda i: self.COL[:, ROW["gnorm"] + l:ROW["gnorm"] + l + 1], mh, ml, tm, 3)
        for b in (sq, ms, os_, zs):
            M.put(b, Q.now())

    def moba(self, mq, tq, mv, tv, mix, tm):
        Q, M = self.Q, self.M
        S = yield from self.room([128, 4, 384])
        PT = yield from self.room([128, 4, 384])
        mx = yield from self.room([128, 4, 8])
        tp, back = {}, []
        for h in (0, 2, 1, 3):
            r = slice(64 * (h % 2), 64 * (h % 2) + 64)
            b, P, f = self.bank()
            for a in range(2):
                n = 128 * (a + 1)
                t = self.mm(P[:, 128 * a:128 * a + n], mq[r, h // 2, a * 128:a * 128 + 128], mq[r, 2 + h // 2, 0:n], True, True, tq, f, inc=a == 1)
            c = [self.stt(S[:, h, 0:128], P[:, 0:128], 0.125, self.causal, MUL, ADD, t, S.dep),
                 self.stt(S[:, h, 256:384], P[:, 256:384], 0.125, self.causal, MUL, ADD, t, S.dep),
                 self.ts("dve", S[:, h, 128:256], P[:, 128:256], 0.125, None, MUL, None, t, S.dep)]
            self.done(b, c)
            sl = [slice(0, 128), slice(128, 384)]
            t = [self.red(mx[:, h, a:a + 1], S[:, h, sl[a]], MAX, c, mx.dep) for a in range(2)]
            t = self.ts("dve", mx[:, h, 2:4], mx[:, h, 0:2], -1.0, None, MUL, None, t)
            t = [self.act(S[:, h, sl[a]], S[:, h, sl[a]], ACT.Exp, t, bias=mx[:, h, 2 + a:3 + a], accum_out=mx[:, h, 4 + a:5 + a]) for a in range(2)]

            def scale(h=h, t=t):
                t = self.rcp(mx[:, h, 6:8], mx[:, h, 4:6], t)
                for a in range(2):
                    tp[h, a] = self.ts("dve", S[:, h, sl[a]], S[:, h, sl[a]], mx[:, h, 6 + a:7 + a], None, MUL, None, t)

            back.append(scale)
            if len(back) > 1:
                back.pop(0)()
            yield
        back.pop(0)()
        yield
        tpt = {}
        for h in range(4):
            b, P, f = self.bank()
            for i in range(3):
                t = self.tr(P[:, i * 128:i * 128 + 128], S[:, h, i * 128:i * 128 + 128], tp[h, 0], tp[h, 1], f, inc=i == 2)
            tpt[h] = self.cp("act", PT[:, h, :], P[:, 0:384], t, PT.dep)
            self.done(b, tpt[h])
            if h % 2:
                yield
        while not mix:
            yield "wait"
        mh, ml = mix
        for p in range(2):
            b, P, f = self.bank()
            for h in (2 * p, 2 * p + 1):
                r = slice(64 * (h % 2), 64 * (h % 2) + 64)
                d = slice(64 * h, 64 * h + 64)
                self.mm(P[r, 0:256], mv[:, 0, d], PT[:, h, 0:256], True, False, tpt[h], tv, f)
                t = self.mm(P[r, 128:256], mv[:, 1, d], PT[:, h, 256:384], False, True, inc=h % 2 == 1)
            t1 = self.cp("act", mh[:, 3 + p, :], P[:, 0:T], t, mh.dep)
            t2 = self.tt("dve", ml[:, 3 + p, :], P[:, 0:T], mh[:, 3 + p, :], SUB, t1, ml.dep)
            self.done(b, t1, t2)
            tm[3 + p] = [t1, t2]
            yield
        for b in (S, PT, mx, mq, mv):
            M.put(b, Q.now())

    def mlstm(self, l, cq, tq, vx, so, ready, rows, mix, tm):
        Q, M = self.Q, self.M
        RT, RB, RC, DC, trt, trb, trc, tdc = rows
        tvx = [ready["tm", n, a] for n in (15, 16) for a in range(2)]
        h6 = lambda ap: rr(ap, "p (h d) -> p h d", h=6)
        q, k = cq[:, 0:3, :], cq[:, 3:6, :]
        Dk, td = yield from self.decays(1, RT, RB, trt, trb)
        qa = yield from self.room([128, 3, T])
        DCc = yield from self.room([128, 3, 4])
        tqa, tpp = [], [None] * 4

        def on_a(p, P, t):
            tqa.append(self.stt(qa[:, p, :], q[:, p, :], 0.125, P[:, 0:T], MUL, MUL, t, tq, qa.dep))
            return tqa[-1]

        yield from self.pairs(128, 1, RC, trc, on_a)
        b, P, f = self.bank()
        for p in range(3):
            t = self.mm(P[:, 4 * p:4 * p + 4], self.sel(64, 32 + 2 * p, 2), DC[0:64, :], True, True, tdc, f, inc=p == 2)
        tdc = self.cp("dve", rr(DCc[:, :, :], "p a b -> p (a b)"), P[:, 0:12], t, DCc.dep)
        self.done(b, tdc)

        def on_p(g, P, t):
            d = rr(Dk[:, 3 * g:3 * g + 3, :], "p u t -> p (u t)")
            tpp[g] = self.stt(d, P[:, 0:384], 0.125, d, MUL, MUL, t, td[g])
            return tpp[g]

        yield from self.units(k, q, tq, on_p)
        ks = yield from self.room([128, 2, 384])
        tks = [None] * 2

        def on_k(a, P, t):
            tks[a] = self.tt("dve", h6(ks[:, a, :]), h6(P[:, 0:384]), bc(RT[:, 0, a, 96:102], 64), MUL, t, trt, ks.dep)
            return tks[a]

        yield from self.tok(k, tq, on_k)
        un = lambda h, a: (h % 2) * 6 + (h // 2) * 2 + a
        Cx = yield from self.room([128, 3, 130])
        nd = yield from self.room([128, 2, 6, 65])
        ts_ = self.mset("pool", Cx[:, :, :], 0.0, Cx.dep)
        tn = []
        for a in range(2):
            bo, Po, fo = self.bank()
            for n in (2 * a, 2 * a + 1):
                o = 64 * (n % 2)
                r, c = slice(o, o + 64), slice(64 * n, 64 * n + 64)
                for p in range(3):
                    tq_ = self.mm(Po[r, p * 130:p * 130 + 130], qa[:, p, c], Cx[:, p, :], p == 0, False, ts_, tqa, fo, inc=p == 2, share=True)
                if n == 3:
                    continue
                b, P, f = self.bank()
                for p in range(3):
                    t = self.mm(P[:, p * 130:p * 130 + 130], ks[r, a, p * 128:p * 128 + 128], rr(vx[r, a, 2 * p:2 * p + 2, :], "p h d -> p (h d)"), True, True, tks, tvx, f, inc=p == 2)
                ts_ = []
                for p in range(3):
                    for e in range(2):
                        q_, cc = slice(64 * e, 64 * e + 64), slice(65 * e, 65 * e + 65)
                        ts_.append(self.stt(Cx[q_, p, cc], Cx[q_, p, cc], DCc[q_, p, n:n + 1], P[q_, p * 130 + 65 * e:p * 130 + 65 * e + 65], MUL, ADD, t, tq_, tdc))
                self.done(b, ts_)
                yield
            for h in range(6):
                t = self.mm(Po[:, h * 65:h * 65 + 65], Dk[:, un(h, a), :], vx[:, a, h, :], False, h == 5, tpp, tvx, inc=h == 5, share=True)
            tn.append(self.cp("act", rr(nd[:, a, :, :], "p h d -> p (h d)"), Po[:, 0:390], t, nd.dep))
            self.done(bo, tn[-1])
            yield
        for b in (Cx, ks, qa, Dk, DCc, cq, vx):
            M.put(b, Q.now())
        hc = yield from self.room([128, 2, 384])
        sq = yield from self.room([128, 2, 384])
        s = yield from self.room([128, 2, 8, 6])
        tf = []
        while not mix:
            yield "wait"
        mh, ml = mix
        tso = [ready["tm", n, a] for n in (12, 13) for a in range(2)]
        t = [[tn[a], s.dep] for a in range(2)]
        two = lambda f: [f(a, t[a]) for a in range(2)]
        t = two(lambda a, t: self.ts("dve", s[:, a, 0, :], nd[:, a, :, 64], -1.0, None, MUL, None, t))
        t = two(lambda a, t: self.tt("dve", s[:, a, 0, :], s[:, a, 0, :], nd[:, a, :, 64], MAX, t))
        t = two(lambda a, t: self.tt("dve", s[:, a, 1, :], s[:, a, 0, :], RT[:, 1, a, 32:38], MAX, t, trt))
        t = two(lambda a, t: self.rcp(s[:, a, 2, :], s[:, a, 1, :], t))
        t = two(lambda a, t: self.tt("dve", h6(hc[:, a, :]), nd[:, a, :, 0:64], bc(s[:, a, 2, :], 64), MUL, t, hc.dep))
        yield
        t = two(lambda a, t: self.tt("dve", hc[:, a, :], hc[:, a, :], so[:, a, :], MUL, t, tso))
        t = two(lambda a, t: self.red(s[:, a, 3, :], h6(hc[:, a, :]), ADD, t))
        t = two(lambda a, t: self.ts("dve", s[:, a, 3, :], s[:, a, 3, :], 1 / 64, None, MUL, None, t))
        t = two(lambda a, t: self.tt("dve", h6(hc[:, a, :]), h6(hc[:, a, :]), bc(s[:, a, 3, :], 64), SUB, t))
        yield
        t = two(lambda a, t: self.act(sq[:, a, :], hc[:, a, :], ACT.Square, t, sq.dep))
        yield
        t = two(lambda a, t: self.red(s[:, a, 4, :], h6(sq[:, a, :]), ADD, t))
        t = two(lambda a, t: self.ts("pool", s[:, a, 5, :], s[:, a, 4, :], 1 / 64, 1e-6, MUL, ADD, t))
        t = two(lambda a, t: self.tt("pool", s[:, a, 6, :], s[:, a, 5, :], self.mhalf[:, 0:6], ALU.pow, t))
        yield
        tf = two(lambda a, t: self.tt("dve", h6(hc[:, a, :]), h6(hc[:, a, :]), bc(s[:, a, 6, :], 64), MUL, t))
        yield
        yield from self.to_mix(hc, tf, 5, lambda i: self.COL[:, ROW["mnorm"] + 3 * l + i:ROW["mnorm"] + 3 * l + i + 1], mh, ml, tm, 3)
        for b in (nd, hc, sq, s, so):
            M.put(b, Q.now())

    def mixer2(self, l, xt, fin):
        Q, M = self.Q, self.M
        XH, XL = self.XH, self.XL
        qs = M.get([128, 4, T])
        K2 = M.get([128, 2, 4, T])
        B2 = M.get([128, 2, 4, T])
        hv = M.get([128, 2, 512])
        hg = M.get([128, 2, 512])
        dqk = M.get([128, 2, 1024])
        dv = M.get([128, 2, 512])
        xq = M.get([128, 4, T])
        R = {}
        lb = self.lower_bounds(l)

        def fm(n, m, P, t):
            i = 2 * (n % 2) + m
            if n < 2:
                R["q", i] = self.act(qs[:, i, :], P[:, 0:T], ACT.Silu, t, qs.dep)
                return R["q", i]
            if n < 6:
                d = (n - 2) // 2
                R["f", d, i] = self.act(K2[:, d, i, :], P[:, 0:T], ACT.Sigmoid, t, K2.dep)
                return R["f", d, i]
            R["x", i] = self.cp("act", xq[:, i, :], P[:, 0:T], t, xq.dep)
            return R["x", i]

        def tm(n, a, P, t):
            s = slice((n % 2) * 256, (n % 2) * 256 + 256)
            if 12 <= n < 14:
                R["v", a, n % 2] = self.cp("act", hv[:, a, s], P[:, 0:256], t, hv.dep)
                return R["v", a, n % 2]
            if n >= 14:
                R["g", a, n % 2] = self.act(hg[:, a, s], P[:, 0:256], ACT.Silu, t, hg.dep)
                return R["g", a, n % 2]
            if n < 10:
                o = (n - 6) * 256
                R["dqk", a, n] = self.cp("act", dqk[:, a, o:o + 256], P[:, 0:256], t, dqk.dep)
                return R["dqk", a, n]
            R["dv", a, n] = self.cp("act", dv[:, a, s], P[:, 0:256], t, dv.dep)
            return R["dv", a, n]

        def got(k):
            return [v for kk, v in R.items() if kk[0] == k]

        tmx, mix = {}, []
        names = lambda k: [kk for kk in R if kk[0] == k]

        def hg_task():
            while len(names("f")) < 8:
                yield "wait"
            yield from self.hg_levels(l, lb, qs, K2, B2, got("q"), got("f"), R)
            while len(names("v")) < 4 or len(names("g")) < 4:
                yield "wait"
            yield from self.hgrn(l, qs, K2, B2, hv, got("v"), hg, got("g"), R, mix, tmx)

        def diff_task():
            while len(names("dqk")) < 8:
                yield "wait"
            yield from self.diff(l, dqk, got("dqk"), dv, R, mix, tmx)

        def memory_task():
            while len(names("x")) < 4 or "st" not in R:
                yield "wait"
            yield from self.memory(l, xq, got("x"), mix, tmx)

        g = hg_task()
        self.tasks += [g, g, g, diff_task(), memory_task()]
        for n in range(18):
            h, H, L, rd = self.take(("win2", l, n))
            if n < 6 or n >= 16:
                te = self.up(h, H, L, rd, XH, XL, xt, 256, lambda m, P, t, n=n: fm(n, m, P, t))
            else:
                te = self.tokmajor(h, H, L, rd, XH, XL, xt, 256, lambda a, P, t, n=n: tm(n, a, P, t))
        M.put(XH, te)
        M.put(XL, te)
        while not M.fits([128, 12, T]):
            assert self.beside(), M.free_
        mh = M.get([128, 12, T], F32R, high=True)
        while not M.fits([128, 12, T]):
            assert self.beside(), M.free_
        mix += [mh, M.get([128, 12, T], F32R, high=True)]
        mh, ml = mix
        while 1 not in tmx:
            assert self.beside()
        ks = [2 * k + i for k in WOUT2 for i in range(2)]
        out = self.down([("wout2", l, k) for k in WOUT2], ks, mh, ml, self.need(tmx), self.once(self.finish_tasks, fin), 2)
        M.put(mh, Q.now("pe"))
        M.put(ml, Q.now("pe"))
        return out

    def memory_kv(self):
        Q, M = self.Q, self.M
        mf, t = self.memf, self.tmf
        eh = M.get([128, 8, T], F32R)
        el = M.get([128, 8, T], F32R)
        fl = lambda b: rr(b[:, :, :], "p k t -> p (k t)")
        t1 = self.cp("act", fl(eh), fl(mf), t, eh.dep)
        t2 = self.tt("dve", fl(el), fl(mf), fl(eh), SUB, t1, el.dep)
        M.put(mf, t1, t2)
        xt = [[t1, t2]] * 8
        self.mkv = []
        for l in range(2):
            mk = M.get([128, 4, T])
            mv = M.get([128, 2, 512])
            o = []
            for n in range(4):
                h, H, L, rd = self.take(("wkv", l, n))
                if l == 0 and n == 2:
                    self.txf = Q.dma("pool", "xf", self.xf[:, :, :], self.dram["xT"], Q.now("dve"))
                if l == 1 and n == 1:
                    self.tc = Q.dma("pool", "c", self.C[:, :], self.dram["cst"], Q.now("dve"))
                    self.xt_ = [Q.dma("pool", "x", self.X[:, a, :], self.dram["x"][a]) for a in range(2)][-1:]
                if l == 1 and n == 2:
                    self.settle()
                    first = self.first_input(0, 0, 0)
                if n < 2:
                    def cb(m, P, t, n=n):
                        o.append(self.cp("act", mk[:, 2 * n + m, :], P[:, 0:T], t, mk.dep))
                        return o[-1]
                    te = self.up(h, H, L, rd, eh, el, xt, 256, cb)
                else:
                    def cb(a, P, t, n=n):
                        s = slice((n % 2) * 256, (n % 2) * 256 + 256)
                        o.append(self.cp("act", mv[:, a, s], P[:, 0:256], t, mv.dep))
                        return o[-1]
                    te = self.tokmajor(h, H, L, rd, eh, el, xt, 256, cb)
            ts_ = [Q.dma("pool", f"kv{l}", self.dram["kv"][l, :, 1024 * i:1024 * i + 1024], rr(b[:, :, :], "p k t -> p (k t)"), o)
                   for i, b in enumerate((mk, mv))]
            self.mkv.append(ts_)
            M.put(mk, ts_)
            M.put(mv, ts_)
        M.put(eh, te)
        M.put(el, te)
        return first

    def lower_bounds(self, l):
        if l == 0:
            return None
        Q, M = self.Q, self.M
        z = M.get([128, 2, 8, 4])
        t_ = []
        for d, name in enumerate(("lbf", "lbb")):
            c = [self.COL[:, ROW[name] + 4 * i:ROW[name] + 4 * i + 4] for i in range(2)]
            t = self.tt("dve", z[:, d, 0, :], c[0], c[1], MAX, z.dep, self.tc2)
            a = [self.tt("dve", z[:, d, 1 + i, :], c[i], z[:, d, 0, :], SUB, t) for i in range(2)]
            a = [self.act(z[:, d, 1 + i, :], z[:, d, 1 + i, :], ACT.Exp, a[i]) for i in range(2)]
            t = self.tt("dve", z[:, d, 3, :], z[:, d, 1, :], z[:, d, 2, :], ADD, a)
            t = self.rcp(z[:, d, 3, :], z[:, d, 3, :], t)
            a = [self.tt("dve", z[:, d, 1 + i, :], z[:, d, 1 + i, :], z[:, d, 3, :], MUL, t) for i in range(2)]
            t = self.tt("dve", z[:, d, 4, :], z[:, d, 1, :], z[:, d, 2, :], ADD, a)
            t = self.tt("dve", z[:, d, 4, :], z[:, d, 4, :], z[:, d, 1, :], SUB, t)
            t_.append(self.ts("dve", z[:, d, 5, :], z[:, d, 4, :], -1.0, 1.0, MUL, ADD, t))
        return z, t_

    def hg_levels(self, l, lb, qs, K2, B2, tq, tf, R):
        Q, M = self.Q, self.M
        lo = 2.0 ** -63
        E = M.get([128, 2, 4, T])
        fl = lambda x: rr(x, "p h t -> p (h t)")
        tk, tb = [], []
        for d in range(2):
            f = fl(K2[:, d, :, :])
            if lb is None:
                t = self.ts("dve", f, f, 1e-20, None, MAX, None, tf)
            else:
                z, tz = lb
                ts_ = [self.ts("dve", K2[:, d, h, :], K2[:, d, h, :], z[:, d, 5, h:h + 1], z[:, d, 4, h:h + 1], MUL, ADD, tf, tz) for h in range(4)]
                t = self.ts("dve", f, f, 1e-20, None, MAX, None, ts_)
            g, g2 = fl(B2[:, d, :, :]), fl(E[:, d, :, :])
            t1 = self.ts("dve", g, f, lo, None, MAX, None, t, B2.dep)
            t2 = self.ts("dve", g2, f, lo, 1 / lo, MIN, MUL, t, E.dep)
            t1 = self.act(g, g, ACT.Ln, t1)
            t2 = self.act(g2, g2, ACT.Ln, t2)
            yield
            tg = self.tt("dve", g2, g, g2, ADD, t1, t2)
            tk.append(self.ts("dve", f, f, -1.0, 1.0, MUL, ADD, t1, t2))
            yield
            for h in range(4):
                s = slice(None) if d == 0 else slice(T - 1, None, -1)
                tb.append(Q.op("dve", lambda g_, h=h, s=s, d=d: g_.tensor_tensor_scan(B2[:, d, h, s], self.rmask, E[:, d, h, s], 0.0, MUL, ADD), [tg]))
            yield
        if lb is not None:
            M.put(lb[0], Q.now("dve"))
        A = M.get([128, 8, 128])
        ta = self.mset("pool", A[:, :, :], 0.0, A.dep)
        KL = [M.get([128, 4, T]) for _ in range(2)]
        QL = [M.get([128, 4, T]) for _ in range(2)]
        kfree = [[x.dep, y.dep] for x, y in zip(KL, QL)]
        efree = [tb, tb]
        todo = []

        def meet(Kl, Ql, mask, tin, s):
            nonlocal ta
            for g in range(2):
                b, P, f = self.bank()
                for j in range(4):
                    u = 4 * g + j
                    h, a = u // 2, u % 2
                    c = slice(a * 128, a * 128 + 128)
                    t = self.mm(P[:, j * 128:j * 128 + 128], Kl[:, h, c], Ql[:, h, c], True, True, tin, f, inc=j == 3)
                mb = mask.bitcast(I32).unsqueeze(1).to_broadcast([128, 4, 128])
                ta = Q.op("dve", lambda e, g=g, P=P, mb=mb: e.copy_predicated(A[:, 4 * g:4 * g + 4, :], mb, rr(P[:, :], "p (u t) -> p u t", u=4)), [t, ta])
                self.done(b, ta)
            if s is not None:
                kfree[s] = t

        t = self.tt("pool", fl(KL[1][:, :, :]), fl(K2[:, 0, :, :]), fl(K2[:, 1, :, :]), ADD, tk, kfree[1])
        todo.append(lambda t=t: meet(KL[1], qs, self.ident, [t, tq], 1))
        yield
        for lv in range(6):
            z = 1 << lv
            s = lv % 2
            v = lambda x: rr(fl(x), "p (n z) -> p n z", z=2 * z)
            w = []
            for d in range(2):
                b, e = v(B2[:, d, :, :]), v(E[:, d, :, :])
                ref = b[:, :, z - 1 + d:z + d].to_broadcast([128, 512 // z, z])
                lw, up = slice(0, z), slice(z, 2 * z)
                x, y = (lw, up) if d == 0 else (up, lw)
                t = [self.tt("pool", e[:, :, x], ref, b[:, :, x], SUB, tb, efree[d]),
                     self.tt("pool", e[:, :, y], b[:, :, y], ref, SUB, tb, efree[d])]
                t = self.act(fl(E[:, d, :, :]), fl(E[:, d, :, :]), ACT.Exp, t)
                yield
                efree[d] = [self.tt("dve", v(KL[s][:, :, :])[:, :, x], v(K2[:, d, :, :])[:, :, x], e[:, :, x], MUL, t, tk, tq, kfree[s]),
                            self.tt("dve", v(QL[s][:, :, :])[:, :, y], v(qs[:, :, :])[:, :, y], e[:, :, y], MUL, t, tk, tq, kfree[s])]
                w += efree[d]
            yield
            todo.append(lambda lv=lv, s=s, w=w: meet(KL[s], QL[s], self.both[:, lv * 128:lv * 128 + 128], w, s))
            todo.pop(0)()
            yield
        todo.pop(0)()
        for x in (*KL, *QL):
            M.put(x, Q.now("pe"))
        R["attn"] = (A, ta, tk, tb, E)
        yield

    def hgrn(self, l, qs, K2, B2, hv, tv, hg, tg, R, mix, tmx):
        Q, M = self.Q, self.M
        A, ta, tk, tb, E = R["attn"]
        tq = [v for k, v in R.items() if k[0] == "q"]
        fl = lambda x: rr(x, "p h t -> p (h t)")
        c4 = lambda x: rr(fl(x), "p (n s) -> p n s", s=64)
        kt = yield from self.room([128, 2, 2, 512])
        dc = yield from self.room([128, 2, 16])
        tkt = {}
        tkd = []
        w = Q.now("dve")
        for d in range(2):
            b = c4(B2[:, d, :, :])
            end = 63 if d == 0 else 0
            last = b[:, :, end:end + 1].to_broadcast([128, 16, 64])
            t = self.tt("dve", c4(E[:, d, :, :]), last, b, SUB, tb, w)
            t = self.act(fl(E[:, d, :, :]), fl(E[:, d, :, :]), ACT.Exp, t)
            x = fl(B2[:, d, :, :])
            t2 = self.act(x, x, ACT.Exp, t, tb)
            yield
            tkd.append(self.tt("dve", fl(E[:, d, :, :]), fl(E[:, d, :, :]), fl(K2[:, d, :, :]), MUL, t, tk))
            td = self.cp("dve", dc[:, d, :], c4(B2[:, d, :, :])[:, :, end], t2, dc.dep)
            R["qe", d] = self.tt("dve", x, x, fl(qs[:, :, :]), MUL, td, tq)
            R["dc", d] = td
            yield
        for d in range(2):
            for a in range(2):
                bb, P, f = self.bank()
                for h in range(4):
                    t = self.tr(P[:, h * 128:h * 128 + 128], E[:, d, h, a * 128:a * 128 + 128], tkd[d], f, inc=h == 3)
                tkt[d, a] = self.cp("act", kt[:, d, a, :], P[:, :], t, kt.dep)
                self.done(bb, tkt[d, a])
            yield
        M.put(E, Q.now("pe"))
        M.put(K2, Q.now("dve"))
        while not mix:
            yield "wait"
        ST = []
        for _ in range(6):
            ST.append((yield from self.room([128, 512])))
        R["st"] = True
        tst = {}
        for d in range(2):
            prev = None
            for i in range(3):
                n = i if d == 0 else 3 - i
                a, o = n // 2, 64 * (n % 2)
                b, P, f = self.bank()
                for h in range(4):
                    c = slice(h * 128, h * 128 + 128)
                    t = self.mm(P[:, c], kt[o:o + 64, d, a, c], hv[o:o + 64, a, c], True, True, tkt[d, a], tv, f, inc=h == 3)
                if i == 0:
                    w = self.cp("act", ST[3 * d][:, :], P[:, :], t, ST[3 * d].dep)
                else:
                    w = [self.stt(ST[3 * d + i][:, h * 128:h * 128 + 128], ST[3 * d + i - 1][:, h * 128:h * 128 + 128],
                                  dc[:, d, 4 * h + n:4 * h + n + 1], P[:, h * 128:h * 128 + 128], MUL, ADD, t, prev, R["dc", d], ST[3 * d + i].dep) for h in range(4)]
                self.done(b, w)
                tst[d, i] = prev = w
                yield
        for x in (kt, dc, qs):
            M.put(x, Q.now())
        o_ = yield from self.room([128, 2, 512])
        sq = yield from self.room([128, 2, 512])
        ms = yield from self.room([128, 4, 4])
        h4 = lambda ap: rr(ap, "p (h d) -> p h d", h=4)
        tf = []
        while not mix:
            yield "wait"
        mh, ml = mix
        for a in range(2):
            b, P, f = self.bank()
            for h in range(4):
                c = slice(h * 128, h * 128 + 128)
                self.mm(P[:, c], A[:, 2 * h + a, :], hv[:, a, c], h == 0, False, ta, tv, f, share=True)
            for n in (2 * a, 2 * a + 1):
                r = slice(64 * (n % 2), 64 * (n % 2) + 64)
                for d in range(2):
                    i = n - 1 if d == 0 else 2 - n
                    if i < 0:
                        continue
                    for h in range(4):
                        c = slice(h * 128, h * 128 + 128)
                        t = self.mm(P[r, c], B2[:, d, h, 64 * n:64 * n + 64], ST[3 * d + i][:, c], False, n == 2 * a + 1 and h == 3 and (d == 1 or n == 3), R["qe", d], tst[d, i],
                                    inc=n == 2 * a + 1 and h == 3, share=True)
            t = self.cp("act", o_[:, a, :], P[:, :], t, o_.dep)
            self.done(b, t)
            tf.append(t)
            yield
        tf = yield from self.head_rms(o_, sq, ms, tf, 1.0)
        tf = [self.tt("dve", o_[:, a, :], o_[:, a, :], hg[:, a, :], MUL, tf[a], tg) for a in range(2)]
        yield
        yield from self.to_mix(o_, tf, 4, lambda i: self.COL[:, ROW["hnorm"] + l:ROW["hnorm"] + l + 1], mh, ml, tmx, 4)
        for x in (A, B2, *ST, o_, sq, ms, hv, hg):
            M.put(x, Q.now())
        R["hg"] = True

    def head_rms(self, o, sq, ms, t, k):
        h4 = lambda ap: rr(ap, "p (h d) -> p h d", h=4)
        two = lambda f: [f(a, t[a]) for a in range(2)]
        t = two(lambda a, t: self.act(sq[:, a, :], o[:, a, :], ACT.Square, t, sq.dep))
        yield
        t = two(lambda a, t: self.red(ms[:, a, :], h4(sq[:, a, :]), ADD, t, ms.dep))
        t = two(lambda a, t: self.ts("pool", ms[:, a, :], ms[:, a, :], 1 / 128, 1e-6, MUL, ADD, t))
        t = two(lambda a, t: self.tt("pool", ms[:, 2 + a, :], ms[:, a, :], self.mhalf[:, 0:4], ALU.pow, t))
        if k != 1.0:
            t = two(lambda a, t: self.ts("pool", ms[:, 2 + a, :], ms[:, 2 + a, :], k, None, MUL, None, t))
        yield
        return two(lambda a, t: self.tt("dve", h4(o[:, a, :]), h4(o[:, a, :]), bc(ms[:, 2 + a, :], 128), MUL, t))

    def rotary(self):
        Q, M = self.Q, self.M
        self.CS = M.get([128, 2, 2, 8])
        z = M.get([128, 2, 4, 8])
        p = M.get([128, 2])
        t = self.cp("dve", p[:, :], self.POS[:, :], self.tpos, p.dep)
        out = []
        c1 = 6.28125
        c2 = float(np.float32(np.round((2 * math.pi - c1) * 2 ** 20) / 2 ** 20))
        c3 = 2 * math.pi - c1 - c2
        big = 1.5 * 2 ** 23
        for a in range(2):
            x, k, r, y = (z[:, a, i, :] for i in range(4))
            t1 = self.ts("dve", x, self.freq, p[:, a:a + 1], None, MUL, None, t, self.tc, z.dep)
            t2 = self.ts("dve", k, x, 1 / (2 * math.pi), None, MUL, None, t1)
            t2 = self.ts("dve", k, k, big, None, ADD, None, t2)
            t2 = self.ts("dve", k, k, -big, None, ADD, None, t2)
            t2 = self.stt(r, k, -c1, x, MUL, ADD, t2)
            t2 = self.stt(r, k, -c2, r, MUL, ADD, t2)
            t2 = self.stt(r, k, -c3, r, MUL, ADD, t2)
            t2 = self.ts("dve", r, r, 3.1415925, -3.1415925, MIN, MAX, t2)
            out.append(self.act(self.CS[:, 1, a, :], r, ACT.Sin, t2, self.CS.dep))
            t3 = self.ts("dve", y, r, -1.0, None, MUL, None, t2)
            t3 = self.tt("dve", y, y, r, MAX, t3)
            t3 = self.ts("dve", y, y, -1.0, math.pi / 2, MUL, ADD, t3)
            out.append(self.act(self.CS[:, 0, a, :], y, ACT.Sin, t3, self.CS.dep))
        M.put(z, out)
        M.put(p, out)
        self.tcs = out

    def soft(self, P, w, scale, mx, out, *after):
        P3 = rr(P, "p (a k) -> p a k", a=2)
        t = self.red(mx[:, 0:2], P3, MAX, after)
        t = self.ts("dve", mx[:, 2:4], mx[:, 0:2], -scale, None, MUL, None, t)
        return [self.act(out[:, a, :], P3[:, a, :], ACT.Exp, t, bias=mx[:, 2 + a:3 + a], scale=scale, accum_out=mx[:, 4 + a:5 + a]) for a in range(2)]

    def diff(self, l, dqk, tqk, dv, R, mix, tmx):
        Q, M = self.Q, self.M
        lam0 = 0.8 - 0.6 * math.exp(-0.3 * l)
        LM = yield from self.room([128, 256])
        lm = yield from self.room([128, 8])
        tlam = Q.dma("pool", "lam", LM[:, :], self.dram["lam"][l:l + 1, :].to_broadcast([128, 256]), LM.dep)
        tm = yield from self.room([128, 2, 4, 16, 8])
        qT = yield from self.room([128, 8, T])
        tr_ = []
        for a in range(2):
            v = rr(dqk[:, a, :], "p (g d) -> p g d", g=16)
            x1, x2 = v[:, :, 0:8], v[:, :, 8:16]
            c, s = (self.CS[:, i, a, :].unsqueeze(1).to_broadcast([128, 16, 8]) for i in range(2))
            u = [self.tt("dve", tm[:, a, i, :, :], x, y, MUL, tqk, self.tcs, tm.dep) for i, (x, y) in enumerate(((x1, c), (x2, s), (x2, c), (x1, s)))]
            tr_.append(self.tt("dve", x1, tm[:, a, 0, :, :], tm[:, a, 1, :, :], SUB, u))
            tr_.append(self.tt("dve", x2, tm[:, a, 2, :, :], tm[:, a, 3, :, :], ADD, u))
            yield
        tT = []
        for i in range(4):
            b, P, f = self.bank()
            for j in range(2):
                for a in range(2):
                    k = 2 * i + j
                    t = self.tr(P[:, j * 256 + a * 128:j * 256 + a * 128 + 128], dqk[:, a, k * 128:k * 128 + 128], tr_, f, inc=j + a == 2)
            tT.append(self.cp("act", rr(qT[:, 2 * i:2 * i + 2, :], "p k t -> p (k t)"), P[:, :], t, qT.dep))
            self.done(b, tT[-1])
            if i % 2:
                yield
        M.put(tm, Q.now("dve"))
        L4 = rr(LM[:, :], "p (a b d) -> p a b d", a=2, b=2)
        t = self.tt("dve", L4[:, :, 0, :], L4[:, :, 0, :], L4[:, :, 1, :], MUL, tlam)
        t = self.red(lm[:, 0:2], L4[:, :, 0, :], ADD, t, lm.dep)
        t = self.act(lm[:, 2:4], lm[:, 0:2], ACT.Exp, t)
        t = self.tt("dve", lm[:, 4:5], lm[:, 3:4], lm[:, 2:3], SUB, t)
        tl = self.ts("dve", lm[:, 5:6], lm[:, 4:5], -lam0, None, ADD, None, t)
        M.put(LM, tl)
        M.put(dqk, Q.now("pe"))
        while sum(k[0] == "dv" for k in R) < 4:
            yield "wait"
        tdv = [v for k, v in R.items() if k[0] == "dv"]
        pp = yield from self.room([128, 2, 2, 2, T])
        mx = yield from self.room([128, 8, 8])
        aT = yield from self.room([128, 2, 2, T])
        out = [self.bank() for _ in range(2)]
        afr = [aT.dep] * 2
        pfr = [pp.dep] * 2
        taT = {}
        back, tout = {}, {}
        for h in range(6):
            if h > 2:
                back[h - 3][2]()
            if h > 1:
                back[h - 2][1]()
                yield
            if h == 4:
                back[h - 1][0]()
            if h > 3:
                continue
            s = h % 2
            tt_ = []
            for c in range(2):
                r = slice(64 * c, 64 * c + 64)
                b, P, f = self.bank()
                for a in range(2):
                    t = self.mm(P[:, a * 256:a * 256 + 256], qT[r, h, a * 128:a * 128 + 128], qT[r, 4 + h, :], True, True, tT, f, inc=a == 1)
                m = mx[:, 2 * h + c, :]
                o = self.soft(P[:, :], 256, 0.125, m, pp[:, s, c, :, :], t, pfr[s], mx.dep)
                self.done(b, o)
                tt_.append(o)

            def weigh(h=h, s=s, tt_=tt_):
                m0, m1 = mx[:, 2 * h, :], mx[:, 2 * h + 1, :]
                t2 = self.rcp(m0[:, 6:8], m0[:, 4:6], tt_[0])
                t = self.rcp(m1[:, 6:8], m1[:, 4:6], tt_[1])
                t = self.ts("dve", m1[:, 0:2], m1[:, 6:8], lm[:, 5:6], None, MUL, None, t, tl)
                o = taT[h] = []
                for a in range(2):
                    t1 = self.ts("dve", pp[:, s, 0, a, :], pp[:, s, 0, a, :], m0[:, 6 + a:7 + a], None, MUL, None, t2, tt_)
                    o.append(self.stt(pp[:, s, 0, a, :], pp[:, s, 1, a, :], m1[:, a:a + 1], pp[:, s, 0, a, :], MUL, ADD, t, t1))

            def turn(h=h, s=s):
                o = taT[h]
                b, P, f = self.bank()
                for kk in range(2):
                    for a in range(2):
                        t = self.tr(P[:, kk * 256 + a * 128:kk * 256 + a * 128 + 128], pp[:, s, 0, a, kk * 128:kk * 128 + 128], o, f, inc=kk + a == 2)
                pfr[s] = t
                taT[h] = self.cp("act", rr(aT[:, s, :, :], "p k t -> p (k t)"), P[:, :], t, afr[s])
                self.done(b, taT[h])

            def sum_up(h=h, s=s):
                c = slice(h * 128, h * 128 + 128)
                for a in range(2):
                    for kk in range(2):
                        t = self.mm(out[a][1][:, c], aT[:, s, kk, a * 128:a * 128 + 128], dv[:, kk, c], kk == 0, kk == 1, taT[h], tdv, out[a][2], inc=kk == 1)
                    tout[a] = t
                afr[s] = t

            back[h] = (weigh, turn, sum_up)
            if h:
                back[h - 1][0]()
            yield
        back[3][2]()
        for x in (pp, qT, aT, dv):
            M.put(x, Q.now("pe"))
        o_ = yield from self.room([128, 2, 512])
        tf = []
        for a in range(2):
            tf.append(self.cp("act", o_[:, a, :], out[a][1][:, :], tout[a], o_.dep))
            self.done(out[a][0], tf[a])
        yield
        sq = yield from self.room([128, 2, 512])
        ms = yield from self.room([128, 4, 4])
        while not mix:
            yield "wait"
        mh, ml = mix
        tf = yield from self.head_rms(o_, sq, ms, tf, 1.0 - lam0)
        yield
        yield from self.to_mix(o_, tf, 0, lambda i: self.COL[:, ROW["dnorm"] + l:ROW["dnorm"] + l + 1], mh, ml, tmx, 4)
        for x in (lm, mx, o_, sq, ms):
            M.put(x, Q.now())

    def memory(self, l, xq, tx, mix, tmx):
        Q, M = self.Q, self.M
        mk = yield from self.room([128, 4, T])
        mv = yield from self.room([128, 2, 512])
        tk, tv = (Q.dma("pool", f"kr{i}", rr(b[:, :, :], "p k t -> p (k t)"), self.dram["kv"][l, :, 1024 * i:1024 * i + 1024], b.dep, self.mkv[l])
                  for i, b in enumerate((mk, mv)))
        while not mix:
            yield "wait"
        mh, ml = mix
        pp = yield from self.room([128, 2, 2, T])
        mx = yield from self.room([128, 4, 8])
        pT = yield from self.room([128, 2, 2, T])
        pfr, tfr = [pp.dep] * 2, [pT.dep] * 2
        back = []
        for h in range(4):
            s = h % 2
            b, P, f = self.bank()
            for a in range(2):
                t = self.mm(P[:, a * 256:a * 256 + 256], xq[:, h, a * 128:a * 128 + 128], mk[:, h, :], True, True, tx, tk, f, inc=a == 1)
            m = mx[:, h, :]
            o = self.soft(P[:, :], 256, 128 ** -0.5, m, pp[:, s, :, :], t, pfr[s], mx.dep)
            self.done(b, o)

            def turn(h=h, s=s, o=o, m=m):
                t = self.rcp(m[:, 6:8], m[:, 4:6], o)
                o = [self.ts("dve", pp[:, s, a, :], pp[:, s, a, :], m[:, 6 + a:7 + a], None, MUL, None, t) for a in range(2)]
                b, P, f = self.bank()
                for kk in range(2):
                    for a in range(2):
                        t = self.tr(P[:, kk * 256 + a * 128:kk * 256 + a * 128 + 128], pp[:, s, a, kk * 128:kk * 128 + 128], o, f, inc=kk + a == 2)
                pfr[s] = t
                t = self.cp("act", rr(pT[:, s, :, :], "p k t -> p (k t)"), P[:, :], t, tfr[s])
                self.done(b, t)
                b, P, f = self.bank()
                for kk in range(2):
                    u = self.mm(P[:, 0:T], mv[:, kk, h * 128:h * 128 + 128], pT[:, s, kk, :], kk == 0, kk == 1, t, tv, f, inc=kk == 1)
                tfr[s] = u
                t1 = self.cp("act", mh[:, 8 + h, :], P[:, 0:T], u, mh.dep)
                t2 = self.tt("dve", ml[:, 8 + h, :], P[:, 0:T], mh[:, 8 + h, :], SUB, t1, ml.dep)
                self.done(b, t1, t2)
                tmx[8 + h] = [t1, t2]

            back.append(turn)
            if h:
                back.pop(0)()
            yield
        back.pop(0)()
        for x in (pp, mx, pT, xq, mk, mv):
            M.put(x, Q.now())

    def first_input(self, p, l, j):
        Q, M = self.Q, self.M
        xf, tx = self.xf, self.txf
        tmp = M.get([128, 2, T])
        self.XH = M.get([128, 8, T], F32R, high=True)
        self.XL = M.get([128, 8, T], F32R, high=True)
        tm = [v for k, v in self.mod_t[p].items() if k != "free"]
        A, B = self.mod[p][:, 1, :], self.mod[p][:, 0, :]
        tf = [tmp.dep] * 2
        out = []
        for f in range(8):
            s = f % 2
            a, b = A[:, f:f + 1], B[:, f:f + 1]
            t1 = self.act(self.XH[:, f, :], xf[:, f, :], ACT.Identity, tx, tm, self.XH.dep, scale=a, bias=b)
            t2 = self.ts("dve", tmp[:, s, :], xf[:, f, :], a, b, MUL, ADD, tx, tm, tf[s])
            t3 = self.tt("dve", self.XL[:, f, :], tmp[:, s, :], self.XH[:, f, :], SUB, t2, t1, self.XL.dep)
            tf[s] = t3
            out.append([t1, t3])
        self.mod_t[p] = {"free": out}
        M.put(xf, out)
        M.put(tmp, out)
        return out

    def rowsof(self, n, i):
        return [VEC[n + "_g"] + i, VEC[n + "_b"] + i]

    def colsof(self, n, i):
        g, b = ROW[n + "_g"] + 8 * i, ROW[n + "_b"] + 8 * i
        return self.COL[:, g:g + 8], self.COL[:, b:b + 8]

    def run(self, until=None):
        Q = self.Q
        self.gate_free = self.abfree = None
        self.start()
        xt = self.memory_kv()
        self.rotary()
        for l in range(2):
            xt = self.ffn1(l, 0, xt, self.post(True, self.rowsof("ln", 3 * l), (*self.colsof("ln", 3 * l), ((3 * l + 1) % 2, l, 1))))
            xt = self.mixer1(l, xt, self.post(True, self.rowsof("ln", 3 * l + 1), (*self.colsof("ln", 3 * l + 1), ((3 * l + 2) % 2, l, 2))))
            if l == 0:
                fin = self.post(True, self.rowsof("ln", 2), (*self.colsof("ln", 2), (1, 1, 0)))
            else:
                fin = self.post(True, self.rowsof("ln", 5), (*self.colsof("lin", 0), None), self.rowsof("lin", 0))
            xt = self.ffn1(l, 1, xt, fin)
        self.M.put(self.G[0], self.gate_free)
        self.M.put(self.acc, self.Q.now("dve", "pe"))
        for l in range(2):
            xt = self.mixer2(l, xt, self.post(False, self.rowsof("ln1", l), (*self.colsof("ln1", l), None)))
            xt = self.ffn2(l, xt, self.post(False, self.rowsof("ln2", l), (*self.colsof("ln2", l), None) if l == 0 else None))
        for a in range(2):
            t = Q.dma("sp", "out", self.dram["out"][a], self.X[:, a, :], self.xt_)
        Q.wait("sp", t)


def build(nc, dram):
    ctx = ExitStack()
    with ctx:
        p = Prog(nc, ctx, dram)
        p.run()
        for n in ("kv0", "kv1"):
            if n in p.Q.cnt:
                p.Q.wait("sp", (n, p.Q.cnt[n]))
        block = ctx.enter_context(nc.Block())

        @block.sync
        def _(e):
            p.Q.play("sp", e)

        @block.tensor
        def _(e):
            p.Q.play("pe", e)

        @block.vector
        def _(e):
            p.Q.play("dve", e)

        @block.scalar
        def _(e):
            p.Q.play("act", e)

        @block.gpsimd
        def _(e):
            p.Q.play("pool", e)


def kernel(**inputs):
    import numpy as _np
    import concourse.bacc as _bacc
    from concourse import mybir as _mybir
    from concourse.bass_utils import run_bass_kernel_spmd as _run

    a = {k: _np.asarray(v) for k, v in inputs.items()}
    arrays = {"in_" + k: _np.ascontiguousarray(v) for k, v in layout(a).items()}
    nc = _bacc.Bacc("TRN2", target_bir_lowering=False, num_devices=1)
    dram = {k[3:]: nc.dram_tensor(k, v.shape, _mybir.dt.from_np(v.dtype), kind="ExternalInput").ap() for k, v in arrays.items()}
    out = nc.dram_tensor("out_0", (2, 128, D), F32, kind="ExternalOutput").ap()
    dram["out"] = out
    dram["kv"] = nc.dram_tensor("kv", (2, 128, 2048), F32, kind="Internal").ap()
    build(nc, dram)
    r = _run(nc, [arrays], core_ids=[0])
    return r.results[0]["out_0"].reshape(1, T, D)
```
